# Optimizing a Trainium2 kernel written in Bass

```python
import math
import jax, jax.numpy as jnp
from jax import lax
import numpy as np

D_MODEL = 1024
BATCH = 1
SEQ = 256
DEPTH = 2

CHUNK = 64
Q_BLOCK = 128
HEAD_DIM = 64
RMS_EPS = 1e-6
A_HEADS = 4
A_V_DIM = 2 * HEAD_DIM
B_HEADS = 8
IDX_HEADS = 4
IDX_DIM = HEAD_DIM
TOPK_MAX = 256
C_HEADS = D_MODEL // HEAD_DIM
C_LEFT_CHUNKS = 8
C_BAND = (C_LEFT_CHUNKS + 1) * CHUNK
C_REL_CLIP = 128
T5_BUCKETS = 32
T5_MAX_DIST = 1024
T5_HEADS = A_HEADS + B_HEADS
N_GROUPS = 4
EXPERTS_PER_GROUP = 8
N_EXPERTS = N_GROUPS * EXPERTS_PER_GROUP
EXPERT_TOPK = 2
D_EXPERT = D_MODEL // 2
N_EVEN = (DEPTH + 1) // 2
N_ODD = DEPTH // 2
AB_WIDTHS = (A_HEADS * 2 * HEAD_DIM, A_HEADS * 2 * HEAD_DIM, A_HEADS * A_V_DIM,
             B_HEADS * HEAD_DIM, HEAD_DIM, HEAD_DIM, IDX_HEADS * IDX_DIM, IDX_DIM, IDX_HEADS)
AB_SPLITS = tuple(sum(AB_WIDTHS[:i + 1]) for i in range(len(AB_WIDTHS) - 1))
AB_IN = sum(AB_WIDTHS)
AB_OUT = A_HEADS * A_V_DIM + B_HEADS * HEAD_DIM
NEG = -1e30

kernel_name = "hybrid_chunk_causal_diff_dsa_band_hmoe"

def rms_norm(x, g):
    xf = x.astype(jnp.float32)
    y = xf * lax.rsqrt(jnp.mean(xf * xf, axis=-1, keepdims=True) + RMS_EPS)
    return (y * g.astype(jnp.float32)).astype(x.dtype)

def masked_softmax(s, mask):
    return jax.nn.softmax(jnp.where(mask, s.astype(jnp.float32), NEG), axis=-1)

def t5_bucket(rel):
    half = T5_BUCKETS // 2
    max_exact = half // 2
    ret = jnp.where(rel > 0, half, 0)
    n = jnp.abs(rel)
    nf = jnp.maximum(n, 1).astype(jnp.float32)
    large = max_exact + (jnp.log(nf / max_exact) / math.log(T5_MAX_DIST / max_exact)
                         * (half - max_exact)).astype(jnp.int32)
    large = jnp.minimum(large, half - 1)
    return (ret + jnp.where(n < max_exact, n, large)).astype(jnp.int32)

def diff_sparse_mixer(xn, w_in, w_out, lam, subln, t5_bias, layer_idx):
    bsz, s_len, _ = xn.shape
    proj = xn @ w_in
    q_a, k_a, v_a, q_b, k_b, v_b, q_i, k_i, w_i = jnp.split(proj, AB_SPLITS, axis=-1)
    q_a = q_a.reshape(bsz, s_len, A_HEADS, 2, HEAD_DIM)
    k_a = k_a.reshape(bsz, s_len, A_HEADS, 2, HEAD_DIM)
    v_a = v_a.reshape(bsz, s_len, A_HEADS, A_V_DIM)
    q_b = q_b.reshape(bsz, s_len, B_HEADS, HEAD_DIM)
    q_i = q_i.reshape(bsz, s_len, IDX_HEADS, IDX_DIM)
    w_i = w_i.astype(jnp.float32) * (IDX_HEADS ** -0.5) * (IDX_DIM ** -0.5)

    lam_init = 0.8 - 0.6 * math.exp(-0.3 * layer_idx)
    lamf = lam.astype(jnp.float32)
    lam_full = jnp.exp(jnp.sum(lamf[0] * lamf[1])) - jnp.exp(jnp.sum(lamf[2] * lamf[3])) + lam_init

    top_k = min(TOPK_MAX, s_len // 4)
    scale = HEAD_DIM ** -0.5
    key_pos = jnp.arange(s_len, dtype=jnp.int32)
    key_chunk = key_pos // CHUNK
    t5_a = t5_bias[:, :A_HEADS]
    t5_b = t5_bias[:, A_HEADS:]
    gather_rows = jax.vmap(lambda arr, idx: arr[idx])

    def block(i):
        start = i * Q_BLOCK
        qpos = start + jnp.arange(Q_BLOCK, dtype=jnp.int32)
        qchunk = qpos // CHUNK
        mask = key_chunk[None, :] <= qchunk[:, None]
        qa = lax.dynamic_slice_in_dim(q_a, start, Q_BLOCK, axis=1)
        bias_a = t5_a[t5_bucket(key_pos[None, :] - qpos[:, None])].transpose(2, 0, 1)
        s_a = jnp.einsum('bqhmd,bshmd->bhmqs', qa, k_a) * scale + bias_a[None, :, None]
        p_a = masked_softmax(s_a, mask[None, None, None])
        attn_a = (p_a[:, :, 0] - lam_full * p_a[:, :, 1]).astype(v_a.dtype)
        out_a = jnp.einsum('bhqs,bshe->bqhe', attn_a, v_a)
        out_a = rms_norm(out_a, subln) * (1.0 - lam_init)
        out_a = out_a.reshape(bsz, Q_BLOCK, A_HEADS * A_V_DIM)
        qi = lax.dynamic_slice_in_dim(q_i, start, Q_BLOCK, axis=1)
        wi = lax.dynamic_slice_in_dim(w_i, start, Q_BLOCK, axis=1)
        isc = jax.nn.relu(jnp.einsum('bqhd,bsd->bqhs', qi, k_i).astype(jnp.float32))
        isc = jnp.einsum('bqhs,bqh->bqs', isc, wi)
        isc = jnp.where(mask[None], isc, -jnp.inf)
        _, sel = lax.top_k(isc, top_k)
        sel_valid = (sel // CHUNK) <= qchunk[None, :, None]
        k_sel = gather_rows(k_b, sel)
        v_sel = gather_rows(v_b, sel)
        qb = lax.dynamic_slice_in_dim(q_b, start, Q_BLOCK, axis=1)
        bias_b = t5_b[t5_bucket(sel - qpos[None, :, None])].transpose(0, 3, 1, 2)
        s_b = jnp.einsum('bqhd,bqkd->bhqk', qb, k_sel) * scale + bias_b
        p_b = masked_softmax(s_b, sel_valid[:, None]).astype(v_sel.dtype)
        out_b = jnp.einsum('bhqk,bqkd->bqhd', p_b, v_sel).reshape(bsz, Q_BLOCK, B_HEADS * HEAD_DIM)
        return jnp.concatenate([out_a, out_b], axis=-1)

    outs = lax.map(block, jnp.arange(s_len // Q_BLOCK))
    y = outs.transpose(1, 0, 2, 3).reshape(bsz, s_len, AB_OUT)
    return y @ w_out

def chunk_band_mixer(xn, w_in, w_out, rel_table):
    bsz, s_len, _ = xn.shape
    q, k, v = jnp.split(xn @ w_in, 3, axis=-1)
    q = q.reshape(bsz, s_len, C_HEADS, HEAD_DIM)
    k = k.reshape(bsz, s_len, C_HEADS, HEAD_DIM)
    v = v.reshape(bsz, s_len, C_HEADS, HEAD_DIM)
    pad = C_LEFT_CHUNKS * CHUNK
    k_pad = jnp.pad(k, ((0, 0), (pad, 0), (0, 0), (0, 0)))
    v_pad = jnp.pad(v, ((0, 0), (pad, 0), (0, 0), (0, 0)))
    qi = jnp.arange(CHUNK, dtype=jnp.int32)
    kj = jnp.arange(C_BAND, dtype=jnp.int32)
    rel = qi[:, None] - (kj[None, :] - pad)
    rel_idx = jnp.clip(rel, -C_REL_CLIP, C_REL_CLIP) + C_REL_CLIP
    bias = rel_table[rel_idx].transpose(2, 0, 1)
    scale = HEAD_DIM ** -0.5

    def chunk(c):
        start = c * CHUNK
        qc = lax.dynamic_slice_in_dim(q, start, CHUNK, axis=1)
        kc = lax.dynamic_slice_in_dim(k_pad, start, C_BAND, axis=1)
        vc = lax.dynamic_slice_in_dim(v_pad, start, C_BAND, axis=1)
        valid = (start - pad + kj) >= 0
        s = jnp.einsum('bqhd,bkhd->bhqk', qc, kc) * scale + bias[None]
        p = masked_softmax(s, valid[None, None, None, :]).astype(vc.dtype)
        return jnp.einsum('bhqk,bkhd->bqhd', p, vc)

    outs = lax.map(chunk, jnp.arange(s_len // CHUNK))
    y = outs.transpose(1, 0, 2, 3, 4).reshape(bsz, s_len, C_HEADS * HEAD_DIM)
    return y @ w_out

def hier_moe(xn, w_rg, b_rg, w_re, b_re, w_gate, w_up, w_down):
    bsz, s_len, d = xn.shape
    xt = xn.reshape(-1, d)
    n_tok = xt.shape[0]
    g_logits = (xt @ w_rg + b_rg).astype(jnp.float32)
    p_g = jax.nn.softmax(g_logits, axis=-1)
    g_sel = jnp.argmax(g_logits, axis=-1)
    p_gsel = jnp.take_along_axis(p_g, g_sel[:, None], axis=1)
    e_logits = (xt @ w_re + b_re).astype(jnp.float32).reshape(n_tok, N_GROUPS, EXPERTS_PER_GROUP)
    e_logits = jnp.take_along_axis(e_logits, g_sel[:, None, None], axis=1)[:, 0]
    p_e = jax.nn.softmax(e_logits, axis=-1)
    top_w, top_i = lax.top_k(p_e, EXPERT_TOPK)
    top_w = top_w / jnp.sum(top_w, axis=-1, keepdims=True)
    w_within = jnp.sum(jax.nn.one_hot(top_i, EXPERTS_PER_GROUP, dtype=jnp.float32) * top_w[..., None], axis=1)
    combine = (jax.nn.one_hot(g_sel, N_GROUPS, dtype=jnp.float32)[:, :, None]
               * w_within[:, None, :]).reshape(n_tok, N_EXPERTS) * p_gsel
    combine = combine.astype(xt.dtype)
    y = jnp.zeros_like(xt)
    for e in range(N_EXPERTS):
        h = jax.nn.silu(xt @ w_gate[e]) * (xt @ w_up[e])
        y = y + combine[:, e:e + 1] * (h @ w_down[e])
    return y.reshape(bsz, s_len, d)

def setup_inputs(seed: int = 0) -> dict:
    key = jax.random.key(seed)
    ks = jax.random.split(key, 20)
    f32 = jnp.float32

    def nrm(k, shape, fan_in):
        return jax.random.normal(k, shape, f32) * (fan_in ** -0.5)

    def gain(k, shape):
        return 1.0 + 0.02 * jax.random.normal(k, shape, f32)

    return {
        "x": jax.random.normal(ks[0], (BATCH, SEQ, D_MODEL), f32),
        "t5_bias": 0.2 * jax.random.normal(ks[1], (T5_BUCKETS, T5_HEADS), f32),
        "ln_mix": gain(ks[2], (DEPTH, D_MODEL)),
        "ln_ffn": gain(ks[3], (DEPTH, D_MODEL)),
        "ln_final": gain(ks[4], (D_MODEL,)),
        "ab_w_in": nrm(ks[5], (N_EVEN, D_MODEL, AB_IN), D_MODEL),
        "ab_w_out": nrm(ks[6], (N_EVEN, AB_OUT, D_MODEL), AB_OUT),
        "diff_lambda": 0.1 * jax.random.normal(ks[7], (N_EVEN, 4, HEAD_DIM), f32),
        "diff_subln": gain(ks[8], (N_EVEN, A_V_DIM)),
        "c_w_in": nrm(ks[9], (N_ODD, D_MODEL, 3 * C_HEADS * HEAD_DIM), D_MODEL),
        "c_w_out": nrm(ks[10], (N_ODD, C_HEADS * HEAD_DIM, D_MODEL), C_HEADS * HEAD_DIM),
        "c_rel_bias": 0.2 * jax.random.normal(ks[11], (N_ODD, 2 * C_REL_CLIP + 1, C_HEADS), f32),
        "moe_w_rg": nrm(ks[12], (DEPTH, D_MODEL, N_GROUPS), D_MODEL),
        "moe_b_rg": 0.01 * jax.random.normal(ks[13], (DEPTH, N_GROUPS), f32),
        "moe_w_re": nrm(ks[14], (DEPTH, D_MODEL, N_EXPERTS), D_MODEL),
        "moe_b_re": 0.01 * jax.random.normal(ks[15], (DEPTH, N_EXPERTS), f32),
        "moe_w_gate": nrm(ks[16], (DEPTH, N_EXPERTS, D_MODEL, D_EXPERT), D_MODEL),
        "moe_w_up": nrm(ks[17], (DEPTH, N_EXPERTS, D_MODEL, D_EXPERT), D_MODEL),
        "moe_w_down": nrm(ks[18], (DEPTH, N_EXPERTS, D_EXPERT, D_MODEL), D_EXPERT),
    }

def reference(x, t5_bias, ln_mix, ln_ffn, ln_final, ab_w_in, ab_w_out, diff_lambda, diff_subln,
              c_w_in, c_w_out, c_rel_bias, moe_w_rg, moe_b_rg, moe_w_re, moe_b_re,
              moe_w_gate, moe_w_up, moe_w_down):
    h = x
    for l in range(DEPTH):
        xn = rms_norm(h, ln_mix[l])
        if l % 2 == 0:
            e = l // 2
            h = h + diff_sparse_mixer(xn, ab_w_in[e], ab_w_out[e], diff_lambda[e], diff_subln[e], t5_bias, l)
        else:
            o = l // 2
            h = h + chunk_band_mixer(xn, c_w_in[o], c_w_out[o], c_rel_bias[o])
        xn = rms_norm(h, ln_ffn[l])
        h = h + hier_moe(xn, moe_w_rg[l], moe_b_rg[l], moe_w_re[l], moe_b_re[l],
                         moe_w_gate[l], moe_w_up[l], moe_w_down[l])
    return rms_norm(h, ln_final)


_drawn_inputs = setup_inputs


def setup_inputs(seed=0):
    import zlib

    import numpy as np

    out = dict(_drawn_inputs(seed))
    spreads = {}
    factors = {'ln_final': 2.867, 'moe_b_rg': 7.136, 'moe_b_re': 2.922}
    for name, (base, spread) in spreads.items():
        noise = np.random.default_rng([zlib.crc32(name.encode()), seed]).standard_normal(out[name].shape)
        drawn = base * np.exp(spread * noise) if base else spread * noise
        out[name] = __import__('jax').numpy.asarray(drawn.astype(out[name].dtype))
    for name, factor in factors.items():
        out[name] = (out[name] * factor).astype(out[name].dtype)
    return out
```

```python
from contextlib import ExitStack

import numpy as np
import concourse.bass as bass
from concourse import mybir

FP32 = mybir.dt.float32
INT32 = mybir.dt.int32
ALU = mybir.AluOpType
ACT = mybir.ActivationFunctionType
AX = mybir.AxisListType

P = 128
SEQ, D, DEPTH = 256, 1024, 2
NT = SEQ // P
NK = D // P
CHUNK = 64
EPS = 1e-6
A_HEADS, B_HEADS, C_HEADS, IDX_HEADS, HD = 4, 8, 16, 4, 64
A_V = 2 * HD
TOPK = SEQ // 4
SCALE = HD ** -0.5
BUCKETS = 32
NEG = -1e30
GONE = -3e38
LAM_INIT = 0.8 - 0.6 * 1.0
GROUPS, PER_GROUP, TOP_EXPERTS = 4, 8, 2
EXPERTS = GROUPS * PER_GROUP
F = D // 2
NF = F // P
ROUTES = GROUPS + EXPERTS

CW = 256
AB_IN = 2500
A_CHUNKS = -(-AB_IN // CW)
C_CHUNKS = 3 * D // CW
IN_CHUNKS = (A_CHUNKS, C_CHUNKS)
SLOT_W = NK * CW
OUT_CHUNKS = D * NK // SLOT_W
KPC = NK // OUT_CHUNKS

AT_ONCE = 2
SLOTS = P // AT_ONCE
PAIRS = EXPERTS // AT_ONCE
MAX_PASSES = SEQ // SLOTS
UP_CHUNKS = 4
KPU = NK // UP_CHUNKS
CHUNKS = 2 * UP_CHUNKS + NF

BL = SEQ + P - 1
BW = BL + 1

PICKS = NT * AT_ONCE
UNITS = 16


def unit_of(layer, u):
    if layer == 0:
        kind, r = ("a", u) if u < 8 else ("b", u - 8)
        return kind, r % 4, r // 4, P * (r // 4 + 1)
    return "c", u % 8, u // 8, P * (u // 8 + 1)


def last_units(layer):
    return (3, 7, 11, 15) if layer == 0 else (7, 15)


def build(nc, x, t5, ln_mix, ln_ffn, ln_final, ab_in, ab_out, lam, subln, c_in, c_out, rel,
          w_rg, b_rg, w_re, b_re, w_gate, w_up, w_down, consts, hot_t5, hot_rel, out):
    ctx = ExitStack()
    with ctx:
        def sb(name, shape, dt=FP32):
            return ctx.enter_context(nc.sbuf_tensor(name, shape, dt))

        def sem(name):
            return ctx.enter_context(nc.semaphore(name))

        def per_layer(name):
            return [sem(f"{name}{l}") for l in range(DEPTH)]

        ring = sb("ring", [P, CHUNKS, SLOT_W])
        wo = sb("wo", [P, OUT_CHUNKS, KPC, D])
        h = sb("h", [P, NT, D])
        xn = sb("xn", [P, NT, D])
        xT = sb("xT", [P, NK, SEQ])
        bias = sb("bias", [P, C_HEADS, SEQ])
        mix = sb("mix", [P, 6144])
        gain = sb("gain", [P, D])
        kon = sb("kon", [P, 4 * P + SEQ])
        att = sb("att", [P, 2, 2, SEQ])
        wr = sb("wr", [P, NK, ROUTES])
        br = sb("br", [P, DEPTH, ROUTES])
        sm = sb("sm", [P, 160])
        more_passes = sb("more_passes", [1, 1], INT32)
        PS = ctx.enter_context(nc.psum_tensor("PS", [P, 8, 512], FP32))
        bounce = nc.dram_tensor("bounce", [DEPTH, C_HEADS, BW], FP32, kind="Internal")

        ident = kon[:, 0:P]
        flip = kon[:, P:2 * P]
        before = kon[:, 2 * P:3 * P]
        ones = kon[:, 3 * P:4 * P]

        def at(base, *shape):
            n = int(np.prod(shape))
            ap = mix[:, base:base + n]
            if len(shape) == 2:
                ap = ap.rearrange("p (a b) -> p a b", b=shape[1])
            if len(shape) == 3:
                ap = ap.rearrange("p (a b c) -> p a b c", b=shape[1], c=shape[2])
            return ap

        qkA = at(0, 8, SEQ)
        vA = at(2048, NT, 512)
        qB = at(3072, 4, SEQ)
        kqi = at(4096, 4, SEQ)
        vB = at(5120, NT, HD)
        wI = at(5248, NT, IDX_HEADS)
        sublnb = at(5256, A_V)
        lamb = at(5384, 4, HD)
        sqA = at(5640, 504)
        qkC = at(0, 16, SEQ)
        vC = at(4096, NT, D)
        xg = at(0, NK, P)
        silu = at(1024, F)
        hid = at(1536, F)
        hidT = at(2048, NF, P)
        ye = at(2560, D)
        pick = at(3584, NT, AT_ONCE * SLOTS)
        pickw = at(3840, NT, AT_ONCE * SLOTS)
        pickT = at(4096, NT, P)
        rank = at(4352, NT, EXPERTS)
        comb = at(4416, NT, EXPERTS)
        chose = at(4480, NT, EXPERTS)
        lg = at(4544, NT, ROUTES)
        prod = at(4616, NT, EXPERTS)
        rsm = at(4680, 256)
        now, now_w, now_slots = at(4936, NT, AT_ONCE), at(4940, NT, AT_ONCE), at(4944, SLOTS)
        tk = xT[:, :, :]
        isc, cand, over, same, upto = tk[:, 0], tk[:, 1], tk[:, 2], tk[:, 3], tk[:, 4]
        drop = [tk[:, 5], tk[:, 6]]
        sq = xT[:, 7, :]
        pT = xT[:, 0:4, :].rearrange("p (a k) n -> p a (k n)", a=2)
        rows_t5, rows_rel = (att[:, a].rearrange("p a n -> p (a n)")[0:n, 0:BW] for a, n in ((0, A_HEADS + B_HEADS), (1, C_HEADS)))
        ss = sm[:, 0:2]
        rstd = sm[:, 2:4]
        half = sm[:, 4:12]
        nmax = sm[:, 12:16].rearrange("p (a b) -> p a b", b=2)
        den = sm[:, 16:48]
        rden = sm[:, 48:80]
        lsum = sm[:, 80:84]
        nlam = sm[:, 84:85]
        ssa = sm[:, 88:96]
        rsa = sm[:, 96:104]
        top8 = sm[:, 104:112]
        left = sm[:, 112:114]
        spare = sm[:, 114:116]
        gate_v = w_gate.rearrange("l e (p k) f -> l p e (k f)", k=NK)
        up_v = w_up.rearrange("l e (p k) f -> l p e (k f)", k=NK)
        down_v = w_down.rearrange("l e (p k) n -> l p e (k n)", k=NF)
        in_v = [ab_in[0].rearrange("(p k) n -> p k n", k=NK), c_in[0].rearrange("(p k) n -> p k n", k=NK)]
        out_v = [ab_out[0].rearrange("(p k) n -> p k n", k=NK), c_out[0].rearrange("(p k) n -> p k n", k=NK)]

        s_x, s_kon, s_half = sem("x_in"), sem("consts_in"), sem("half_set")
        s_tab, s_lamin = sem("tables_in"), sem("lambda_in")
        s_vec, s_vecsb, s_vecout, s_z = sem("bias_rows"), sem("bias_rows_sb"), sem("bias_rows_out"), per_layer("bias_raw_in")
        s_flip, s_bd, s_ba, s_bias = per_layer("flipped"), per_layer("bias_dve"), per_layer("bias_act"), per_layer("bias_ready")
        s_gain, s_ss, s_ms, s_rs, s_xn = sem("gain_in"), sem("squares"), sem("mean_sq"), sem("rstd"), sem("normed")
        s_turn, s_td, s_ta = sem("turned"), sem("turned_dve"), sem("turned_act")
        s_in = [sem(f"w_in_{c}") for c in range(C_CHUNKS)]
        s_wo = per_layer("w_out_in")
        s_proj, s_pa, s_pd = per_layer("projected"), per_layer("proj_act"), per_layer("proj_dve")
        s_is, s_ir, s_drop = sem("index_scores"), sem("index_relu"), sem("selection")
        s_sc, s_lo, s_ex, s_co = per_layer("scored"), per_layer("logits"), per_layer("exped"), sem("combined")
        s_tp, s_pt, s_pv, s_out = per_layer("p_turned"), per_layer("pT_ready"), per_layer("pv_done"), per_layer("out_read")
        s_ssa, s_msa, s_rsa = sem("a_squares"), sem("a_mean_sq"), sem("a_rstd")
        s_lexp, s_lred = sem("lambda_exp"), sem("lambda_sums")
        s_y, s_od = per_layer("mixed"), per_layer("out_projected")
        s_h = sem("residual")
        s_wr, s_br = per_layer("router_in"), sem("router_bias_in")
        s_lg, s_rd, s_re, s_ch, s_rk, s_go = (per_layer("route_logits"), per_layer("route_diff"), per_layer("route_exp"),
                                              per_layer("chosen"), per_layer("ranked"), per_layer("routed"))
        s_ci = [[sem(f"chunk_in{l}_{c}") for c in range(CHUNKS)] for l in range(DEPTH)]
        s_used = per_layer("chunks_used")
        s_now, s_pk, s_pw = per_layer("columns_copied"), per_layer("picked"), per_layer("pick_weighted")
        s_g, s_xg, s_pkt, s_pkT = per_layer("gathered"), per_layer("xg_ready"), per_layer("pick_turned"), per_layer("pickT_ready")
        s_si, s_hi = per_layer("silu_ready"), per_layer("hidden_ready")
        s_ht, s_hT = per_layer("hid_turned"), per_layer("hidT_ready")
        s_ya, s_yd = per_layer("ye_act"), per_layer("ye_dve")
        s_sca, s_add = per_layer("scattered"), per_layer("added")
        s_zero = sem("zeroed")
        s_dve, s_final = sem("dve_chain"), sem("final_out")

        block = ctx.enter_context(nc.Block())

        def proj_dst(l, c):
            if l == 0:
                return [qkA[:, 0:2], qkA[:, 2:4], qkA[:, 4:6], qkA[:, 6:8], vA[:, :, 0:CW], vA[:, :, CW:2 * CW],
                        qB[:, 0:2], qB[:, 2:4], kqi[:, 0:2], kqi[:, 2:4]][c]
            return qkC[:, 2 * c:2 * c + 2] if c < 8 else vC[:, :, (c - 8) * CW:(c - 7) * CW]

        @block.sync
        def _(sp):
            sp.dma_start(h[:, :, :], x[0].rearrange("(t p) d -> p t d", p=P)).then_inc(s_x, 16)
            sp.dma_start(kon[:, :], consts).then_inc(s_kon, 16)

            def w_in(l, c):
                n = min(CW, in_v[l].shape[2] - c * CW)
                dst = ring[:, c, :].rearrange("p (k n) -> p k n", n=CW)[:, :, 0:n]
                sp.dma_start(dst, in_v[l][:, :, c * CW:c * CW + n]).then_inc(s_in[c], 16)

            def w_out(l):
                for c in range(OUT_CHUNKS):
                    sp.dma_start(wo[:, c], out_v[l][:, c * KPC:(c + 1) * KPC, :]).then_inc(s_wo[l], 16)

            def chunk(l, pair, c):
                if c < 2 * UP_CHUNKS:
                    src, j, w = (gate_v, c, KPU * F) if c < UP_CHUNKS else (up_v, c - UP_CHUNKS, KPU * F)
                else:
                    src, j, w = down_v, c - 2 * UP_CHUNKS, D
                sp.dma_start(ring[:, c, :].rearrange("p (e n) -> p e n", e=AT_ONCE),
                             src[l, :, bass.ds(pair * AT_ONCE, AT_ONCE), j * w:(j + 1) * w]).then_inc(s_ci[l][c], 16)

            for l in range(DEPTH):
                for c in range(IN_CHUNKS[l]):
                    if l:
                        sp.wait_ge(s_used[0], CHUNKS * (trips - 1) + c + 1)
                    w_in(l, c)
                if l:
                    sp.wait_ge(s_od[0], 4)
                w_out(l)
                for c in range(CHUNKS):
                    if c < IN_CHUNKS[l]:
                        sp.wait_ge(s_proj[l], c + 1)
                    chunk(l, 0, c)
                sp.wait_ge(s_go[l], 1)
                trips = sp.snap(sp.value_load(more_passes[0:1, 0:1], min_val=0, max_val=MAX_PASSES - 1) * PAIRS + PAIRS)
                with sp.Fori(0, trips - 1) as i:
                    for c in range(CHUNKS):
                        sp.wait_ge(s_used[l], i * CHUNKS + (c + 1))
                        chunk(l, (i + 1) % PAIRS, c)
            sp.wait_ge(s_xn, 2 * 5)
            sp.dma_start(out[0].rearrange("(t p) d -> p t d", p=P), xn[:, :, :]).then_inc(s_final, 16)
            sp.wait_ge(s_final, 16)

        @block.gpsimd
        def _(pool):
            pool.memset(half, -0.5).then_inc(s_half, 1)
            pool.dma_start(xn[0:BUCKETS, 0, 0:BW], hot_t5).then_inc(s_tab, 16)
            pool.dma_start(xn[0:BUCKETS, 0, BW:BW + A_HEADS + B_HEADS], t5).then_inc(s_tab, 16)
            pool.dma_start(xn[:, 1, 0:2 * BW], hot_rel.rearrange("(a p) n -> p a n", p=P)).then_inc(s_tab, 16)
            pool.dma_start(xn[:, 1, 2 * BW:2 * BW + 2 * C_HEADS],
                           rel[0, 1:1 + 2 * P, :].rearrange("(a p) n -> p a n", p=P)).then_inc(s_tab, 16)
            pool.dma_start(lamb, lam[0:1].broadcast_to((P, 4, HD))).then_inc(s_lamin, 16)
            pool.dma_start(sublnb, subln[0:1].broadcast_to((P, A_V))).then_inc(s_lamin, 16)
            for l in range(DEPTH):
                pool.dma_start(br[:, l, 0:GROUPS], b_rg[l:l + 1].broadcast_to((P, GROUPS))).then_inc(s_br, 16)
                pool.dma_start(br[:, l, GROUPS:ROUTES], b_re[l:l + 1].broadcast_to((P, EXPERTS))).then_inc(s_br, 16)
            pool.wait_ge(s_vecsb, 2)
            pool.dma_start(bounce.ap()[0, 0:A_HEADS + B_HEADS], rows_t5).then_inc(s_vecout, 16)
            pool.dma_start(bounce.ap()[1], rows_rel).then_inc(s_vecout, 16)
            pool.wait_ge(s_vecout, 32)

            def raw_bias(l, heads):
                pool.dma_start(bias[:, 0:heads, :], bass.AP(bounce, l * C_HEADS * BW, [[1, P], [BW, heads], [1, SEQ]]))\
                    .then_inc(s_z[l], 16)

            def mask_bias(l, heads):
                pool.wait_ge(s_bd[l], -(-heads // 4))
                pool.wait_ge(s_ba[l], heads // 4)
                pool.memset(bias[0:CHUNK, 0:heads, SEQ - CHUNK:SEQ], NEG).then_inc(s_bias[l], 1)

            def rstd_of(n):
                pool.wait_ge(s_ss, 2 * n + 2)
                pool.tensor_scalar(rstd, ss, 1.0 / D, EPS, ALU.mult, ALU.add).then_inc(s_ms, 1)
                pool.wait_ge(s_ms, n + 1)
                pool.tensor_tensor(rstd, rstd, half[:, 0:2], ALU.pow).then_inc(s_rs, 1)

            def carry_waits(site):
                pool.tensor_tensor(spare[:, site:site + 1], half[:, 0:1], half[:, 0:1], ALU.mult)

            raw_bias(0, A_HEADS + B_HEADS)
            rstd_of(0)
            pool.wait_ge(s_half, 1)
            mask_bias(0, A_HEADS + B_HEADS)
            for l in range(DEPTH):
                pool.dma_start(wr[:, :, 0:GROUPS], w_rg[l].rearrange("(p k) g -> p k g", k=NK)).then_inc(s_wr[l], 16)
                pool.dma_start(wr[:, :, GROUPS:ROUTES], w_re[l].rearrange("(p k) g -> p k g", k=NK)).then_inc(s_wr[l], 16)
                if l == 0:
                    for qt in range(NT):
                        pool.wait_ge(s_ssa, qt + 1)
                        pool.tensor_scalar(rsa[:, 4 * qt:4 * qt + 4], ssa[:, 4 * qt:4 * qt + 4], 1.0 / A_V, EPS,
                                           ALU.mult, ALU.add).then_inc(s_msa, 1)
                        pool.wait_ge(s_msa, qt + 1)
                        pool.tensor_tensor(rsa[:, 4 * qt:4 * qt + 4], rsa[:, 4 * qt:4 * qt + 4], half[:, 0:4],
                                           ALU.pow).then_inc(s_rsa, 1)
                rstd_of(2 * l + 1)
                if l == 0:
                    pool.wait_ge(s_lo[0], UNITS)
                    raw_bias(1, C_HEADS)
                    mask_bias(1, C_HEADS)
                pool.wait_ge(s_go[l], 1)
                more = pool.value_load(more_passes[0:1, 0:1], min_val=0, max_val=MAX_PASSES - 1)

                def pick_rows(i, first):
                    experts = bass.ds(i % PAIRS * AT_ONCE, AT_ONCE)
                    if not first:
                        pool.wait_ge(s_pw[l], i * PICKS)
                    pool.tensor_copy(now, rank[:, :, experts]).then_inc(s_now[l], 1)
                    pool.tensor_copy(now_w, comb[:, :, experts]).then_inc(s_now[l], 1)
                    pool.tensor_copy(now_slots, kon[:, bass.ds(i // PAIRS * SLOTS + 4 * P, SLOTS)]).then_inc(s_now[l], 1)
                    pool.wait_ge(s_now[l], i * 3 + 3)
                    if not first:
                        pool.wait_ge(s_g[l], i * 2)
                        carry_waits(0)
                    for t in range(NT):
                        for e in range(AT_ONCE):
                            pool.tensor_scalar(pick[:, t, e * SLOTS:(e + 1) * SLOTS], now_slots, now[:, t, e:e + 1],
                                               None, ALU.is_equal).then_inc(s_pk[l], 1)
                    if not first:
                        pool.wait_ge(s_pkt[l], i)
                        carry_waits(1)
                    for t in range(NT):
                        for e in range(AT_ONCE):
                            pool.tensor_scalar(pickw[:, t, e * SLOTS:(e + 1) * SLOTS], now_slots, now[:, t, e:e + 1],
                                               now_w[:, t, e:e + 1], ALU.is_equal, ALU.mult).then_inc(s_pw[l], 1)

                pick_rows(0, True)
                with pool.Fori(0, pool.snap(more * PAIRS + (PAIRS - 1))) as before_it:
                    pick_rows(before_it + 1, False)
                if l + 1 < DEPTH:
                    rstd_of(2 * l + 2)
            rstd_of(2 * DEPTH)

        @block.scalar
        def _(act):
            gains = [ln_mix[0:1], ln_ffn[0:1], ln_mix[1:2], ln_ffn[1:2], ln_final.rearrange("(a d) -> a d", a=1)]

            def load_gain(n):
                if n:
                    act.wait_ge(s_xn, 2 * n)
                act.dma_start(gain[:, :], gains[n].broadcast_to((P, D))).then_inc(s_gain, 16)

            def turn_copy(j):
                for b in (1, 3):
                    act.wait_ge(s_turn, 4 * j + b + 1)
                    act.activation(xT[:, 2 * b:2 * b + 2, :], PS[:, b].rearrange("p (k n) -> p k n", k=2), ACT.Copy)\
                        .then_inc(s_ta, 1)

            def bias_copy(l, heads):
                for b in range(1, heads // 2, 2):
                    act.wait_ge(s_flip[l], b + 1)
                    act.activation(bias[:, 2 * b:2 * b + 2, :], PS[:, b].rearrange("p (a n) -> p a n", a=2), ACT.Copy)\
                        .then_inc(s_ba[l], 1)

            def attention(l):
                def exps(u):
                    act.wait_ge(s_lo[l], u + 1)
                    n = unit_of(l, u)[3]
                    for j in range(2):
                        act.activation(att[:, u % 2, j, 0:n], att[:, u % 2, j, 0:n], ACT.Exp, bias=nmax[:, u % 2, j:j + 1],
                                       accum_out=den[:, 2 * u + j:2 * u + j + 1]).then_inc(s_ex[l], 1)

                def probs_copy(u):
                    kind, _, _, n = unit_of(l, u)
                    w = n if kind == "a" else 2 * n
                    act.wait_ge(s_tp[l], u + 1)
                    if u >= 2:
                        act.wait_ge(s_pv[l], u - 1)
                    act.activation(pT[:, u % 2, 0:w], PS[:, 4 + u % 2, 0:w], ACT.Copy).then_inc(s_pt[l], 1)

                for u in range(UNITS + 1):
                    if u < UNITS:
                        exps(u)
                    if u >= 1:
                        probs_copy(u - 1)

            load_gain(0)
            act.wait_ge(s_vec, 2)
            act.activation(rows_rel, PS[0:C_HEADS, 5, 0:BW], ACT.Copy).then_inc(s_vecsb, 1)
            turn_copy(0)
            bias_copy(0, A_HEADS + B_HEADS)
            act.wait_ge(s_lred, 2)
            act.activation(lsum[:, 2:4], lsum[:, 0:2], ACT.Exp).then_inc(s_lexp, 1)
            for l in range(DEPTH):
                if l:
                    turn_copy(3 * l)
                for c in range(0, IN_CHUNKS[l], 2):
                    act.wait_ge(s_proj[l], c + 1)
                    act.activation(proj_dst(l, c), PS[:, (4 + c) % 8].rearrange("p (a n) -> p a n", a=2), ACT.Copy)\
                        .then_inc(s_pa[l], 1)
                if l == 0:
                    act.wait_ge(s_proj[0], A_CHUNKS)
                    act.activation(vB, PS[:, 6, 0:NT * HD].rearrange("p (t n) -> p t n", t=NT), ACT.Copy).then_inc(s_pa[0], 1)
                    act.activation(wI, PS[:, 6, NT * HD:NT * (HD + IDX_HEADS)].rearrange("p (t n) -> p t n", t=NT), ACT.Copy,
                                   scale=(IDX_HEADS ** -0.5) * (HD ** -0.5)).then_inc(s_pa[0], 1)
                    for v in range(4):
                        n = P * (v // 2 + 1)
                        act.wait_ge(s_is, v + 1)
                        if v == 0:
                            act.wait_ge(s_vecout, 32)
                        if v >= 2:
                            act.wait_ge(s_drop, 2 * (v - 1))
                        act.activation(att[:, v % 2, :, 0:n], PS[:, 2 * (v % 2):2 * (v % 2) + 2, 0:n], ACT.Relu).then_inc(s_ir, 1)
                attention(l)
                load_gain(2 * l + 1)
                turn_copy(3 * l + 1)
                turn_copy(3 * l + 2)
                act.wait_ge(s_rd[l], 1)
                act.activation(rsm[:, 8:16], rsm[:, 0:8], ACT.Exp).then_inc(s_re[l], 1)
                act.wait_ge(s_rd[l], 2)
                act.activation(rsm[:, 32:48], rsm[:, 16:32], ACT.Exp).then_inc(s_re[l], 1)
                load_gain(2 * l + 2)
                if l == 0:
                    bias_copy(1, C_HEADS)
                act.wait_ge(s_go[l], 1)
                more = act.value_load(more_passes[0:1, 0:1], min_val=0, max_val=MAX_PASSES - 1)

                def experts(i, first):
                    for b in range(2):
                        act.wait_ge(s_g[l], i * 2 + (b + 1))
                        if b == 0 and not first:
                            act.wait_ge(s_used[l], i * CHUNKS)
                        act.activation(xg[:, 4 * b:4 * b + 4, :], PS[:, b].rearrange("p (k n) -> p k n", k=4), ACT.Copy)\
                            .then_inc(s_xg[l], 1)
                    act.wait_ge(s_used[l], i * CHUNKS + UP_CHUNKS)
                    if not first:
                        act.wait_ge(s_hi[l], i)
                    act.activation(silu, PS[:, 2], ACT.Silu).then_inc(s_si[l], 1)
                    act.wait_ge(s_ht[l], i + 1)
                    act.activation(hidT, PS[:, 4].rearrange("p (k n) -> p k n", k=NF), ACT.Copy).then_inc(s_hT[l], 1)
                    act.wait_ge(s_used[l], i * CHUNKS + CHUNKS)
                    if not first:
                        act.wait_ge(s_sca[l], i * 4)
                    act.activation(ye[:, 0:512], PS[:, 6], ACT.Copy).then_inc(s_ya[l], 1)

                experts(0, True)
                with act.Fori(0, act.snap(more * PAIRS + (PAIRS - 1))) as before_it:
                    experts(before_it + 1, False)

        @block.vector
        def _(dve):
            chain = [0]

            def link(ins):
                chain[0] += 1
                ins.then_inc(s_dve, 1)
                dve.wait_ge(s_dve, chain[0])

            def norm(n):
                for t in range(NT):
                    dve.tensor_tensor_reduce(xn[:, t], h[:, t], h[:, t], 1.0, 0.0, ALU.mult, ALU.add, ss[:, t:t + 1])\
                        .then_inc(s_ss, 1)
                dve.wait_ge(s_rs, n + 1)
                dve.wait_ge(s_gain, 16 * (n + 1))
                for t in range(NT):
                    dve.scalar_tensor_tensor(xn[:, t], h[:, t], rstd[:, t:t + 1], gain[:, :], ALU.mult, ALU.mult)\
                        .then_inc(s_xn, 1)

            def turn_copy(j):
                for b in (0, 2):
                    dve.wait_ge(s_turn, 4 * j + b + 1)
                    dve.tensor_copy(xT[:, 2 * b:2 * b + 2, :], PS[:, b].rearrange("p (k n) -> p k n", k=2)).then_inc(s_td, 1)

            def bias_copy(l, heads):
                for b in range(0, heads // 2, 2):
                    dve.wait_ge(s_flip[l], b + 1)
                    dve.tensor_copy(bias[:, 2 * b:2 * b + 2, :], PS[:, b].rearrange("p (a n) -> p a n", a=2))\
                        .then_inc(s_bd[l], 1)

            def first_of(k, scores, top, out_sel, w):
                link(dve.tensor_scalar(over[:, 0:w], scores, top, 0.0, ALU.is_gt, ALU.add, accum_out=left[:, 0:1]))
                link(dve.tensor_scalar(same[:, 0:w], scores, top, None, ALU.is_equal))
                link(dve.tensor_scalar(left[:, 1:2], left[:, 0:1], -1.0, float(k), ALU.mult, ALU.add))
                link(dve.tensor_tensor_scan(upto[:, 0:w], same[:, 0:w], same[:, 0:w], 0.0, ALU.add, ALU.max))
                link(dve.scalar_tensor_tensor(same[:, 0:w], upto[:, 0:w], left[:, 1:2], same[:, 0:w], ALU.is_le, ALU.mult))
                link(dve.tensor_tensor(out_sel, same[:, 0:w], over[:, 0:w], ALU.add))

            def select(qt):
                n = P * (qt + 1)
                for v in range(2):
                    dve.wait_ge(s_ir, 2 * qt + v + 1)
                    for j in range(2):
                        hd = 2 * v + j
                        if hd == 0:
                            ins = dve.tensor_scalar(isc[:, 0:n], att[:, 0, 0, 0:n], wI[:, qt, 0:1], None, ALU.mult)
                        else:
                            ins = dve.scalar_tensor_tensor(isc[:, 0:n], att[:, v, j, 0:n], wI[:, qt, hd:hd + 1],
                                                           isc[:, 0:n], ALU.mult, ALU.add)
                        ins.then_inc(s_drop, 1)
                        dve.wait_ge(s_drop, 4 * qt + hd + 1)
                link(dve.memset(isc[0:CHUNK, n - CHUNK:n], NEG))
                link(dve.tensor_copy(cand[:, 0:n], isc[:, 0:n]))
                for r in range(TOPK // 8):
                    link(dve.max(top8, cand[:, 0:n]))
                    if r + 1 < TOPK // 8:
                        link(dve.match_replace(cand[:, 0:n], top8, cand[:, 0:n], GONE))
                first_of(TOPK, isc[:, 0:n], top8[:, 7:8], same[:, 0:n], n)
                link(dve.tensor_scalar(drop[qt][:, 0:n], same[:, 0:n], -1.0, -NEG, ALU.add, ALU.mult))

            def attention(l):
                def logits(u):
                    kind, j, qt, n = unit_of(l, u)
                    hd = {"a": j, "b": A_HEADS + 2 * j, "c": 2 * j}[kind]
                    if kind == "a":
                        tile = bias[:, hd:hd + 1, SEQ - n:SEQ].broadcast_to((P, 2, n))
                    else:
                        tile = bias[:, hd:hd + 2, SEQ - n:SEQ]
                    dve.wait_ge(s_sc[l], u + 1)
                    if u >= 2:
                        dve.wait_ge(s_tp[l], u - 1)
                    a = att[:, u % 2, :, 0:n]
                    link(dve.scalar_tensor_tensor(a, PS[:, 2 * (u % 2):2 * (u % 2) + 2, 0:n], SCALE, tile, ALU.mult, ALU.add))
                    if kind == "b":
                        link(dve.tensor_tensor(a, a, drop[qt][:, 0:n].unsqueeze(1).broadcast_to((P, 2, n)), ALU.add))
                    dve.tensor_reduce(nmax[:, u % 2, :], a, AX.X, ALU.max, negate=True).then_inc(s_lo[l], 1)

                def combine(u):
                    n = unit_of(l, u)[3]
                    dve.wait_ge(s_ex[l], 2 * u + 2)
                    link(dve.reciprocal(rden[:, 2 * u:2 * u + 2], den[:, 2 * u:2 * u + 2]))
                    link(dve.tensor_scalar(rden[:, 2 * u + 1:2 * u + 2], rden[:, 2 * u + 1:2 * u + 2], nlam, None, ALU.mult))
                    link(dve.tensor_scalar(att[:, u % 2, 1, 0:n], att[:, u % 2, 1, 0:n], rden[:, 2 * u + 1:2 * u + 2], None, ALU.mult))
                    dve.scalar_tensor_tensor(att[:, u % 2, 0, 0:n], att[:, u % 2, 0, 0:n], rden[:, 2 * u:2 * u + 1],
                                             att[:, u % 2, 1, 0:n], ALU.mult, ALU.add).then_inc(s_co, 1)

                def outputs(u):
                    kind, _, qt, _ = unit_of(l, u)
                    dve.wait_ge(s_pv[l], u + 1)
                    if kind == "a":
                        o = PS[:, 6 + qt].rearrange("p (a n) -> p a n", n=A_V)
                        ya = xn[:, qt, 0:512].rearrange("p (a n) -> p a n", n=A_V)
                        yb = xn[:, qt, 512:1024].rearrange("p (a n) -> p a n", n=A_V)
                        ins = dve.tensor_copy(ya, o)
                        link(ins)
                        link(dve.tensor_tensor(yb, ya, ya, ALU.mult))
                        dve.tensor_reduce(ssa[:, 4 * qt:4 * qt + 4], yb, AX.X, ALU.add).then_inc(s_ssa, 1)
                        dve.wait_ge(s_rsa, qt + 1)
                        link(dve.tensor_tensor(ya, ya, rsa[:, 4 * qt:4 * qt + 4].unsqueeze(2).broadcast_to((P, 4, A_V)), ALU.mult))
                        dve.tensor_tensor(ya, ya, sublnb.unsqueeze(1).broadcast_to((P, 4, A_V)), ALU.mult).then_inc(s_out[l], 1)
                        return
                    first, heads, col, bank = (8 + 4 * qt, 8, 512, 6 + qt) if kind == "b" else (8 * qt, 16, 0, 6)
                    r = rden[:, 2 * first:2 * first + heads]
                    dve.wait_ge(s_ex[l], 2 * u + 2)
                    link(dve.reciprocal(r, den[:, 2 * first:2 * first + heads]))
                    for b in range(heads // 8):
                        dve.tensor_tensor(xn[:, qt, col + 512 * b:col + 512 * b + 512].rearrange("p (a n) -> p a n", n=HD),
                                          PS[:, bank + b].rearrange("p (a n) -> p a n", n=HD),
                                          r[:, 8 * b:8 * b + 8].unsqueeze(2).broadcast_to((P, 8, HD)), ALU.mult).then_inc(s_out[l], 1)

                last = last_units(l)
                for u in range(UNITS + 3):
                    if u < UNITS:
                        logits(u)
                    if 1 <= u <= UNITS and unit_of(l, u - 1)[0] == "a":
                        combine(u - 1)
                    if u - 3 in last:
                        outputs(u - 3)

            def residual(l):
                for q in range(4):
                    t, n = q // 2, q % 2
                    dve.wait_ge(s_od[l], q + 1)
                    link(dve.tensor_tensor(h[:, t, 512 * n:512 * n + 512], PS[:, 4 + q], h[:, t, 512 * n:512 * n + 512], ALU.add))

            def route(l):
                g2, e2 = (P, NT, GROUPS), (P, NT, GROUPS, PER_GROUP)
                view = lambda a, n: a.rearrange("p (t n) -> p t n", n=n)
                gd, ge = view(rsm[:, 0:8], GROUPS), view(rsm[:, 8:16], GROUPS)
                ed, ee = view(rsm[:, 16:32], PER_GROUP), view(rsm[:, 32:48], PER_GROUP)
                group = view(rsm[:, 48:56], GROUPS)
                upg = view(rsm[:, 56:64], GROUPS)
                es = view(rsm[:, 64:80], PER_GROUP)
                sel = view(rsm[:, 80:96], PER_GROUP)
                t8 = view(rsm[:, 96:112], 8)
                mor = view(rsm[:, 112:128], PER_GROUP)
                sam = view(rsm[:, 128:144], PER_GROUP)
                upe = view(rsm[:, 144:160], PER_GROUP)
                gm, gs, em, es1, cnt, fac = (rsm[:, 160 + 2 * j:162 + 2 * j] for j in range(6))
                mxc = rsm[:, 180:181]
                stp = rsm[:, 184:188]
                lgg = lg[:, :, 0:GROUPS]
                wide = lambda a, s: a.unsqueeze(2).broadcast_to(s)
                dve.wait_ge(s_lg[l], 1)
                dve.wait_ge(s_br, 16 * 4)
                link(dve.tensor_tensor(lg, PS[:, 4, 0:NT * ROUTES].rearrange("p (t n) -> p t n", t=NT),
                                       br[:, l].unsqueeze(1).broadcast_to((P, NT, ROUTES)), ALU.add))
                link(dve.tensor_reduce(gm, lgg, AX.X, ALU.max))
                dve.tensor_tensor(gd, lgg, wide(gm, g2), ALU.subtract).then_inc(s_rd[l], 1)
                link(dve.tensor_tensor(group, lgg, wide(gm, g2), ALU.is_equal))
                for t in range(NT):
                    link(dve.tensor_tensor_scan(upg[:, t], group[:, t], group[:, t], 0.0, ALU.add, ALU.max))
                link(dve.scalar_tensor_tensor(group, upg, 1.0, group, ALU.is_le, ALU.mult))
                dve.wait_ge(s_re[l], 1)
                link(dve.tensor_reduce(gs, ge, AX.X, ALU.add))
                link(dve.reciprocal(gs, gs))
                for t in range(NT):
                    link(dve.tensor_tensor(prod[:, t].rearrange("p (g e) -> p g e", g=GROUPS),
                                           lg[:, t, GROUPS:ROUTES].rearrange("p (g e) -> p g e", g=GROUPS),
                                           group[:, t].unsqueeze(2).broadcast_to((P, GROUPS, PER_GROUP)), ALU.mult))
                    link(dve.tensor_reduce(es[:, t], prod[:, t].rearrange("p (g e) -> p e g", g=GROUPS), AX.X, ALU.add))
                link(dve.tensor_reduce(em, es, AX.X, ALU.max))
                dve.tensor_tensor(ed, es, wide(em, (P, NT, PER_GROUP)), ALU.subtract).then_inc(s_rd[l], 1)
                dve.wait_ge(s_re[l], 2)
                for t in range(NT):
                    link(dve.max(t8[:, t], ee[:, t]))
                    link(dve.tensor_scalar(mor[:, t], ee[:, t], t8[:, t, 1:2], 0.0, ALU.is_gt, ALU.add, accum_out=cnt[:, t:t + 1]))
                    link(dve.tensor_scalar(sam[:, t], ee[:, t], t8[:, t, 1:2], None, ALU.is_equal))
                    link(dve.tensor_tensor_scan(upe[:, t], sam[:, t], sam[:, t], 0.0, ALU.add, ALU.max))
                link(dve.tensor_scalar(cnt, cnt, -1.0, float(TOP_EXPERTS), ALU.mult, ALU.add))
                for t in range(NT):
                    link(dve.scalar_tensor_tensor(sam[:, t], upe[:, t], cnt[:, t:t + 1], sam[:, t], ALU.is_le, ALU.mult))
                link(dve.tensor_tensor(sel, sam, mor, ALU.add))
                link(dve.tensor_tensor(ee, ee, sel, ALU.mult))
                link(dve.tensor_reduce(es1, ee, AX.X, ALU.add))
                link(dve.reciprocal(fac, es1))
                link(dve.tensor_tensor(fac, fac, gs, ALU.mult))
                link(dve.tensor_tensor(ee, ee, wide(fac, (P, NT, PER_GROUP)), ALU.mult))
                for t in range(NT):
                    g4 = group[:, t].unsqueeze(2).broadcast_to((P, GROUPS, PER_GROUP))
                    link(dve.tensor_tensor(comb[:, t].rearrange("p (g e) -> p g e", g=GROUPS), g4,
                                           ee[:, t].unsqueeze(1).broadcast_to((P, GROUPS, PER_GROUP)), ALU.mult))
                    dve.tensor_tensor(chose[:, t].rearrange("p (g e) -> p g e", g=GROUPS), g4,
                                      sel[:, t].unsqueeze(1).broadcast_to((P, GROUPS, PER_GROUP)), ALU.mult).then_inc(s_ch[l], 1)
                dve.wait_ge(s_ch[l], 2)
                dve.wait_ge(s_rk[l], 1)
                link(dve.scalar_tensor_tensor(rank, PS[:, 5, 0:NT * EXPERTS].rearrange("p (t n) -> p t n", t=NT), 1.0, chose,
                                              ALU.add, ALU.mult))
                link(dve.tensor_scalar(rank, rank, -1.0, None, ALU.add))
                link(dve.tensor_reduce(mxc, PS[:, 5, NT * EXPERTS:(NT + 1) * EXPERTS], AX.X, ALU.max))
                for j in range(1, MAX_PASSES):
                    link(dve.tensor_scalar(stp[:, j:j + 1], mxc, float(SLOTS * j), None, ALU.is_gt))
                link(dve.tensor_reduce(stp[:, 0:1], stp[:, 1:MAX_PASSES], AX.X, ALU.add))
                dve.tensor_copy(more_passes[:, :], stp[0:1, 0:1]).then_inc(s_go[l], 1)

            dve.wait_ge(s_vec, 1)
            dve.tensor_copy(rows_t5, PS[0:A_HEADS + B_HEADS, 4, 0:BW]).then_inc(s_vecsb, 1)
            dve.wait_ge(s_vec, 2)
            dve.wait_ge(s_x, 16)
            norm(0)
            turn_copy(0)
            bias_copy(0, A_HEADS + B_HEADS)
            dve.wait_ge(s_lamin, 32)
            for j in range(2):
                link(dve.tensor_tensor(lamb[:, 2 * j], lamb[:, 2 * j], lamb[:, 2 * j + 1], ALU.mult))
                dve.tensor_reduce(lsum[:, j:j + 1], lamb[:, 2 * j], AX.X, ALU.add).then_inc(s_lred, 1)
            dve.wait_ge(s_lexp, 1)
            link(dve.tensor_tensor(nlam, lsum[:, 3:4], lsum[:, 2:3], ALU.subtract))
            link(dve.tensor_scalar(nlam, nlam, -LAM_INIT, None, ALU.add))
            link(dve.tensor_scalar(sublnb, sublnb, 1.0 - LAM_INIT, None, ALU.mult))
            for l in range(DEPTH):
                if l:
                    norm(2 * l)
                    turn_copy(3 * l)
                for c in range(1, IN_CHUNKS[l], 2):
                    dve.wait_ge(s_proj[l], c + 1)
                    dve.tensor_copy(proj_dst(l, c), PS[:, (4 + c) % 8].rearrange("p (a n) -> p a n", a=2)).then_inc(s_pd[l], 1)
                if l == 0:
                    dve.wait_ge(s_pa[0], 7)
                    for qt in range(NT):
                        select(qt)
                dve.wait_ge(s_bias[l], 1)
                attention(l)
                dve.wait_ge(s_out[l], 4)
                dve.nop().then_inc(s_y[l], 1)
                turn_copy(3 * l + 1)
                residual(l)
                norm(2 * l + 1)
                turn_copy(3 * l + 2)
                route(l)
                if l == 0:
                    bias_copy(1, C_HEADS)
                dve.wait_ge(s_go[l], 1)
                more = dve.value_load(more_passes[0:1, 0:1], min_val=0, max_val=MAX_PASSES - 1)
                trips = dve.snap(more * PAIRS + PAIRS)

                def experts(i, first):
                    dve.wait_ge(s_pkt[l], i + 1)
                    if not first:
                        dve.wait_ge(s_sca[l], i * 4)
                    dve.tensor_copy(pickT, PS[:, 5, 0:NT * P].rearrange("p (t n) -> p t n", t=NT)).then_inc(s_pkT[l], 1)
                    dve.wait_ge(s_used[l], i * CHUNKS + 2 * UP_CHUNKS)
                    dve.wait_ge(s_si[l], i + 1)
                    if not first:
                        dve.wait_ge(s_ht[l], i)
                    dve.tensor_tensor(hid, PS[:, 3], silu, ALU.mult).then_inc(s_hi[l], 1)
                    dve.wait_ge(s_used[l], i * CHUNKS + CHUNKS)
                    if not first:
                        dve.wait_ge(s_sca[l], i * 4)
                    dve.tensor_copy(ye[:, 512:1024], PS[:, 7]).then_inc(s_yd[l], 1)
                    if not first:
                        dve.wait_ge(s_add[l], i * 4)
                    for q in range(4):
                        n, t = q // 2, q % 2
                        dve.wait_ge(s_sca[l], i * 4 + (q + 1))
                        dve.tensor_tensor(h[:, t, 512 * n:512 * n + 512], PS[:, t], h[:, t, 512 * n:512 * n + 512],
                                          ALU.add).then_inc(s_add[l], 1)

                experts(0, True)
                with dve.Fori(0, trips - 1) as before_it:
                    experts(before_it + 1, False)
                dve.wait_ge(s_add[l], trips * 4)
            norm(2 * DEPTH)

        @block.tensor
        def _(pe):
            mm = nc.tensor.matmul
            turns = [0]

            def turn():
                for b in range(4):
                    for kk in range(2):
                        for t in range(NT):
                            last = nc.tensor.transpose(PS[:, b, (kk * NT + t) * P:(kk * NT + t + 1) * P],
                                                       xn[:, t, 2 * b + kk:D:NK], ident)
                    last.then_inc(s_turn, 1)
                turns[0] += 1

            def turned():
                pe.wait_ge(s_td, 2 * turns[0])
                pe.wait_ge(s_ta, 2 * turns[0])

            def make_bias(l, heads):
                pe.wait_ge(s_z[l], 16)
                for b in range(heads // 2):
                    mm(PS[:, b], flip, bias[:, 2 * b:2 * b + 2, :], start=True, stop=True).then_inc(s_flip[l], 1)

            def project(l):
                for c in range(IN_CHUNKS[l]):
                    w = ring[:, c, :].rearrange("p (k n) -> p k n", n=CW)
                    pe.wait_ge(s_in[c], 32 if l and c < A_CHUNKS else 16)
                    if c >= 8:
                        pe.wait_ge((s_pa if c % 2 == 0 else s_pd)[l], (c - 8) // 2 + 1)
                    bank = PS[:, (4 + c) % 8]
                    transposed = c not in (4, 5) if l == 0 else c < 8
                    if transposed:
                        tiles = {(0, 8): [(0, True), (128, False)], (0, 9): [(0, False), (128, True)]}\
                            .get((l, c), [(0, False), (128, False)])
                        for j, (col, twice) in enumerate(tiles):
                            for k in range(NK):
                                for r in range(2) if twice else [None]:
                                    rows = slice(0, P) if r is None else slice(HD * r, HD * r + HD)
                                    last = mm(bank[rows, j * SEQ:(j + 1) * SEQ], w[:, k, col:col + (P if r is None else HD)],
                                              xT[:, k, :], start=(k == 0), stop=(k == NK - 1))
                    else:
                        for t in range(NT):
                            for k in range(NK):
                                last = mm(bank[:, t * CW:(t + 1) * CW], xT[:, k, t * P:(t + 1) * P], w[:, k, :],
                                          start=(k == 0), stop=(k == NK - 1))
                    if l == 0 and c >= 8:
                        if c == 8:
                            pe.wait_ge(s_pa[0], 2)
                        col, n, o = (HD, HD, 0) if c == 8 else (3 * HD, IDX_HEADS, NT * HD)
                        for t in range(NT):
                            for k in range(NK):
                                extra = mm(PS[:, 6, o + t * n:o + t * n + n], xT[:, k, t * P:(t + 1) * P], w[:, k, col:col + n],
                                           start=(k == 0), stop=(k == NK - 1))
                        last = extra
                    last.then_inc(s_proj[l], 1)
                pe.wait_ge(s_pa[l], IN_CHUNKS[l] // 2 + (2 if l == 0 else 0))
                pe.wait_ge(s_pd[l], IN_CHUNKS[l] // 2)

            def pair_scores(v, q, ka, kb, qt, n, signal):
                for j, kt in enumerate((ka, kb)):
                    last = mm(PS[:, 2 * (v % 2) + j, 0:n], q[HD * j:HD * j + HD, qt * P:(qt + 1) * P], kt[HD * j:HD * j + HD, 0:n],
                              start=True, stop=True)
                last.then_inc(signal, 1)

            def index_scores():
                for v in range(4):
                    if v >= 2:
                        pe.wait_ge(s_ir, v - 1)
                    pair_scores(v, kqi[:, 1 + v % 2], kqi[:, 3], kqi[:, 3], v // 2, P * (v // 2 + 1), s_is)
                pe.wait_ge(s_ir, 4)

            def attention(l):
                def scores(u):
                    kind, j, qt, n = unit_of(l, u)
                    if kind == "a":
                        q, kt = qkA[:, j], qkA[:, 4 + j]
                    elif kind == "b":
                        q, kt = qB[:, j], kqi[:, 0]
                    else:
                        q, kt = qkC[:, j], qkC[:, 8 + j]
                    if u >= 2:
                        pe.wait_ge(s_lo[l], u - 1)
                    pair_scores(u, q, kt, kt, qt, n, s_sc[l])

                def turn_probs(u):
                    kind, _, qt, n = unit_of(l, u)
                    if kind == "a":
                        pe.wait_ge(s_co, u + 1)
                    else:
                        pe.wait_ge(s_ex[l], 2 * u + 2)
                    if u >= 2:
                        pe.wait_ge(s_pt[l], u - 1)
                    for j in range(1 if kind == "a" else 2):
                        for kt in range(n // P):
                            o = (j * (n // P) + kt) * P
                            last = nc.tensor.transpose(PS[:, 4 + u % 2, o:o + P], att[:, u % 2, j, kt * P:(kt + 1) * P], ident)
                    last.then_inc(s_tp[l], 1)

                def values(u):
                    kind, i, qt, n = unit_of(l, u)
                    pe.wait_ge(s_pt[l], u + 1)
                    if kind == "b" and i == 0:
                        pe.wait_ge(s_out[0], qt + 1)
                    if kind == "c" and u == 8:
                        pe.wait_ge(s_out[1], 2)
                    for j in range(1 if kind == "a" else 2):
                        for kt in range(n // P):
                            o = (j * (n // P) + kt) * P
                            if kind == "a":
                                dst, v = PS[:, 6 + qt, i * A_V:(i + 1) * A_V], vA[:, kt, i * A_V:(i + 1) * A_V]
                            elif kind == "b":
                                dst, v = PS[:, 6 + qt, (2 * i + j) * HD:(2 * i + j + 1) * HD], vB[:, kt]
                            else:
                                hd = 2 * i + j
                                dst, v = PS[:, 6 + hd // 8, hd % 8 * HD:(hd % 8 + 1) * HD], vC[:, kt, hd * HD:(hd + 1) * HD]
                            last = mm(dst, pT[:, u % 2, o:o + P], v, start=(kt == 0), stop=(kt == n // P - 1))
                    last.then_inc(s_pv[l], 1)

                for u in range(UNITS + 2):
                    if u < UNITS:
                        scores(u)
                    if 1 <= u <= UNITS:
                        turn_probs(u - 1)
                    if u >= 2:
                        values(u - 2)

            def out_project(l):
                pe.wait_ge(s_wo[l], 16 * OUT_CHUNKS)
                for q in range(4):
                    t, n = q // 2, q % 2
                    for k in range(NK):
                        last = mm(PS[:, 4 + q], xT[:, k, t * P:(t + 1) * P], wo[:, k // KPC, k % KPC, 512 * n:512 * n + 512],
                                  start=(k == 0), stop=(k == NK - 1))
                    last.then_inc(s_od[l], 1)

            def route(l):
                pe.wait_ge(s_wr[l], 32)
                for t in range(NT):
                    for k in range(NK):
                        last = mm(PS[:, 4, t * ROUTES:(t + 1) * ROUTES], xT[:, k, t * P:(t + 1) * P], wr[:, k, :],
                                  start=(k == 0), stop=(k == NK - 1))
                last.then_inc(s_lg[l], 1)
                pe.wait_ge(s_ch[l], 2)
                mm(PS[:, 5, 0:EXPERTS], before, chose[:, 0], start=True, stop=True)
                mm(PS[:, 5, EXPERTS:2 * EXPERTS], ones, chose[:, 0], start=True, stop=False)
                mm(PS[:, 5, EXPERTS:2 * EXPERTS], before, chose[:, 1], start=False, stop=True)
                mm(PS[:, 5, 2 * EXPERTS:3 * EXPERTS], ones, chose[:, 0], start=True, stop=False)
                mm(PS[:, 5, 2 * EXPERTS:3 * EXPERTS], ones, chose[:, 1], start=False, stop=True).then_inc(s_rk[l], 1)

            def experts(l):
                more = pe.value_load(more_passes[0:1, 0:1], min_val=0, max_val=MAX_PASSES - 1)

                def pair(i, first):
                    pe.wait_ge(s_pk[l], i * PICKS + PICKS)
                    if not first:
                        pe.wait_ge(s_add[l], i * 4)
                    for b in range(2):
                        for kk in range(4):
                            for t in range(NT):
                                last = mm(PS[:, b, kk * P:(kk + 1) * P], xn[:, t, 4 * b + kk:D:NK], pick[:, t],
                                          start=(t == 0), stop=(t == NT - 1))
                        last.then_inc(s_g[l], 1)
                    pe.wait_ge(s_pw[l], i * PICKS + PICKS)
                    if not first:
                        pe.wait_ge(s_pkT[l], i)
                    for t in range(NT):
                        last = nc.tensor.transpose(PS[:, 5, t * P:(t + 1) * P], pickw[:, t], ident)
                    last.then_inc(s_pkt[l], 1)
                    for part, bank in ((0, 2), (1, 3)):
                        if not first:
                            pe.wait_ge((s_si, s_hi)[part][l], i)
                        for c in range(UP_CHUNKS):
                            ch = part * UP_CHUNKS + c
                            pe.wait_ge(s_ci[l][ch], i * 16 + 16)
                            if part == 0 and c % 2 == 0:
                                pe.wait_ge(s_xg[l], i * 2 + (c // 2 + 1))
                            w = ring[:, ch, :].rearrange("p (e k n) -> p e k n", e=AT_ONCE, k=KPU)
                            for kk in range(KPU):
                                k = c * KPU + kk
                                for e in range(AT_ONCE):
                                    last = mm(PS[e * SLOTS:(e + 1) * SLOTS, bank, :], xg[:, k, e * SLOTS:(e + 1) * SLOTS],
                                              w[:, e, kk, :], start=(k == 0), stop=(k == NK - 1))
                            last.then_inc(s_used[l], 1)
                    pe.wait_ge(s_hi[l], i + 1)
                    if not first:
                        pe.wait_ge(s_hT[l], i)
                    for k in range(NF):
                        last = nc.tensor.transpose(PS[:, 4, k * P:(k + 1) * P], hid[:, k:F:NF], ident)
                    last.then_inc(s_ht[l], 1)
                    pe.wait_ge(s_hT[l], i + 1)
                    if not first:
                        pe.wait_ge(s_ya[l], i)
                        pe.wait_ge(s_yd[l], i)
                    for k in range(NF):
                        ch = 2 * UP_CHUNKS + k
                        pe.wait_ge(s_ci[l][ch], i * 16 + 16)
                        w = ring[:, ch, :].rearrange("p (e n) -> p e n", e=AT_ONCE)
                        for n in range(2):
                            for e in range(AT_ONCE):
                                last = mm(PS[e * SLOTS:(e + 1) * SLOTS, 6 + n, :], hidT[:, k, e * SLOTS:(e + 1) * SLOTS],
                                          w[:, e, 512 * n:512 * n + 512], start=(k == 0), stop=(k == NF - 1))
                        last.then_inc(s_used[l], 1)
                    pe.wait_ge(s_pkT[l], i + 1)
                    for q in range(4):
                        n, t = q // 2, q % 2
                        if q == 0:
                            pe.wait_ge(s_ya[l], i + 1)
                        if q == 2:
                            pe.wait_ge(s_yd[l], i + 1)
                        if q >= 2:
                            pe.wait_ge(s_add[l], i * 4 + (q - 1))
                        mm(PS[:, t], pickT[:, t], ye[:, 512 * n:512 * n + 512], start=True, stop=True).then_inc(s_sca[l], 1)

                pair(0, True)
                with pe.Fori(0, pe.snap(more * PAIRS + (PAIRS - 1))) as before_it:
                    pair(before_it + 1, False)

            pe.wait_ge(s_tab, 16 * 4)
            mm(PS[0:A_HEADS + B_HEADS, 4, 0:BW], xn[0:BUCKETS, 0, BW:BW + A_HEADS + B_HEADS], xn[0:BUCKETS, 0, 0:BW],
               start=True, stop=True).then_inc(s_vec, 1)
            for a in range(2):
                last = mm(PS[0:C_HEADS, 5, 0:BW], xn[:, 1, 2 * BW + a * C_HEADS:2 * BW + (a + 1) * C_HEADS],
                          xn[:, 1, a * BW:(a + 1) * BW], start=(a == 0), stop=(a == 1))
            last.then_inc(s_vec, 1)
            pe.wait_ge(s_kon, 16)
            pe.wait_ge(s_xn, 2)
            turn()
            turned()
            make_bias(0, A_HEADS + B_HEADS)
            for l in range(DEPTH):
                if l:
                    pe.wait_ge(s_xn, 4 * l + 2)
                    turn()
                    turned()
                else:
                    pe.wait_ge(s_bias[0], 1)
                project(l)
                if l == 0:
                    index_scores()
                attention(l)
                pe.wait_ge(s_y[l], 1)
                turn()
                turned()
                out_project(l)
                pe.wait_ge(s_xn, 4 * l + 4)
                turn()
                turned()
                route(l)
                if l == 0:
                    pe.wait_ge(s_go[0], 1)
                    make_bias(1, C_HEADS)
                    pe.wait_ge(s_bias[1], 1)
                pe.wait_ge(s_go[l], 1)
                experts(l)


_INS = ["x", "t5_bias", "ln_mix", "ln_ffn", "ln_final", "ab_w_in", "ab_w_out", "diff_lambda", "diff_subln", "c_w_in",
        "c_w_out", "c_rel_bias", "moe_w_rg", "moe_b_rg", "moe_w_re", "moe_b_re", "moe_w_gate", "moe_w_up", "moe_w_down"]


def shape_constants():
    import math

    consts = np.zeros((P, 4 * P + SEQ), np.float32)
    consts[:, 0:P] = np.eye(P)
    consts[:, P:2 * P] = np.eye(P)[::-1]
    consts[:, 2 * P:3 * P] = np.triu(np.ones((P, P)), 1)
    consts[:, 3 * P:4 * P] = 1
    consts[:, 4 * P:] = np.arange(SEQ)
    j = np.arange(BW)
    dist = np.minimum(j, BL - 1) - (SEQ - 1)
    half, exact, far = BUCKETS // 2, BUCKETS // 4, 1024
    n = np.abs(dist)
    nf = np.maximum(n, 1).astype(np.float32)
    large = exact + (np.log(nf / np.float32(exact)) / np.float32(math.log(far / exact)) * np.float32(half - exact)).astype(np.int32)
    bucket = np.where(dist > 0, half, 0) + np.where(n < exact, n, np.minimum(large, half - 1))
    hot_t5 = (np.arange(BUCKETS)[:, None] == bucket[None, :]).astype(np.float32)
    row = np.clip(-dist, -P, P) + P - 1
    hot_rel = (np.arange(2 * P)[:, None] == row[None, :]).astype(np.float32)
    return {"consts": consts, "hot_t5": hot_t5, "hot_rel": hot_rel}


def kernel(**inputs):
    import concourse.bacc as _bacc
    from concourse.bass_utils import run_bass_kernel_spmd as _run

    nc = _bacc.Bacc("TRN2", target_bir_lowering=False, num_devices=1)
    arrays, args = {}, []
    given = {n: inputs[n] for n in _INS} | shape_constants()
    for name, a in given.items():
        a = np.ascontiguousarray(a)
        arrays[f"in_{name}"] = a
        args.append(nc.dram_tensor(f"in_{name}", a.shape, mybir.dt.from_np(a.dtype), kind="ExternalInput").ap())
    args.append(nc.dram_tensor("out_0", (1, SEQ, D), FP32, kind="ExternalOutput").ap())
    build(nc, *args)
    r = _run(nc, [arrays], core_ids=[0])
    return r.results[0]["out_0"]
```

```python
from contextlib import ExitStack

import numpy as np
import concourse.bass as bass
from concourse import mybir

FP32 = mybir.dt.float32
INT32 = mybir.dt.int32
ALU = mybir.AluOpType
ACT = mybir.ActivationFunctionType
AX = mybir.AxisListType

P = 128
SEQ, D, DEPTH = 256, 1024, 2
NT = SEQ // P
NK = D // P
CHUNK = 64
EPS = 1e-6
A_HEADS, B_HEADS, C_HEADS, IDX_HEADS, HD = 4, 8, 16, 4, 64
A_V = 2 * HD
TOPK = SEQ // 4
SCALE = HD ** -0.5
BUCKETS = 32
NEG = -1e30
GONE = -3e38
LAM_INIT = 0.8 - 0.6 * 1.0
GROUPS, PER_GROUP, TOP_EXPERTS = 4, 8, 2
EXPERTS = GROUPS * PER_GROUP
F = D // 2
NF = F // P
ROUTES = GROUPS + EXPERTS

CW = 256
AB_IN = 2500
A_CHUNKS = -(-AB_IN // CW)
C_CHUNKS = 3 * D // CW
IN_CHUNKS = (A_CHUNKS, C_CHUNKS)
SLOT_W = NK * CW
OUT_CHUNKS = D * NK // SLOT_W
KPC = NK // OUT_CHUNKS

AT_ONCE = 2
SLOTS = P // AT_ONCE
PAIRS = EXPERTS // AT_ONCE
MAX_PASSES = SEQ // SLOTS
PEELED = 2
UP_CHUNKS = 4
KPU = NK // UP_CHUNKS
CHUNKS = 2 * UP_CHUNKS + NF

EXTRA = OUT_CHUNKS + 1 + C_HEADS * SEQ // SLOT_W + 1

BL = SEQ + P - 1
BW = BL + 1

PICKS = NT * AT_ONCE
UNITS = 16
ATT = 3
FLUSH = 4


def unit_of(layer, u):
    g, qt, j = u // 4, u // 2 % 2, u % 2
    kind = "c" if layer else ("b", "b", "a", "a")[g]
    return kind, 2 * (g if layer else g % 2) + j, qt, P * (qt + 1)


ORDER = ([8, 9, 6, 7, 0, 2, 4, 1, 3, 5], [0, 4, 8, 1, 5, 9, 2, 6, 10, 3, 7, 11])
BY_DVE = ([9, 1, 3], [4, 1, 9, 6, 3, 11])
STEP_AFTER = ([(0, 3), (2, 1), (2, 3), (4, 0), (4, 1), (4, 3), (1, 0), (1, 1), (1, 3), (3, 0), (3, 1), (3, 3),
               (5, 0), (5, 1), (5, 3)],
              [(1, 1), (1, 3), (5, 1), (5, 3), (2, 1), (2, 3), (6, 1), (6, 3), (3, 0), (3, 2), (7, 0), (7, 3),
               (11, 0), (11, 1), (11, 3)])
FLIP_AFTER = {(7, 1): [0], (7, 2): [1], (7, 3): [2], (0, 0): [3], (0, 1): [4], (0, 2): [5]}
SPREAD_AFTER = (6, 0)
INDEX_AFTER = {(6, 1): 0, (6, 2): 1, (6, 3): 2, (7, 0): 3}


def events(layer):
    out, step = [], 0
    for pos, c in enumerate(ORDER[layer]):
        for quarter in range(4):
            out.append(("tile", pos, quarter))
            if quarter == 3:
                out.append(("copy", pos, None))
            if layer == 0:
                out += [("flip", b, None) for b in FLIP_AFTER.get((c, quarter), [])]
                if (c, quarter) == SPREAD_AFTER:
                    out.append(("spread", None, None))
                if (c, quarter) in INDEX_AFTER:
                    out.append(("index", INDEX_AFTER[c, quarter], None))
            if (c, quarter) in STEP_AFTER[layer]:
                out.append(("step", step, None))
                step += 1
    return out + [("step", n, None) for n in range(step, UNITS + FLUSH)]


def output_due(n):
    return n >= FLUSH and (n - FLUSH) % 2 == 1


def by_dve(layer, pos):
    return ORDER[layer][pos] in BY_DVE[layer]


def copies(layer, pos):
    return sum(by_dve(layer, n) == by_dve(layer, pos) for n in range(pos + 1))


def build(nc, x, t5, ln_mix, ln_ffn, ln_final, ab_in, ab_out, lam, subln, c_in, c_out, rel,
          w_rg, b_rg, w_re, b_re, w_gate, w_up, w_down, consts, hot_t5, hot_rel, out):
    ctx = ExitStack()
    with ctx:
        def sb(name, shape, dt=FP32):
            return ctx.enter_context(nc.sbuf_tensor(name, shape, dt))

        def sem(name):
            return ctx.enter_context(nc.semaphore(name))

        def per_layer(name):
            return [sem(f"{name}{l}") for l in range(DEPTH)]

        ring = sb("ring", [P, CHUNKS, SLOT_W])
        wo = sb("wo", [P, OUT_CHUNKS, KPC, D])
        h = sb("h", [P, NT, D])
        xn = sb("xn", [P, NT, D])
        xT = sb("xT", [P, NK, SEQ])
        bias = sb("bias", [P, C_HEADS, SEQ])
        mix = sb("mix", [P, 6144])
        gain_att = sb("gain_att", [P, D + ATT * 2 * SEQ])
        kon = sb("kon", [P, 4 * P + SEQ])
        wr = sb("wr", [P, NK, ROUTES])
        br = sb("br", [P, DEPTH, ROUTES])
        drop0 = sb("drop0", [P, P])
        sm = sb("sm", [P, 128])
        more_passes = sb("more_passes", [1, 1], INT32)
        PS = ctx.enter_context(nc.psum_tensor("PS", [P, 8, 512], FP32))
        bounce = nc.dram_tensor("bounce", [DEPTH, C_HEADS, BW], FP32, kind="Internal")

        gain = gain_att[:, 0:D]
        att = gain_att[:, D:].rearrange("p (u a n) -> p u a n", u=ATT, a=2)
        ident = kon[:, 0:P]
        flip = kon[:, P:2 * P]
        before = kon[:, 2 * P:3 * P]
        ones = kon[:, 3 * P:4 * P]

        def at(base, *shape):
            n = int(np.prod(shape))
            ap = mix[:, base:base + n]
            if len(shape) == 2:
                ap = ap.rearrange("p (a b) -> p a b", b=shape[1])
            if len(shape) == 3:
                ap = ap.rearrange("p (a b c) -> p a b c", b=shape[1], c=shape[2])
            return ap

        qkA = at(0, 8, SEQ)
        vA = at(2048, NT, 512)
        qB = at(3072, 4, SEQ)
        kqi = at(4096, 4, SEQ)
        vB = at(5120, NT, HD)
        wI = at(5248, NT, IDX_HEADS)
        sublnb = at(5256, A_V)
        lamb = at(5384, 4, HD)
        qkC = at(0, 16, SEQ)
        vC = at(4096, NT, D)
        xg = at(0, NK, P)
        silu = at(1024, F)
        hid = at(1536, F)
        hidT = at(2048, NF, P)
        ye = at(2560, D)
        pick = at(3584, NT, AT_ONCE * SLOTS)
        pickw = at(3840, NT, AT_ONCE * SLOTS)
        pickT = at(4096, NT, P)
        rank = at(4352, NT, EXPERTS)
        comb = at(4416, NT, EXPERTS)
        chose = at(4480, NT, EXPERTS)
        lg = at(4544, NT, ROUTES)
        prod = at(4616, NT, EXPERTS)
        rsm = at(4680, 256)
        rd_g, re_g, rd_e, re_e = (rsm[:, o:o + NT * n].rearrange("p (t n) -> p t n", t=NT)
                                  for o, n in ((0, GROUPS), (8, GROUPS), (16, PER_GROUP), (32, PER_GROUP)))
        now, now_w, now_slots = at(4936, NT, AT_ONCE), at(4940, NT, AT_ONCE), at(4944, SLOTS)
        isc, cand, over, same = (bias[:, 12 + j] for j in range(4))
        sqa = bias[:, 12:16]
        drop = [drop0[:, :], over]
        pT = gain.rearrange("p (a n) -> p a n", a=2)
        raw = bias[:, :, :].rearrange("p a n -> p (a n)")
        hot5, tab5 = raw[0:BUCKETS, 0:BW], raw[0:BUCKETS, BW:BW + A_HEADS + B_HEADS]
        hotr = raw[:, 512:512 + 2 * BW].rearrange("p (a n) -> p a n", a=2)
        tabr = raw[:, 512 + 2 * BW:512 + 2 * BW + 2 * C_HEADS].rearrange("p (a n) -> p a n", a=2)
        rows_t5, rows_rel = (att[:, a].rearrange("p a n -> p (a n)")[0:n, 0:BW] for a, n in ((0, A_HEADS + B_HEADS), (1, C_HEADS)))
        ss = sm[:, 0:2]
        rstd = sm[:, 2:4]
        half = sm[:, 4:12]
        nmax = sm[:, 120:120 + 2 * ATT].rearrange("p (a b) -> p a b", b=2)
        den = sm[:, 16:48]
        rden = sm[:, 48:80]
        lsum = sm[:, 80:84]
        nlam = sm[:, 84:85]
        ssa = sm[:, 88:96]
        rsa = sm[:, 96:104]
        top8 = sm[:, 104:112]
        left = sm[:, 112:114]
        spare = sm[:, 114:116]
        gate_v = w_gate.rearrange("l e (p k) f -> l p e (k f)", k=NK)
        up_v = w_up.rearrange("l e (p k) f -> l p e (k f)", k=NK)
        down_v = w_down.rearrange("l e (p k) n -> l p e (k n)", k=NF)
        in_v = [ab_in[0].rearrange("(p k) n -> p k n", k=NK), c_in[0].rearrange("(p k) n -> p k n", k=NK)]
        out_v = [ab_out[0].rearrange("(p k) n -> p k n", k=NK), c_out[0].rearrange("(p k) n -> p k n", k=NK)]

        def early(l, i, c):
            return isinstance(i, int) and i == 1 and c < EXTRA

        def slot(l, i, c):
            if early(l, i, c):
                if c < OUT_CHUNKS:
                    return wo[:, c].rearrange("p k n -> p (k n)")
                if c == OUT_CHUNKS:
                    return xT[:, :, :].rearrange("p k n -> p (k n)")
                if c == EXTRA - 1:
                    return gain_att[:, 0:SLOT_W]
                return raw[:, (c - OUT_CHUNKS - 1) * SLOT_W:(c - OUT_CHUNKS) * SLOT_W]
            return ring[:, c, :]

        s_x, s_kon, s_half = [sem(f"x_in{t}") for t in range(NT)], sem("consts_in"), sem("half_set")
        s_tab, s_lamin = sem("tables_in"), sem("lambda_in")
        s_vec, s_vecsb, s_vecout, s_z = sem("bias_rows"), sem("bias_rows_sb"), sem("bias_rows_out"), per_layer("bias_raw_in")
        s_flip, s_ba = per_layer("flipped"), per_layer("bias_copied")
        s_gain, s_ss, s_ms, s_rs, s_xn = sem("gain_in"), sem("squares"), sem("mean_sq"), sem("rstd"), sem("normed")
        s_turn, s_td, s_ta = sem("turned"), sem("turned_dve"), sem("turned_act")
        s_in = [sem(f"w_in_{c}") for c in range(C_CHUNKS)]
        s_wo = per_layer("w_out_in")
        s_proj, s_pa, s_pd = per_layer("projected"), per_layer("proj_act"), per_layer("proj_dve")
        s_is, s_ir, s_drop = sem("index_scores"), sem("index_relu"), sem("selection")
        s_sc, s_sr, s_lo, s_ex, s_co = per_layer("scored"), per_layer("scores_read"), per_layer("logits"), per_layer("exped"), sem("combined")
        s_tp, s_pt, s_pv, s_out = per_layer("p_turned"), per_layer("pT_ready"), per_layer("pv_done"), per_layer("out_read")
        s_vb, s_spread, s_twice = sem("values_b_ready"), sem("spread"), sem("keys_twice")
        s_ssa, s_msa, s_rsa = sem("a_squares"), sem("a_mean_sq"), sem("a_rstd")
        s_lexp, s_lred = sem("lambda_exp"), sem("lambda_sums")
        s_sub, s_od = sem("sub_normed"), per_layer("out_projected")
        s_h = sem("residual")
        s_wr, s_br = per_layer("router_in"), sem("router_bias_in")
        s_lg, s_rd, s_re, s_ch, s_rk, s_go = (per_layer("route_logits"), per_layer("route_diff"), per_layer("route_exp"),
                                              per_layer("chosen"), per_layer("ranked"), per_layer("routed"))
        s_ci = [[sem(f"chunk_in{l}_{c}") for c in range(CHUNKS)] for l in range(DEPTH)]
        s_used = per_layer("chunks_used")
        s_now, s_pk, s_pw = per_layer("columns_copied"), per_layer("picked"), per_layer("pick_weighted")
        s_g, s_xg, s_pkt, s_pkT = per_layer("gathered"), per_layer("xg_ready"), per_layer("pick_turned"), per_layer("pickT_ready")
        s_si, s_hi = per_layer("silu_ready"), per_layer("hidden_ready")
        s_ht, s_hT = per_layer("hid_turned"), per_layer("hidT_ready")
        s_ya, s_yd = per_layer("ye_act"), per_layer("ye_dve")
        s_sca, s_add = per_layer("scattered"), per_layer("added")
        s_zero = sem("zeroed")
        s_dve, s_final = sem("dve_chain"), sem("final_out")

        def in_count(l, pos):
            return 16 * (1 + (l > 0) * ((pos < A_CHUNKS) + (pos < EXTRA)))

        block = ctx.enter_context(nc.Block())

        def proj_dst(l, c):
            if l == 0:
                return [qkA[:, 0:2], qkA[:, 2:4], qkA[:, 4:6], qkA[:, 6:8], vA[:, :, 0:CW], vA[:, :, CW:2 * CW],
                        qB[:, 0:2], qB[:, 2:4], kqi[:, 0:2], kqi[:, 2:4]][c]
            return qkC[:, 2 * c:2 * c + 2] if c < 8 else vC[:, :, (c - 8) * CW:(c - 7) * CW]

        @block.sync
        def _(sp):
            for t in range(NT):
                sp.dma_start(h[:, t, :], x[0, t * P:(t + 1) * P, :]).then_inc(s_x[t], 16)

            def w_in(l, pos):
                c = ORDER[l][pos]
                n = min(CW, in_v[l].shape[2] - c * CW)
                dst = ring[:, pos, :].rearrange("p (k n) -> p k n", n=CW)[:, :, 0:n]
                sp.dma_start(dst, in_v[l][:, :, c * CW:c * CW + n]).then_inc(s_in[pos], 16)

            def w_out(l):
                for c in range(OUT_CHUNKS):
                    sp.dma_start(wo[:, c], out_v[l][:, c * KPC:(c + 1) * KPC, :]).then_inc(s_wo[l], 16)

            def chunk(l, pair, c, dst, signal):
                if c < 2 * UP_CHUNKS:
                    src, j, w = (gate_v, c, KPU * F) if c < UP_CHUNKS else (up_v, c - UP_CHUNKS, KPU * F)
                else:
                    src, j, w = down_v, c - 2 * UP_CHUNKS, D
                sp.dma_start(dst.rearrange("p (e n) -> p e n", e=AT_ONCE),
                             src[l, :, bass.ds(pair * AT_ONCE, AT_ONCE), j * w:(j + 1) * w]).then_inc(signal, 16)

            for l in range(DEPTH):
                for c in range(IN_CHUNKS[l]):
                    if l == 0 and c == 2:
                        sp.wait_ge(s_tab, 16 * 4)
                    if l == 0 and c == 3:
                        sp.wait_ge(s_vecout, 32)
                    if l == 0 and c == 4:
                        sp.wait_ge(s_z[0], 16)
                    if l:
                        sp.wait_ge(s_used[0], CHUNKS * (trips - 1) + c + 1)
                    w_in(l, c)
                w_out(l)
                for c in range(CHUNKS):
                    if c < IN_CHUNKS[l]:
                        sp.wait_ge(s_proj[l], c + 1)
                    chunk(l, 0, c, slot(l, 0, c), s_ci[l][c])
                for c in range(CHUNKS):
                    if c == 0:
                        sp.wait_ge(s_od[l], 4)
                    if c == OUT_CHUNKS:
                        sp.wait_ge(s_lg[l], 2)
                    if c >= EXTRA:
                        sp.wait_ge(s_used[l], c + 1)
                    chunk(l, 1, c, slot(l, 1, c), s_in[c] if early(l, 1, c) else s_ci[l][c])
                sp.wait_ge(s_go[l], 1)
                trips = sp.snap(sp.value_load(more_passes[0:1, 0:1], min_val=0, max_val=MAX_PASSES - 1) * PAIRS + PAIRS)
                with sp.Fori(0, trips - PEELED) as i:
                    for c in range(CHUNKS):
                        sp.wait_ge(s_used[l], i * CHUNKS + (CHUNKS + c + 1))
                        chunk(l, (i + PEELED) % PAIRS, c, ring[:, c, :], s_ci[l][c])
            for t in range(NT):
                sp.wait_ge(s_xn, 2 * 4 + t + 1)
                sp.dma_start(out[0, t * P:(t + 1) * P, :], xn[:, t, :]).then_inc(s_final, 16)
            sp.wait_ge(s_final, 16 * NT)

        @block.gpsimd
        def _(pool):
            pool.memset(half, -0.5).then_inc(s_half, 1)
            pool.dma_start(hot5, hot_t5).then_inc(s_tab, 16)
            pool.dma_start(tab5, t5).then_inc(s_tab, 16)
            pool.dma_start(hotr, hot_rel.rearrange("(a p) n -> p a n", p=P)).then_inc(s_tab, 16)
            pool.dma_start(tabr, rel[0, 1:1 + 2 * P, :].rearrange("(a p) n -> p a n", p=P)).then_inc(s_tab, 16)
            def rstd_of(n, t):
                pool.wait_ge(s_ss, 2 * n + t + 1)
                pool.tensor_scalar(rstd[:, t:t + 1], ss[:, t:t + 1], 1.0 / D, EPS, ALU.mult, ALU.add).then_inc(s_ms, 1)
                pool.wait_ge(s_ms, 2 * n + t + 1)
                pool.tensor_tensor(rstd[:, t:t + 1], rstd[:, t:t + 1], half[:, 0:1], ALU.pow).then_inc(s_rs, 1)

            def carry_waits(site):
                pool.tensor_tensor(spare[:, site:site + 1], half[:, 0:1], half[:, 0:1], ALU.mult)

            pool.wait_ge(s_half, 1)
            for t in range(NT):
                rstd_of(0, t)
            pool.dma_start(lamb, lam[0:1].broadcast_to((P, 4, HD))).then_inc(s_lamin, 16)
            pool.dma_start(sublnb, subln[0:1].broadcast_to((P, A_V))).then_inc(s_lamin, 16)
            for l in range(DEPTH):
                pool.dma_start(br[:, l, 0:GROUPS], b_rg[l:l + 1].broadcast_to((P, GROUPS))).then_inc(s_br, 16)
                pool.dma_start(br[:, l, GROUPS:ROUTES], b_re[l:l + 1].broadcast_to((P, EXPERTS))).then_inc(s_br, 16)
            pool.wait_ge(s_vecsb, 2)
            pool.dma_start(bounce.ap()[0, 0:A_HEADS + B_HEADS], rows_t5).then_inc(s_vecout, 16)
            pool.dma_start(bounce.ap()[1], rows_rel).then_inc(s_vecout, 16)
            pool.wait_ge(s_vecout, 32)

            def raw_bias(l, heads):
                pool.dma_start(bias[:, 0:heads, :], bass.AP(bounce, l * C_HEADS * BW, [[1, P], [BW, heads], [1, SEQ]]))\
                    .then_inc(s_z[l], 16)

            raw_bias(0, A_HEADS + B_HEADS)
            for l in range(DEPTH):
                pool.dma_start(wr[:, :, 0:GROUPS], w_rg[l].rearrange("(p k) g -> p k g", k=NK)).then_inc(s_wr[l], 16)
                pool.dma_start(wr[:, :, GROUPS:ROUTES], w_re[l].rearrange("(p k) g -> p k g", k=NK)).then_inc(s_wr[l], 16)
                if l == 0:
                    for n in range(4):
                        cols = slice(2 * n, 2 * n + 2)
                        pool.wait_ge(s_ssa, 3 * n + 3)
                        pool.tensor_scalar(rsa[:, cols], ssa[:, cols], 1.0 / A_V, EPS, ALU.mult, ALU.add).then_inc(s_msa, 1)
                        pool.wait_ge(s_msa, n + 1)
                        pool.tensor_tensor(rsa[:, cols], rsa[:, cols], half[:, 0:2], ALU.pow).then_inc(s_rsa, 1)
                        pool.wait_ge(s_rsa, 2 * n + 1)
                        ya = xn[:, n % 2, CW * (n // 2):CW * (n // 2 + 1)].rearrange("p (a n) -> p a n", n=A_V)
                        pool.tensor_tensor(ya, ya, rsa[:, cols].unsqueeze(2).broadcast_to((P, 2, A_V)), ALU.mult).then_inc(s_rsa, 1)
                        pool.wait_ge(s_rsa, 2 * n + 2)
                        pool.tensor_tensor(ya, ya, sublnb.unsqueeze(1).broadcast_to((P, 2, A_V)), ALU.mult).then_inc(s_sub, 1)
                for t in range(NT):
                    rstd_of(2 * l + 1, t)

                def pick_rows(i):
                    experts = bass.ds(i % PAIRS * AT_ONCE, AT_ONCE)
                    pool.wait_ge(s_pw[l], i * PICKS)
                    pool.tensor_copy(now, rank[:, :, experts]).then_inc(s_now[l], 1)
                    pool.tensor_copy(now_w, comb[:, :, experts]).then_inc(s_now[l], 1)
                    pool.tensor_copy(now_slots, kon[:, bass.ds(i // PAIRS * SLOTS + 4 * P, SLOTS)]).then_inc(s_now[l], 1)
                    pool.wait_ge(s_now[l], i * 3)
                    pool.wait_ge(s_g[l], i * 2)
                    carry_waits(0)
                    for t in range(NT):
                        for e in range(AT_ONCE):
                            pool.tensor_scalar(pick[:, t, e * SLOTS:(e + 1) * SLOTS], now_slots, now[:, t, e:e + 1],
                                               None, ALU.is_equal).then_inc(s_pk[l], 1)
                    pool.wait_ge(s_pkt[l], i)
                    carry_waits(1)
                    for t in range(NT):
                        for e in range(AT_ONCE):
                            pool.tensor_scalar(pickw[:, t, e * SLOTS:(e + 1) * SLOTS], now_slots, now[:, t, e:e + 1],
                                               now_w[:, t, e:e + 1], ALU.is_equal, ALU.mult).then_inc(s_pw[l], 1)

                pool.wait_ge(s_pw[l], PICKS)
                pick_rows(1)
                if l == 0:
                    pool.wait_ge(s_used[0], CHUNKS + EXTRA - 1)
                    raw_bias(1, C_HEADS)
                pool.wait_ge(s_go[l], 1)
                more = pool.value_load(more_passes[0:1, 0:1], min_val=0, max_val=MAX_PASSES - 1)
                with pool.Fori(0, pool.snap(more * PAIRS + (PAIRS - PEELED))) as i:
                    pick_rows(i + PEELED)
                if l + 1 < DEPTH:
                    for t in range(NT):
                        rstd_of(2 * l + 2, t)
            for t in range(NT):
                rstd_of(2 * DEPTH, t)

        @block.scalar
        def _(act):
            gains = [ln_mix[0:1], ln_ffn[0:1], ln_mix[1:2], ln_ffn[1:2], ln_final.rearrange("(a d) -> a d", a=1)]

            def load_gain(n):
                if n:
                    act.wait_ge(s_xn, 2 * n)
                act.dma_start(gain, gains[n].broadcast_to((P, D))).then_inc(s_gain, 16)

            def squares(n, t, junk):
                act.activation(junk, h[:, t], ACT.Square, accum_out=ss[:, t:t + 1]).then_inc(s_ss, 1)

            def turn_copy(j, t):
                act.wait_ge(s_turn, 4 * j + 2 * t + 2)
                act.activation(xT[:, 4:8, t * P:(t + 1) * P], PS[:, 2 * t + 1].rearrange("p (k n) -> p k n", k=4), ACT.Copy)\
                    .then_inc(s_ta, 1)

            def bias_copy(l, b, bank):
                act.wait_ge(s_flip[l], b + 1)
                act.activation(bias[:, 2 * b:2 * b + 2, :], PS[:, bank].rearrange("p (a n) -> p a n", a=2), ACT.Copy)\
                    .then_inc(s_ba[l], 1)

            def exps(l, u):
                act.wait_ge(s_lo[l], u + 1)
                n = unit_of(l, u)[3]
                for j in range(2):
                    act.activation(att[:, u % ATT, j, 0:n], att[:, u % ATT, j, 0:n], ACT.Exp, bias=nmax[:, u % ATT, j:j + 1],
                                   accum_out=den[:, 2 * u + j:2 * u + j + 1]).then_inc(s_ex[l], 1)

            def probs_copy(l, u):
                kind, _, _, n = unit_of(l, u)
                w = n if kind == "a" else 2 * n
                act.wait_ge(s_tp[l], u + 1)
                if u >= 2:
                    act.wait_ge(s_pv[l], u - 1)
                act.activation(pT[:, u % 2, 0:w], PS[:, 2 + u % 2, 0:w], ACT.Copy).then_inc(s_pt[l], 1)

            def outputs_a(u):
                g, qt = u // 4, u // 2 % 2
                n = 2 * (g - 2) + qt
                act.wait_ge(s_pv[0], u + 1)
                for j in range(2):
                    act.activation(sqa[:, n, j * A_V:(j + 1) * A_V], PS[:, 4 + qt, j * A_V:(j + 1) * A_V], ACT.Square,
                                   accum_out=ssa[:, 2 * n + j:2 * n + j + 1]).then_inc(s_ssa, 1)
                act.activation(xn[:, qt, CW * (g - 2):CW * (g - 1)], PS[:, 4 + qt, 0:CW], ACT.Copy).then_inc(s_ssa, 1)

            def spread_copy():
                act.wait_ge(s_spread, 1)
                act.activation(vB, PS[:, 5, 0:NT * HD].rearrange("p (t n) -> p t n", t=NT), ACT.Copy).then_inc(s_vb, 1)
                act.activation(wI, PS[:, 5, NT * HD:NT * (HD + IDX_HEADS)].rearrange("p (t n) -> p t n", t=NT), ACT.Copy,
                               scale=(IDX_HEADS ** -0.5) * (HD ** -0.5)).then_inc(s_vb, 1)

            def index_relu(v):
                n = P * (v // 2 + 1)
                act.wait_ge(s_is, v + 1)
                if v == 0:
                    act.wait_ge(s_vecout, 32)
                if v >= 2:
                    act.wait_ge(s_drop, 2 * (v - 1))
                act.activation(att[:, v % 2, :, 0:n], PS[:, 0:2, 0:n], ACT.Relu).then_inc(s_ir, 1)

            def mixer(l):
                for what, n, _ in events(l):
                    if what == "copy" and not by_dve(l, n):
                        act.wait_ge(s_proj[l], n + 1)
                        act.activation(proj_dst(l, ORDER[l][n]), PS[:, 6 + n % 2].rearrange("p (a n) -> p a n", a=2), ACT.Copy)\
                            .then_inc(s_pa[l], 1)
                    elif what == "flip":
                        bias_copy(0, n, 2 + n % 2)
                    elif what == "spread":
                        spread_copy()
                    elif what == "index":
                        index_relu(n)
                    elif what == "step":
                        if n == 0:
                            act.wait_ge(s_xn, 4 * l + 2)
                        if 2 <= n <= UNITS + 1:
                            probs_copy(l, n - 2)
                        if n < UNITS:
                            exps(l, n)
                        if output_due(n) and unit_of(l, n - FLUSH)[0] == "a":
                            outputs_a(n - FLUSH)

            load_gain(0)
            act.dma_start(kon[:, :], consts).then_inc(s_kon, 16)
            for t in range(NT):
                act.wait_ge(s_x[t], 16)
                squares(0, t, xn[:, t])
            for t in range(NT):
                turn_copy(0, t)
            act.wait_ge(s_vec, 2)
            act.activation(rows_rel, PS[0:C_HEADS, 5, 0:BW], ACT.Copy).then_inc(s_vecsb, 1)
            act.wait_ge(s_lred, 2)
            act.activation(lsum[:, 2:4], lsum[:, 0:2], ACT.Exp).then_inc(s_lexp, 1)
            for l in range(DEPTH):
                if l:
                    for t in range(NT):
                        turn_copy(3 * l, t)
                mixer(l)
                act.wait_ge(s_pv[l], UNITS)
                load_gain(2 * l + 1)
                for t in range(NT):
                    turn_copy(3 * l + 1, t)
                for t in range(NT):
                    act.wait_ge(s_h, 4 * l + 2 * t + 2)
                    squares(2 * l + 1, t, mix[:, t * D:(t + 1) * D])
                    turn_copy(3 * l + 2, t)
                    for j, (a, b) in enumerate(((rd_g, re_g), (rd_e, re_e))):
                        act.wait_ge(s_rd[l], 2 * t + j + 1)
                        act.activation(b[:, t], a[:, t], ACT.Exp).then_inc(s_re[l], 1)

                def experts(i, first):
                    for b in range(2):
                        act.wait_ge(s_g[l], i * 2 + (b + 1))
                        if b == 0 and not first:
                            act.wait_ge(s_used[l], i * CHUNKS)
                        act.activation(xg[:, 4 * b:4 * b + 4, :], PS[:, b].rearrange("p (k n) -> p k n", k=4), ACT.Copy)\
                            .then_inc(s_xg[l], 1)
                    act.wait_ge(s_used[l], i * CHUNKS + UP_CHUNKS)
                    if not first:
                        act.wait_ge(s_hi[l], i)
                    act.activation(silu, PS[:, 2], ACT.Silu).then_inc(s_si[l], 1)
                    act.wait_ge(s_ht[l], i + 1)
                    act.activation(hidT, PS[:, 4].rearrange("p (k n) -> p k n", k=NF), ACT.Copy).then_inc(s_hT[l], 1)
                    act.wait_ge(s_used[l], i * CHUNKS + CHUNKS)
                    if not first:
                        act.wait_ge(s_sca[l], i * 4)
                    act.activation(ye[:, 0:512], PS[:, 6], ACT.Copy).then_inc(s_ya[l], 1)

                experts(0, True)
                experts(1, False)
                act.wait_ge(s_used[l], CHUNKS + EXTRA)
                load_gain(2 * l + 2)
                if l == 0:
                    for b in range(C_HEADS // 2):
                        bias_copy(1, b, b % 2)
                act.wait_ge(s_go[l], 1)
                more = act.value_load(more_passes[0:1, 0:1], min_val=0, max_val=MAX_PASSES - 1)
                trips = act.snap(more * PAIRS + PAIRS)
                with act.Fori(0, trips - PEELED) as i:
                    experts(i + PEELED, False)
                for t in range(NT):
                    act.wait_ge(s_add[l], trips * 4 - 2 * (NT - 1 - t))
                    squares(2 * l + 2, t, xn[:, t])

        @block.vector
        def _(dve):
            chain = [0]

            def link(ins):
                chain[0] += 1
                ins.then_inc(s_dve, 1)
                dve.wait_ge(s_dve, chain[0])

            def scaled(n, t):
                dve.wait_ge(s_rs, 2 * n + t + 1)
                dve.wait_ge(s_gain, 16 * (n + 1))
                dve.scalar_tensor_tensor(xn[:, t], h[:, t], rstd[:, t:t + 1], gain, ALU.mult, ALU.mult)\
                    .then_inc(s_xn, 1)

            def norm(n):
                for t in range(NT):
                    scaled(n, t)

            def turn_copy(j, t):
                dve.wait_ge(s_turn, 4 * j + 2 * t + 1)
                dve.tensor_copy(xT[:, 0:4, t * P:(t + 1) * P], PS[:, 2 * t].rearrange("p (k n) -> p k n", k=4)).then_inc(s_td, 1)

            def mask_bias(l, heads):
                dve.wait_ge(s_ba[l], heads // 2)
                link(dve.memset(bias[0:CHUNK, 0:heads, SEQ - CHUNK:SEQ], NEG))

            def first_of(k, scores, top, out_sel, w):
                link(dve.tensor_scalar(over[:, 0:w], scores, top, 0.0, ALU.is_gt, ALU.add, accum_out=left[:, 0:1]))
                link(dve.tensor_scalar(same[:, 0:w], scores, top, None, ALU.is_equal))
                link(dve.tensor_scalar(left[:, 1:2], left[:, 0:1], -1.0, float(k), ALU.mult, ALU.add))
                link(dve.tensor_tensor_scan(cand[:, 0:w], same[:, 0:w], same[:, 0:w], 0.0, ALU.add, ALU.max))
                link(dve.scalar_tensor_tensor(same[:, 0:w], cand[:, 0:w], left[:, 1:2], same[:, 0:w], ALU.is_le, ALU.mult))
                link(dve.tensor_tensor(out_sel, same[:, 0:w], over[:, 0:w], ALU.add))

            def select(qt):
                n = P * (qt + 1)
                if qt == 0:
                    dve.wait_ge(s_vb, 2)
                for v in range(2):
                    dve.wait_ge(s_ir, 2 * qt + v + 1)
                    for j in range(2):
                        hd = 2 * v + j
                        if hd == 0:
                            ins = dve.tensor_scalar(isc[:, 0:n], att[:, 0, 0, 0:n], wI[:, qt, 0:1], None, ALU.mult)
                        else:
                            ins = dve.scalar_tensor_tensor(isc[:, 0:n], att[:, v, j, 0:n], wI[:, qt, hd:hd + 1],
                                                           isc[:, 0:n], ALU.mult, ALU.add)
                        ins.then_inc(s_drop, 1)
                        dve.wait_ge(s_drop, 4 * qt + hd + 1)
                link(dve.memset(isc[0:CHUNK, n - CHUNK:n], NEG))
                link(dve.tensor_copy(cand[:, 0:n], isc[:, 0:n]))
                for r in range(TOPK // 8):
                    link(dve.max(top8, cand[:, 0:n]))
                    if r + 1 < TOPK // 8:
                        link(dve.match_replace(cand[:, 0:n], top8, cand[:, 0:n], GONE))
                first_of(TOPK, isc[:, 0:n], top8[:, 7:8], same[:, 0:n], n)
                link(dve.tensor_scalar(drop[qt][:, 0:n], same[:, 0:n], -1.0, -NEG, ALU.add, ALU.mult))

            def logits(l, u):
                kind, j, qt, n = unit_of(l, u)
                hd = {"a": j, "b": A_HEADS + 2 * j, "c": 2 * j}[kind]
                if kind == "a":
                    tile = bias[:, hd:hd + 1, SEQ - n:SEQ].broadcast_to((P, 2, n))
                else:
                    tile = bias[:, hd:hd + 2, SEQ - n:SEQ]
                dve.wait_ge(s_sc[l], u + 1)
                if u >= ATT:
                    dve.wait_ge(s_tp[l], u - ATT + 1)
                a = att[:, u % ATT, :, 0:n]
                dve.scalar_tensor_tensor(a, PS[:, 0:2, 0:n], SCALE, tile, ALU.mult, ALU.add).then_inc(s_sr[l], 1)
                dve.wait_ge(s_sr[l], u + 1)
                if kind == "b":
                    link(dve.tensor_tensor(a, a, drop[qt][:, 0:n].unsqueeze(1).broadcast_to((P, 2, n)), ALU.add))
                dve.tensor_reduce(nmax[:, u % ATT, :], a, AX.X, ALU.max, negate=True).then_inc(s_lo[l], 1)

            def combine(l, u):
                n = unit_of(l, u)[3]
                dve.wait_ge(s_ex[l], 2 * u + 2)
                link(dve.reciprocal(rden[:, 2 * u:2 * u + 2], den[:, 2 * u:2 * u + 2]))
                link(dve.tensor_scalar(att[:, u % ATT, 1, 0:n], att[:, u % ATT, 1, 0:n], rden[:, 2 * u + 1:2 * u + 2], nlam,
                                       ALU.mult, ALU.mult))
                dve.scalar_tensor_tensor(att[:, u % ATT, 0, 0:n], att[:, u % ATT, 0, 0:n], rden[:, 2 * u:2 * u + 1],
                                         att[:, u % ATT, 1, 0:n], ALU.mult, ALU.add).then_inc(s_co, 1)

            def outputs(l, u):
                kind, j, qt, _ = unit_of(l, u)
                g = u // 4
                dve.wait_ge(s_pv[l], u + 1)
                src = PS[:, 4 + qt, 0:CW]
                heads = slice(8 * g + 4 * qt, 8 * g + 4 * qt + 4)
                dve.wait_ge(s_ex[l], 2 * u + 2)
                link(dve.reciprocal(rden[:, heads], den[:, heads]))
                col = (D // 2 if kind == "b" else 0) + CW * g
                dve.tensor_tensor(xn[:, qt, col:col + CW].rearrange("p (a n) -> p a n", n=HD),
                                  src.rearrange("p (a n) -> p a n", n=HD),
                                  rden[:, heads].unsqueeze(2).broadcast_to((P, 4, HD)), ALU.mult).then_inc(s_out[l], 1)

            def mixer(l):
                for what, n, _ in events(l):
                    if what == "copy" and by_dve(l, n):
                        dve.wait_ge(s_proj[l], n + 1)
                        src = PS[:, 6 + n % 2].rearrange("p (a n) -> p a n", a=2)
                        if (l, ORDER[l][n]) == (0, A_CHUNKS - 1):
                            m = AB_IN % P
                            dve.tensor_copy(kqi[:, 2], src[:, 0])
                            dve.tensor_copy(kqi[0:m, 3], src[0:m, 1]).then_inc(s_pd[l], 1)
                        else:
                            dve.tensor_copy(proj_dst(l, ORDER[l][n]), src).then_inc(s_pd[l], 1)
                    elif what == "spread":
                        dve.wait_ge(s_spread, 2)
                        dve.tensor_copy(kqi[HD:P, 0:4:3], PS[HD:P, 4].rearrange("p (a n) -> p a n", a=2)).then_inc(s_twice, 1)
                    elif what == "index" and n % 2 == 1:
                        select(n // 2)
                    elif what == "step":
                        if l == 0 and n == 0:
                            mask_bias(0, A_HEADS + B_HEADS)
                        if n < UNITS:
                            logits(l, n)
                        if 1 <= n <= UNITS and unit_of(l, n - 1)[0] == "a":
                            combine(l, n - 1)
                        if output_due(n) and unit_of(l, n - FLUSH)[0] != "a":
                            outputs(l, n - FLUSH)

            def residual(l, q):
                t, n = q // 2, q % 2
                dve.wait_ge(s_od[l], q + 1)
                dve.tensor_tensor(h[:, t, 512 * n:512 * n + 512], PS[:, 4 + q], h[:, t, 512 * n:512 * n + 512], ALU.add)\
                    .then_inc(s_h, 1)

            def gained(l, t):
                dve.wait_ge(s_h, 4 * l + 2 * t + 2)
                dve.wait_ge(s_gain, 16 * (2 * l + 2))
                dve.tensor_tensor(xn[:, t], h[:, t], gain, ALU.mult).then_inc(s_xn, 1)

            def rescaled(l, t):
                dve.wait_ge(s_turn, 4 * (3 * l + 2) + 2 * t + 2)
                dve.wait_ge(s_rs, 2 * (2 * l + 1) + t + 1)
                dve.tensor_scalar(xn[:, t], xn[:, t], rstd[:, t:t + 1], None, ALU.mult)

            rsm_view = lambda o, n: rsm[:, o:o + NT * n].rearrange("p (t n) -> p t n", n=n)
            group, upg = rsm_view(48, GROUPS), rsm_view(56, GROUPS)
            es, sel, t8 = rsm_view(64, PER_GROUP), rsm_view(80, PER_GROUP), rsm_view(96, 8)
            mor, sam, upe = rsm_view(112, PER_GROUP), rsm_view(128, PER_GROUP), rsm_view(144, PER_GROUP)
            gm, gs, em, es1, cnt, fac = (rsm[:, 160 + 2 * j:162 + 2 * j] for j in range(6))
            mxc, stp = rsm[:, 180:181], rsm[:, 184:188]

            def route(l, t):
                def col(a):
                    return a[:, t:t + 1]

                def ge(a):
                    return a.rearrange("p (g e) -> p g e", g=GROUPS)

                dve.wait_ge(s_lg[l], t + 1)
                if t == 0:
                    dve.wait_ge(s_br, 16 * 4)
                link(dve.scalar_tensor_tensor(lg[:, t], PS[:, 4 + t, 0:ROUTES], rstd[:, t:t + 1], br[:, l], ALU.mult, ALU.add))
                link(dve.tensor_reduce(col(gm), lg[:, t, 0:GROUPS], AX.X, ALU.max))
                dve.tensor_scalar(rd_g[:, t], lg[:, t, 0:GROUPS], col(gm), None, ALU.subtract).then_inc(s_rd[l], 1)
                link(dve.tensor_scalar(group[:, t], lg[:, t, 0:GROUPS], col(gm), None, ALU.is_equal))
                link(dve.tensor_tensor_scan(upg[:, t], group[:, t], group[:, t], 0.0, ALU.add, ALU.max))
                link(dve.scalar_tensor_tensor(group[:, t], upg[:, t], 1.0, group[:, t], ALU.is_le, ALU.mult))
                g4 = group[:, t].unsqueeze(2).broadcast_to((P, GROUPS, PER_GROUP))
                link(dve.tensor_tensor(ge(prod[:, t]), ge(lg[:, t, GROUPS:ROUTES]), g4, ALU.mult))
                link(dve.tensor_reduce(es[:, t], prod[:, t].rearrange("p (g e) -> p e g", g=GROUPS), AX.X, ALU.add))
                link(dve.tensor_reduce(col(em), es[:, t], AX.X, ALU.max))
                dve.tensor_scalar(rd_e[:, t], es[:, t], col(em), None, ALU.subtract).then_inc(s_rd[l], 1)
                dve.wait_ge(s_re[l], 2 * t + 1)
                link(dve.tensor_reduce(col(gs), re_g[:, t], AX.X, ALU.add))
                ee = re_e[:, t]
                dve.wait_ge(s_re[l], 2 * t + 2)
                link(dve.max(t8[:, t], ee))
                dve.tensor_scalar(sam[:, t], ee, t8[:, t, 1:2], None, ALU.is_equal)
                link(dve.tensor_scalar(mor[:, t], ee, t8[:, t, 1:2], 0.0, ALU.is_gt, ALU.add, accum_out=col(cnt)))
                link(dve.tensor_tensor_scan(upe[:, t], sam[:, t], sam[:, t], 0.0, ALU.add, ALU.max))
                link(dve.tensor_scalar(upe[:, t], upe[:, t], col(cnt), float(TOP_EXPERTS), ALU.add, ALU.is_le))
                link(dve.tensor_tensor(sam[:, t], upe[:, t], sam[:, t], ALU.mult))
                link(dve.tensor_tensor(sel[:, t], sam[:, t], mor[:, t], ALU.add))
                dve.tensor_tensor(ge(chose[:, t]), g4, sel[:, t].unsqueeze(1).broadcast_to((P, GROUPS, PER_GROUP)),
                                  ALU.mult).then_inc(s_ch[l], 1)
                link(dve.tensor_tensor(ee, ee, sel[:, t], ALU.mult))
                link(dve.tensor_reduce(col(es1), ee, AX.X, ALU.add))
                link(dve.tensor_tensor(col(fac), col(es1), col(gs), ALU.mult))
                link(dve.reciprocal(col(fac), col(fac)))
                link(dve.tensor_scalar(ee, ee, col(fac), None, ALU.mult))
                link(dve.tensor_tensor(ge(comb[:, t]), g4, ee.unsqueeze(1).broadcast_to((P, GROUPS, PER_GROUP)), ALU.mult))

            def ranks(l):
                dve.wait_ge(s_ch[l], 2)
                dve.wait_ge(s_rk[l], 1)
                link(dve.scalar_tensor_tensor(rank, PS[:, 6, 0:NT * EXPERTS].rearrange("p (t n) -> p t n", t=NT), 1.0, chose,
                                              ALU.add, ALU.mult))
                link(dve.tensor_scalar(rank, rank, -1.0, None, ALU.add))
                shape = (P, AT_ONCE, SLOTS)
                split = lambda a: a.rearrange("p (e s) -> p e s", e=AT_ONCE)
                for t in range(NT):
                    dve.tensor_tensor(split(pick[:, t]), kon[:, 4 * P:4 * P + SLOTS].unsqueeze(1).broadcast_to(shape),
                                      rank[:, t, 0:AT_ONCE].unsqueeze(2).broadcast_to(shape), ALU.is_equal)\
                        .then_inc(s_pk[l], PICKS // NT)
                dve.wait_ge(s_pk[l], PICKS)
                for t in range(NT):
                    dve.tensor_tensor(split(pickw[:, t]), split(pick[:, t]),
                                      comb[:, t, 0:AT_ONCE].unsqueeze(2).broadcast_to(shape), ALU.mult)\
                        .then_inc(s_pw[l], PICKS // NT)
                link(dve.tensor_reduce(mxc, PS[:, 6, NT * EXPERTS:(NT + 1) * EXPERTS], AX.X, ALU.max))
                for j in range(1, MAX_PASSES):
                    link(dve.tensor_scalar(stp[:, j:j + 1], mxc, float(SLOTS * j), None, ALU.is_gt))
                link(dve.tensor_reduce(stp[:, 0:1], stp[:, 1:MAX_PASSES], AX.X, ALU.add))
                dve.tensor_copy(more_passes[:, :], stp[0:1, 0:1]).then_inc(s_go[l], 1)

            norm(0)
            for t in range(NT):
                turn_copy(0, t)
            dve.wait_ge(s_vec, 1)
            dve.tensor_copy(rows_t5, PS[0:A_HEADS + B_HEADS, 4, 0:BW]).then_inc(s_vecsb, 1)
            dve.wait_ge(s_lamin, 32)
            for j in range(2):
                link(dve.tensor_tensor(lamb[:, 2 * j], lamb[:, 2 * j], lamb[:, 2 * j + 1], ALU.mult))
                dve.tensor_reduce(lsum[:, j:j + 1], lamb[:, 2 * j], AX.X, ALU.add).then_inc(s_lred, 1)
            dve.wait_ge(s_lexp, 1)
            link(dve.tensor_tensor(nlam, lsum[:, 3:4], lsum[:, 2:3], ALU.subtract))
            link(dve.tensor_scalar(nlam, nlam, -LAM_INIT, None, ALU.add))
            link(dve.tensor_scalar(sublnb, sublnb, 1.0 - LAM_INIT, None, ALU.mult))
            for l in range(DEPTH):
                if l:
                    norm(2 * l)
                    for t in range(NT):
                        turn_copy(3 * l, t)
                mixer(l)
                turn_copy(3 * l + 1, 0)
                turn_copy(3 * l + 1, 1)
                residual(l, 0)
                residual(l, 1)
                gained(l, 0)
                residual(l, 2)
                turn_copy(3 * l + 2, 0)
                rescaled(l, 0)
                route(l, 0)
                residual(l, 3)
                gained(l, 1)
                turn_copy(3 * l + 2, 1)
                rescaled(l, 1)
                route(l, 1)
                ranks(l)

                def experts(i, first):
                    dve.wait_ge(s_pkt[l], i + 1)
                    if not first:
                        dve.wait_ge(s_sca[l], i * 4)
                    dve.tensor_copy(pickT, PS[:, 5, 0:NT * P].rearrange("p (t n) -> p t n", t=NT)).then_inc(s_pkT[l], 1)
                    dve.wait_ge(s_used[l], i * CHUNKS + 2 * UP_CHUNKS)
                    dve.wait_ge(s_si[l], i + 1)
                    if not first:
                        dve.wait_ge(s_ht[l], i)
                    dve.tensor_tensor(hid, PS[:, 3], silu, ALU.mult).then_inc(s_hi[l], 1)
                    dve.wait_ge(s_used[l], i * CHUNKS + CHUNKS)
                    if not first:
                        dve.wait_ge(s_sca[l], i * 4)
                    dve.tensor_copy(ye[:, 512:1024], PS[:, 7]).then_inc(s_yd[l], 1)
                    if not first:
                        dve.wait_ge(s_add[l], i * 4)
                    for q in range(4):
                        t, n = q // 2, q % 2
                        dve.wait_ge(s_sca[l], i * 4 + (q + 1))
                        dve.tensor_tensor(h[:, t, 512 * n:512 * n + 512], PS[:, n], h[:, t, 512 * n:512 * n + 512],
                                          ALU.add).then_inc(s_add[l], 1)

                experts(0, True)
                experts(1, False)
                if l == 0:
                    mask_bias(1, C_HEADS)
                dve.wait_ge(s_go[l], 1)
                more = dve.value_load(more_passes[0:1, 0:1], min_val=0, max_val=MAX_PASSES - 1)
                trips = dve.snap(more * PAIRS + PAIRS)
                with dve.Fori(0, trips - PEELED) as i:
                    experts(i + PEELED, False)
                dve.wait_ge(s_add[l], trips * 4)
            norm(2 * DEPTH)

        @block.tensor
        def _(pe):
            mm = nc.tensor.matmul
            turns = [0]

            def turn(t):
                for b in range(2):
                    for kk in range(4):
                        last = nc.tensor.transpose(PS[:, 2 * t + b, kk * P:(kk + 1) * P], xn[:, t, 4 * b + kk:D:NK], ident)
                    last.then_inc(s_turn, 1)
                turns[0] += 1

            def turned():
                pe.wait_ge(s_td, turns[0])
                pe.wait_ge(s_ta, turns[0])

            def turn_bias(l, b, bank):
                mm(PS[:, bank], flip, bias[:, 2 * b:2 * b + 2, :], start=True, stop=True).then_inc(s_flip[l], 1)

            def copied(l, c):
                pos = ORDER[l].index(c)
                pe.wait_ge((s_pd if by_dve(l, pos) else s_pa)[l], copies(l, pos))

            def project_tile(l, pos, quarter):
                half, ks = quarter // 2, range(quarter % 2 * NK // 2, (quarter % 2 + 1) * NK // 2)
                c = ORDER[l][pos]
                w = ring[:, pos, :].rearrange("p (k n) -> p k n", n=CW)
                bank = PS[:, 6 + pos % 2]
                if quarter == 0:
                    pe.wait_ge(s_in[pos], in_count(l, pos))
                    if pos >= 2:
                        copied(l, ORDER[l][pos - 2])
                if c not in (4, 5) if l == 0 else c < 8:
                    m = min(P, in_v[l].shape[2] - c * CW - half * P)
                    for k in ks:
                        last = mm(bank[0:m, half * SEQ:(half + 1) * SEQ], w[:, k, half * P:half * P + m], xT[:, k, :],
                                  start=(k == 0), stop=(k == NK - 1))
                else:
                    for k in ks:
                        last = mm(bank[:, half * CW:(half + 1) * CW], xT[:, k, half * P:half * P + P], w[:, k, :],
                                  start=(k == 0), stop=(k == NK - 1))
                if quarter == 3:
                    last.then_inc(s_proj[l], 1)

            def pair_scores(q, kt, qt, n, signal):
                for j in range(2):
                    last = mm(PS[:, j, 0:n], q[HD * j:HD * j + HD, qt * P:(qt + 1) * P],
                              kt[HD * j:HD * j + HD, 0:n], start=True, stop=True)
                last.then_inc(signal, 1)

            def spread():
                copied(0, 8)
                copied(0, 9)
                for t in range(NT):
                    for n, o, src in ((HD, t * HD, kqi[HD:P, 0]), (IDX_HEADS, NT * HD + t * IDX_HEADS, kqi[HD:HD + IDX_HEADS, 3])):
                        last = nc.tensor.transpose(PS[:, 5, o:o + n], src[:, t * P:(t + 1) * P], ident[HD:HD + n, HD:HD + n])
                last.then_inc(s_spread, 1)
                for j in range(2):
                    last = mm(PS[HD:P, 4, j * SEQ:(j + 1) * SEQ], ident[0:HD, 0:HD], kqi[0:HD, 3 * j], start=True, stop=True)
                last.then_inc(s_spread, 1)

            def index_scores(v):
                if v:
                    pe.wait_ge(s_ir, v)
                else:
                    pe.wait_ge(s_twice, 1)
                pair_scores(kqi[:, 1 + v % 2], kqi[:, 3], v // 2, P * (v // 2 + 1), s_is)

            def scores(l, u):
                kind, j, qt, n = unit_of(l, u)
                if u == 0 and l == 0:
                    pe.wait_ge(s_ir, 4)
                if u:
                    pe.wait_ge(s_sr[l], u)
                if kind == "a":
                    copied(0, j // 2)
                    copied(0, 2 + j // 2)
                    q, kt = qkA[:, j], qkA[:, 4 + j]
                elif kind == "b":
                    copied(0, 6 + j // 2)
                    q, kt = qB[:, j], kqi[:, 0]
                else:
                    copied(1, j // 2)
                    copied(1, 4 + j // 2)
                    q, kt = qkC[:, j], qkC[:, 8 + j]
                pair_scores(q, kt, qt, n, s_sc[l])

            def turn_probs(l, u):
                kind, _, qt, n = unit_of(l, u)
                if kind == "a":
                    pe.wait_ge(s_co, u - 8 + 1)
                else:
                    pe.wait_ge(s_ex[l], 2 * u + 2)
                if u >= 2:
                    pe.wait_ge(s_pt[l], u - 1)
                for j in range(1 if kind == "a" else 2):
                    for kt in range(n // P):
                        o = (j * (n // P) + kt) * P
                        last = nc.tensor.transpose(PS[:, 2 + u % 2, o:o + P], att[:, u % ATT, j, kt * P:(kt + 1) * P], ident)
                last.then_inc(s_tp[l], 1)

            def values(l, u):
                kind, i, qt, n = unit_of(l, u)
                g = u // 4
                pe.wait_ge(s_pt[l], u + 1)
                if u % 2 == 0 and g:
                    if l == 0 and g == 3:
                        pe.wait_ge(s_ssa, 3 * (qt + 1))
                    else:
                        pe.wait_ge(s_out[l], 2 * (g - 1) + qt + 1)
                if kind == "a":
                    copied(0, 4 + i // 2)
                elif kind == "b":
                    pe.wait_ge(s_vb, 2)
                else:
                    copied(1, 8 + i // 2)
                for j in range(1 if kind == "a" else 2):
                    for kt in range(n // P):
                        o = (j * (n // P) + kt) * P
                        col = i % 2 * A_V if kind == "a" else (i % 2 * 2 + j) * HD
                        if kind == "a":
                            dst, v = PS[:, 4 + qt, col:col + A_V], vA[:, kt, i * A_V:(i + 1) * A_V]
                        else:
                            hd = 2 * i + j
                            dst, v = PS[:, 4 + qt, col:col + HD], (vB[:, kt] if kind == "b" else vC[:, kt, hd * HD:(hd + 1) * HD])
                        last = mm(dst, pT[:, u % 2, o:o + P], v, start=(kt == 0), stop=(kt == n // P - 1))
                last.then_inc(s_pv[l], 1)

            def mixer(l):
                for what, n, quarter in events(l):
                    if what == "tile":
                        project_tile(l, n, quarter)
                    elif what == "flip":
                        if n == 0:
                            pe.wait_ge(s_z[0], 16)
                        if n >= 2:
                            pe.wait_ge(s_ba[0], n - 1)
                        turn_bias(0, n, 2 + n % 2)
                    elif what == "index":
                        index_scores(n)
                    elif what == "spread":
                        spread()
                    elif what == "step":
                        if n == 0 and l == 0:
                            pe.wait_ge(s_ba[0], (A_HEADS + B_HEADS) // 2)
                        if n < UNITS:
                            scores(l, n)
                        if 2 <= n <= UNITS + 1:
                            turn_probs(l, n - 2)
                        if 3 <= n <= UNITS + 2:
                            values(l, n - 3)

            def out_project(l, q):
                t, n = q // 2, q % 2
                if q == 0:
                    pe.wait_ge(s_wo[l], 16 * OUT_CHUNKS)
                for k in range(NK):
                    last = mm(PS[:, 4 + q], xT[:, k, t * P:(t + 1) * P], wo[:, k // KPC, k % KPC, 512 * n:512 * n + 512],
                              start=(k == 0), stop=(k == NK - 1))
                last.then_inc(s_od[l], 1)

            def route(l, t):
                if t == 0:
                    pe.wait_ge(s_wr[l], 32)
                for k in range(NK):
                    last = mm(PS[:, 4 + t, 0:ROUTES], xT[:, k, t * P:(t + 1) * P], wr[:, k, :], start=(k == 0), stop=(k == NK - 1))
                last.then_inc(s_lg[l], 1)

            def ranks(l):
                pe.wait_ge(s_ch[l], 1)
                mm(PS[:, 6, 0:EXPERTS], before, chose[:, 0], start=True, stop=True)
                pe.wait_ge(s_ch[l], 2)
                mm(PS[:, 6, EXPERTS:2 * EXPERTS], ones, chose[:, 0], start=True, stop=False)
                mm(PS[:, 6, EXPERTS:2 * EXPERTS], before, chose[:, 1], start=False, stop=True)
                mm(PS[:, 6, 2 * EXPERTS:3 * EXPERTS], ones, chose[:, 0], start=True, stop=False)
                mm(PS[:, 6, 2 * EXPERTS:3 * EXPERTS], ones, chose[:, 1], start=False, stop=True).then_inc(s_rk[l], 1)

            def experts(l):
                def chunk_there(i, c):
                    if early(l, i, c):
                        pe.wait_ge(s_in[c], in_count(l, c) + 16)
                    elif isinstance(i, int):
                        pe.wait_ge(s_ci[l][c], i * 16 + 16)
                    else:
                        pe.wait_ge(s_ci[l][c], i * 16 + (0 if c < EXTRA else 16))

                def pair(i, first):
                    pe.wait_ge(s_pk[l], i * PICKS + PICKS)
                    if not first:
                        pe.wait_ge(s_add[l], i * 4)
                    for b in range(2):
                        for kk in range(4):
                            for t in range(NT):
                                last = mm(PS[:, b, kk * P:(kk + 1) * P], xn[:, t, 4 * b + kk:D:NK], pick[:, t],
                                          start=(t == 0), stop=(t == NT - 1))
                        last.then_inc(s_g[l], 1)
                    pe.wait_ge(s_pw[l], i * PICKS + PICKS)
                    if not first:
                        pe.wait_ge(s_pkT[l], i)
                    for t in range(NT):
                        last = nc.tensor.transpose(PS[:, 5, t * P:(t + 1) * P], pickw[:, t], ident)
                    last.then_inc(s_pkt[l], 1)
                    for part, bank in ((0, 2), (1, 3)):
                        if not first:
                            pe.wait_ge((s_si, s_hi)[part][l], i)
                        for c in range(UP_CHUNKS):
                            ch = part * UP_CHUNKS + c
                            chunk_there(i, ch)
                            if part == 0 and c % 2 == 0:
                                pe.wait_ge(s_xg[l], i * 2 + (c // 2 + 1))
                            w = slot(l, i, ch).rearrange("p (e k n) -> p e k n", e=AT_ONCE, k=KPU)
                            for kk in range(KPU):
                                k = c * KPU + kk
                                for e in range(AT_ONCE):
                                    last = mm(PS[e * SLOTS:(e + 1) * SLOTS, bank, :], xg[:, k, e * SLOTS:(e + 1) * SLOTS],
                                              w[:, e, kk, :], start=(k == 0), stop=(k == NK - 1))
                            last.then_inc(s_used[l], 1)
                    pe.wait_ge(s_hi[l], i + 1)
                    if not first:
                        pe.wait_ge(s_hT[l], i)
                    for k in range(NF):
                        last = nc.tensor.transpose(PS[:, 4, k * P:(k + 1) * P], hid[:, k:F:NF], ident)
                    last.then_inc(s_ht[l], 1)
                    pe.wait_ge(s_hT[l], i + 1)
                    if not first:
                        pe.wait_ge(s_ya[l], i)
                        pe.wait_ge(s_yd[l], i)
                    for k in range(NF):
                        ch = 2 * UP_CHUNKS + k
                        chunk_there(i, ch)
                        w = slot(l, i, ch).rearrange("p (e n) -> p e n", e=AT_ONCE)
                        for n in range(2):
                            for e in range(AT_ONCE):
                                last = mm(PS[e * SLOTS:(e + 1) * SLOTS, 6 + n, :], hidT[:, k, e * SLOTS:(e + 1) * SLOTS],
                                          w[:, e, 512 * n:512 * n + 512], start=(k == 0), stop=(k == NF - 1))
                        last.then_inc(s_used[l], 1)
                    pe.wait_ge(s_pkT[l], i + 1)
                    for q in range(4):
                        t, n = q // 2, q % 2
                        if q == 0:
                            pe.wait_ge(s_ya[l], i + 1)
                        if q == 1:
                            pe.wait_ge(s_yd[l], i + 1)
                        if q >= 2:
                            pe.wait_ge(s_add[l], i * 4 + (q - 1))
                        mm(PS[:, n], pickT[:, t], ye[:, 512 * n:512 * n + 512], start=True, stop=True).then_inc(s_sca[l], 1)

                pair(0, True)
                pair(1, False)
                if l == 0:
                    pe.wait_ge(s_z[1], 16)
                    pe.wait_ge(s_add[0], 8)
                    for b in range(C_HEADS // 2):
                        if b >= 2:
                            pe.wait_ge(s_ba[1], b - 1)
                        turn_bias(1, b, b % 2)
                    pe.wait_ge(s_ba[1], C_HEADS // 2)
                pe.wait_ge(s_go[l], 1)
                more = pe.value_load(more_passes[0:1, 0:1], min_val=0, max_val=MAX_PASSES - 1)
                with pe.Fori(0, pe.snap(more * PAIRS + (PAIRS - PEELED))) as i:
                    pair(i + PEELED, False)

            pe.wait_ge(s_kon, 16)
            for l in range(DEPTH):
                for t in range(NT):
                    pe.wait_ge(s_xn, 4 * l + t + 1)
                    turn(t)
                turned()
                if l == 0:
                    pe.wait_ge(s_tab, 16 * 4)
                    mm(PS[0:A_HEADS + B_HEADS, 4, 0:BW], tab5, hot5, start=True, stop=True).then_inc(s_vec, 1)
                    for a in range(2):
                        last = mm(PS[0:C_HEADS, 5, 0:BW], tabr[:, a], hotr[:, a], start=(a == 0), stop=(a == 1))
                    last.then_inc(s_vec, 1)
                    pe.wait_ge(s_vecsb, 2)
                mixer(l)
                pe.wait_ge(s_out[l], 7 if l else 3)
                if l == 0:
                    pe.wait_ge(s_sub, 3)
                turn(0)
                turned()
                out_project(l, 0)
                pe.wait_ge(s_out[l], 8 if l else 4)
                if l == 0:
                    pe.wait_ge(s_sub, 4)
                turn(1)
                out_project(l, 1)
                turned()
                out_project(l, 2)
                pe.wait_ge(s_xn, 4 * l + 3)
                turn(0)
                turned()
                route(l, 0)
                out_project(l, 3)
                pe.wait_ge(s_xn, 4 * l + 4)
                turn(1)
                turned()
                route(l, 1)
                ranks(l)
                experts(l)


_INS = ["x", "t5_bias", "ln_mix", "ln_ffn", "ln_final", "ab_w_in", "ab_w_out", "diff_lambda", "diff_subln", "c_w_in",
        "c_w_out", "c_rel_bias", "moe_w_rg", "moe_b_rg", "moe_w_re", "moe_b_re", "moe_w_gate", "moe_w_up", "moe_w_down"]


def shape_constants():
    import math

    consts = np.zeros((P, 4 * P + SEQ), np.float32)
    consts[:, 0:P] = np.eye(P)
    consts[:, P:2 * P] = np.eye(P)[::-1]
    consts[:, 2 * P:3 * P] = np.triu(np.ones((P, P)), 1)
    consts[:, 3 * P:4 * P] = 1
    consts[:, 4 * P:] = np.arange(SEQ)
    j = np.arange(BW)
    dist = np.minimum(j, BL - 1) - (SEQ - 1)
    half, exact, far = BUCKETS // 2, BUCKETS // 4, 1024
    n = np.abs(dist)
    nf = np.maximum(n, 1).astype(np.float32)
    large = exact + (np.log(nf / np.float32(exact)) / np.float32(math.log(far / exact)) * np.float32(half - exact)).astype(np.int32)
    bucket = np.where(dist > 0, half, 0) + np.where(n < exact, n, np.minimum(large, half - 1))
    hot_t5 = (np.arange(BUCKETS)[:, None] == bucket[None, :]).astype(np.float32)
    row = np.clip(-dist, -P, P) + P - 1
    hot_rel = (np.arange(2 * P)[:, None] == row[None, :]).astype(np.float32)
    return {"consts": consts, "hot_t5": hot_t5, "hot_rel": hot_rel}


def kernel(**inputs):
    import concourse.bacc as _bacc
    from concourse.bass_utils import run_bass_kernel_spmd as _run

    nc = _bacc.Bacc("TRN2", target_bir_lowering=False, num_devices=1)
    arrays, args = {}, []
    given = {n: inputs[n] for n in _INS} | shape_constants()
    for name, a in given.items():
        a = np.ascontiguousarray(a)
        arrays[f"in_{name}"] = a
        args.append(nc.dram_tensor(f"in_{name}", a.shape, mybir.dt.from_np(a.dtype), kind="ExternalInput").ap())
    args.append(nc.dram_tensor("out_0", (1, SEQ, D), FP32, kind="ExternalOutput").ap())
    build(nc, *args)
    r = _run(nc, [arrays], core_ids=[0])
    return r.results[0]["out_0"]
```

```python
from contextlib import ExitStack

import numpy as np
import concourse.bass as bass
from concourse import mybir

FP32 = mybir.dt.float32
INT32 = mybir.dt.int32
ALU = mybir.AluOpType
ACT = mybir.ActivationFunctionType
AX = mybir.AxisListType

P = 128
SEQ, D, DEPTH = 256, 1024, 2
NT = SEQ // P
NK = D // P
CHUNK = 64
EPS = 1e-6
A_HEADS, B_HEADS, C_HEADS, IDX_HEADS, HD = 4, 8, 16, 4, 64
A_V = 2 * HD
TOPK = SEQ // 4
SCALE = HD ** -0.5
BUCKETS = 32
NEG = -1e30
GONE = -3e38
LAM_INIT = 0.8 - 0.6 * 1.0
GROUPS, PER_GROUP, TOP_EXPERTS = 4, 8, 2
EXPERTS = GROUPS * PER_GROUP
F = D // 2
NF = F // P
ROUTES = GROUPS + EXPERTS

CW = 256
AB_IN = 2500
A_CHUNKS = -(-AB_IN // CW)
C_CHUNKS = 3 * D // CW
IN_CHUNKS = (A_CHUNKS, C_CHUNKS)
SLOT_W = NK * CW
OUT_CHUNKS = D * NK // SLOT_W
KPC = NK // OUT_CHUNKS

AT_ONCE = 2
SLOTS = P // AT_ONCE
PAIRS = EXPERTS // AT_ONCE
MAX_PASSES = SEQ // SLOTS
PEELED = 2
LAST = 3
AHEAD = 2
UP_CHUNKS = 4
KPU = NK // UP_CHUNKS
CHUNKS = 2 * UP_CHUNKS + NF

BL = SEQ + P - 1
BW = BL + 1

PICKS = NT * AT_ONCE
UNITS = 16
ATT = 3
FLUSH = 4
PLACES = CHUNKS + OUT_CHUNKS
IN_BIAS = C_HEADS * SEQ // SLOT_W
ONCE = 1 + IN_BIAS + 2
ROUND = PLACES // (PLACES - CHUNKS)


def once(i, c):
    return c - OUT_CHUNKS if i == 1 and 0 <= c - OUT_CHUNKS < ONCE else None


def place_of(i, c):
    return (i * CHUNKS + c - (ONCE if (i, c) >= (1, OUT_CHUNKS) else 0)) % PLACES


def loads(layer, i, c):
    p = place_of(i, c)
    mixer = p < IN_CHUNKS[layer] or p >= CHUNKS
    return mixer + sum(once(*n) is None and place_of(*n) == p for n in
                       [divmod(m, CHUNKS) for m in range(i * CHUNKS + c + 1)])


def left_at(p):
    return ROUND * CHUNKS - 1 - max(m for m in range(ROUND * CHUNKS) if once(*divmod(m, CHUNKS)) is None
                                    and place_of(*divmod(m, CHUNKS)) == p)


def used_before(i, c):
    p = place_of(i, c)
    return 1 + max(m for m in range(i * CHUNKS + c) if once(*divmod(m, CHUNKS)) is None and place_of(*divmod(m, CHUNKS)) == p)


def unit_of(layer, u):
    g, qt, j = u // 4, u // 2 % 2, u % 2
    kind = "c" if layer else ("b", "b", "a", "a")[g]
    return kind, 2 * (g if layer else g % 2) + j, qt, P * (qt + 1)


ORDER = ([8, 9, 6, 7, 0, 2, 4, 1, 3, 5], [8, 0, 4, 1, 5, 9, 2, 6, 10, 3, 7, 11])
BY_DVE = ([9, 1, 3], [4, 1, 9, 6, 3, 11])
STEP_AFTER = ([(0, 3), (2, 1), (2, 3), (4, 0), (4, 1), (4, 3), (1, 0), (1, 1), (1, 3), (3, 0), (3, 1), (3, 3),
               (5, 0), (5, 1), (5, 3)],
              [(1, 1), (1, 3), (5, 1), (5, 3), (2, 1), (2, 3), (6, 1), (6, 3), (3, 0), (3, 2), (7, 0), (7, 3),
               (11, 0), (11, 1), (11, 3)])
FLIP_AFTER = {(7, 1): [0], (7, 2): [1], (7, 3): [2], (0, 0): [3], (0, 1): [4], (0, 2): [5]}
SPREAD_AFTER = (6, 0)
INDEX_AFTER = {(6, 1): 0, (6, 2): 1, (6, 3): 2, (7, 0): 3}


def events(layer):
    out, step = [], 0
    for pos, c in enumerate(ORDER[layer]):
        for quarter in range(4):
            out.append(("tile", pos, quarter))
            if quarter == 3:
                out.append(("copy", pos, None))
            if layer == 0:
                out += [("flip", b, None) for b in FLIP_AFTER.get((c, quarter), [])]
                if (c, quarter) == SPREAD_AFTER:
                    out.append(("spread", None, None))
                if (c, quarter) in INDEX_AFTER:
                    out.append(("index", INDEX_AFTER[c, quarter], None))
            if (c, quarter) in STEP_AFTER[layer]:
                out.append(("step", step, None))
                step += 1
    return out + [("step", n, None) for n in range(step, UNITS + FLUSH)]


OUT_ORDER = ([4, 5, 6, 7, 0, 1, 2, 3], [0, 1, 2, 3, 4, 5, 6, 7])
EARLY = 4


OUT_BANK = (6, 7, 4, 5)


def output_due(n):
    return n >= FLUSH and (n - FLUSH) % 2 == 1


def by_dve(layer, pos):
    return ORDER[layer][pos] in BY_DVE[layer]


def copies(layer, pos):
    return sum(by_dve(layer, n) == by_dve(layer, pos) for n in range(pos + 1))


def build(nc, x, t5, ln_mix, ln_ffn, ln_final, ab_in, ab_out, lam, subln, c_in, c_out, rel,
          w_rg, b_rg, w_re, b_re, w_gate, w_up, w_down, consts, hot_t5, hot_rel, out):
    ctx = ExitStack()
    with ctx:
        def sb(name, shape, dt=FP32):
            return ctx.enter_context(nc.sbuf_tensor(name, shape, dt))

        def sem(name):
            return ctx.enter_context(nc.semaphore(name))

        def per_layer(name):
            return [sem(f"{name}{l}") for l in range(DEPTH)]

        ring = sb("ring", [P, CHUNKS, SLOT_W])
        wo = sb("wo", [P, OUT_CHUNKS, KPC, D])
        h = sb("h", [P, NT, D])
        xn = sb("xn", [P, NT, D])
        xT = sb("xT", [P, NK, SEQ])
        bias = sb("bias", [P, C_HEADS, SEQ])
        mix = sb("mix", [P, 6144])
        gain_att = sb("gain_att", [P, D + ATT * 2 * SEQ])
        kon = sb("kon", [P, 4 * P + SEQ])
        wr = sb("wr", [P, NK, ROUTES])
        br = sb("br", [P, DEPTH, ROUTES])
        drop0 = sb("drop0", [P, P])
        sm = sb("sm", [P, 128])
        more_passes = sb("more_passes", [1, 1], INT32)
        PS = ctx.enter_context(nc.psum_tensor("PS", [P, 8, 512], FP32))
        bounce = nc.dram_tensor("bounce", [DEPTH, C_HEADS, BW], FP32, kind="Internal")

        gain = gain_att[:, 0:D]
        att = gain_att[:, D:].rearrange("p (u a n) -> p u a n", u=ATT, a=2)
        ident = kon[:, 0:P]
        flip = kon[:, P:2 * P]
        before = kon[:, 2 * P:3 * P]
        ones = kon[:, 3 * P:4 * P]

        def at(base, *shape):
            n = int(np.prod(shape))
            ap = mix[:, base:base + n]
            if len(shape) == 2:
                ap = ap.rearrange("p (a b) -> p a b", b=shape[1])
            if len(shape) == 3:
                ap = ap.rearrange("p (a b c) -> p a b c", b=shape[1], c=shape[2])
            return ap

        qkA = at(0, 8, SEQ)
        vA = at(2048, NT, 512)
        qB = at(3072, 4, SEQ)
        kqi = at(4096, 4, SEQ)
        vB = at(5120, NT, HD)
        wI = at(5248, NT, IDX_HEADS)
        sublnb = at(5256, A_V)
        lamb = at(5384, 4, HD)
        qkC = at(0, 16, SEQ)
        vC = at(4096, NT, D)
        xg = at(0, NK, P)
        hid = at(1024, F)
        hidT = gain_att[:, SLOT_W:SLOT_W + F].rearrange("p (a b) -> p a b", a=NF)
        ye = at(2560, D)
        logT = at(2560, NT, P)
        pick = at(3584, NT, AT_ONCE * SLOTS)
        pickw = at(3840, NT, AT_ONCE * SLOTS)
        pickT = at(4096, NT, P)
        rank = at(4352, NT, EXPERTS)
        comb = at(4416, NT, EXPERTS)
        chose = at(4480, NT, EXPERTS)
        lg = at(4544, NT, ROUTES)
        prod = at(4616, NT, EXPERTS)
        rsm = at(4680, 256)
        rd_g, re_g, rd_e, re_e = (rsm[:, o:o + NT * n].rearrange("p (t n) -> p t n", t=NT)
                                  for o, n in ((0, GROUPS), (8, GROUPS), (16, PER_GROUP), (32, PER_GROUP)))
        now, now_w, now_slots = at(4936, NT, AT_ONCE), at(4940, NT, AT_ONCE), at(4944, SLOTS)
        isc, cand, over, same = (bias[:, 12 + j] for j in range(4))
        sqa = bias[:, 12:16]
        drop = [drop0[:, :], over]
        pT = gain.rearrange("p (a n) -> p a n", a=2)
        raw = bias[:, :, :].rearrange("p a n -> p (a n)")
        hot5, tab5 = raw[0:BUCKETS, 0:BW], raw[0:BUCKETS, BW:BW + A_HEADS + B_HEADS]
        hotr = raw[:, 512:512 + 2 * BW].rearrange("p (a n) -> p a n", a=2)
        tabr = raw[:, 512 + 2 * BW:512 + 2 * BW + 2 * C_HEADS].rearrange("p (a n) -> p a n", a=2)
        rows_t5, rows_rel = (att[:, a].rearrange("p a n -> p (a n)")[0:n, 0:BW] for a, n in ((0, A_HEADS + B_HEADS), (1, C_HEADS)))
        ss = sm[:, 0:2]
        rstd = sm[:, 2:4]
        half = sm[:, 4:12]
        nmax = sm[:, 120:120 + 2 * ATT].rearrange("p (a b) -> p a b", b=2)
        den = sm[:, 16:48]
        rden = sm[:, 48:80]
        lsum = sm[:, 80:84]
        nlam = sm[:, 84:85]
        ssa = sm[:, 88:96]
        rsa = sm[:, 96:104]
        top8 = sm[:, 104:112]
        left = sm[:, 112:114]
        spare = sm[:, 114:116]
        gate_v = w_gate.rearrange("l e (p k) f -> l p e (k f)", k=NK)
        up_v = w_up.rearrange("l e (p k) f -> l p e (k f)", k=NK)
        down_v = w_down.rearrange("l e (p k) n -> l p e (k n)", k=NF)
        in_v = [ab_in[0].rearrange("(p k) n -> p k n", k=NK), c_in[0].rearrange("(p k) n -> p k n", k=NK)]
        out_v = [ab_out[0].rearrange("(k p) n -> p k n", k=NK), c_out[0].rearrange("(k p) n -> p k n", k=NK)]

        def place(p):
            return ring[:, p, :] if p < CHUNKS else wo[:, p - CHUNKS].rearrange("p k n -> p (k n)")

        def whole(i, c):
            n = once(i, c)
            if n is None:
                return place(place_of(i, c))
            if n == 0:
                return xT[:, :, :].rearrange("p k n -> p (k n)")
            if n <= IN_BIAS:
                return raw[:, (n - 1) * SLOT_W:n * SLOT_W]
            return gain_att[:, 0:SLOT_W]

        def slot(i, c, e):
            w = SLOT_W // AT_ONCE
            return at((5120, 1536)[e], w) if once(i, c) == ONCE - 1 else whole(i, c)[:, e * w:(e + 1) * w]

        s_x, s_kon, s_half = [sem(f"x_in{t}") for t in range(NT)], sem("consts_in"), sem("half_set")
        s_tab, s_lamin = sem("tables_in"), sem("lambda_in")
        s_vec, s_vecsb, s_vecout, s_z = sem("bias_rows"), sem("bias_rows_sb"), sem("bias_rows_out"), per_layer("bias_raw_in")
        s_flip, s_ba = per_layer("flipped"), per_layer("bias_copied")
        s_gain, s_ss, s_ms, s_rs, s_xn = sem("gain_in"), sem("squares"), sem("mean_sq"), sem("rstd"), sem("normed")
        s_turn, s_td, s_ta = sem("turned"), sem("turned_dve"), sem("turned_act")
        s_place = [[sem(f"loaded{l}_{p}") for p in range(PLACES)] for l in range(DEPTH)]
        s_once = [sem(f"once_{n}") for n in range(ONCE)]
        s_proj, s_pa, s_pd = per_layer("projected"), per_layer("proj_act"), per_layer("proj_dve")
        s_is, s_ir, s_drop = sem("index_scores"), sem("index_relu"), sem("selection")
        s_sc, s_sr, s_lo, s_ex, s_co = per_layer("scored"), per_layer("scores_read"), per_layer("logits"), per_layer("exped"), per_layer("combined")
        s_tp, s_pt, s_pv, s_out = per_layer("p_turned"), per_layer("pT_ready"), per_layer("pv_done"), per_layer("out_read")
        s_vb, s_spread, s_twice = sem("values_b_ready"), sem("spread"), sem("keys_twice")
        s_ssa, s_msa, s_rsa = sem("a_squares"), sem("a_mean_sq"), sem("a_rstd")
        s_lexp, s_lred = sem("lambda_exp"), sem("lambda_sums")
        s_sub, s_od = sem("sub_normed"), per_layer("out_projected")
        s_h = sem("residual")
        s_wr, s_br = per_layer("router_in"), sem("router_bias_in")
        s_lg, s_rd, s_re, s_ch, s_rk, s_go = (per_layer("route_logits"), per_layer("route_diff"), per_layer("route_exp"),
                                              per_layer("chosen"), per_layer("ranked"), per_layer("routed"))
        s_used = per_layer("chunks_used")
        s_now, s_pk, s_pw = per_layer("columns_copied"), per_layer("picked"), per_layer("pick_weighted")
        s_g, s_xg, s_pkt, s_pkT = per_layer("gathered"), per_layer("xg_ready"), per_layer("pick_turned"), per_layer("pickT_ready")
        s_si, s_hi = per_layer("silu_ready"), per_layer("hidden_ready")
        s_ht, s_hT = per_layer("hid_turned"), per_layer("hidT_ready")
        s_ya, s_yd = per_layer("ye_act"), per_layer("ye_dve")
        s_sca, s_add = per_layer("scattered"), per_layer("added")
        s_lT, s_lc = per_layer("route_products"), per_layer("route_copied")
        s_dve, s_final = sem("dve_chain"), sem("final_out")

        def raw_rows(l, heads):
            return bass.AP(bounce, l * C_HEADS * BW, [[1, P], [BW, heads], [1, SEQ]])

        block = ctx.enter_context(nc.Block())

        def proj_dst(l, c):
            if l == 0:
                return [qkA[:, 0:2], qkA[:, 2:4], qkA[:, 4:6], qkA[:, 6:8], vA[:, :, 0:CW], vA[:, :, CW:2 * CW],
                        qB[:, 0:2], qB[:, 2:4], kqi[:, 0:2], kqi[:, 2:4]][c]
            return qkC[:, 2 * c:2 * c + 2] if c < 8 else vC[:, :, (c - 8) * CW:(c - 7) * CW]

        @block.sync
        def _(sp):
            for t in range(NT):
                sp.dma_start(h[:, t, :], x[0, t * P:(t + 1) * P, :]).then_inc(s_x[t], 16)

            def w_in(l, pos):
                c = ORDER[l][pos]
                n = min(CW, in_v[l].shape[2] - c * CW)
                dst = place(pos).rearrange("p (k n) -> p k n", n=CW)[:, :, 0:n]
                sp.dma_start(dst, in_v[l][:, :, c * CW:c * CW + n]).then_inc(s_place[l][pos], 16)

            def w_out(l, c):
                sp.dma_start(wo[:, c], out_v[l][:, c * KPC:(c + 1) * KPC, :]).then_inc(s_place[l][CHUNKS + c], 16)

            def chunk(l, pair, i, c):
                n = once(i, c)
                signal = s_place[l][place_of(i, c)] if n is None else s_once[n]
                if c < 2 * UP_CHUNKS:
                    src, j, w = (gate_v, c, KPU * F) if c < UP_CHUNKS else (up_v, c - UP_CHUNKS, KPU * F)
                else:
                    src, j, w = down_v, c - 2 * UP_CHUNKS, D
                if n == ONCE - 1:
                    for e in range(AT_ONCE):
                        sp.dma_start(slot(i, c, e), src[l, :, pair * AT_ONCE + e, j * w:(j + 1) * w]).then_inc(signal, 16)
                    return
                sp.dma_start(whole(i, c).rearrange("p (e n) -> p e n", e=AT_ONCE),
                             src[l, :, bass.ds(pair * AT_ONCE, AT_ONCE), j * w:(j + 1) * w]).then_inc(signal, 16)

            for l in range(DEPTH):
                for c in range(IN_CHUNKS[l]):
                    if l == 0 and c == 2:
                        sp.wait_ge(s_tab, 16 * 4)
                    if l == 0 and c == 3:
                        sp.wait_ge(s_vecout, 32)
                    if l == 0 and c == 4:
                        sp.wait_ge(s_z[0], 16)
                    if l:
                        sp.wait_ge(s_used[0], trips * CHUNKS - left_at(c))
                    w_in(l, c)
                for c in range(OUT_CHUNKS):
                    if l:
                        sp.wait_ge(s_used[0], trips * CHUNKS - left_at(CHUNKS + c))
                    w_out(l, c)
                for c in range(CHUNKS):
                    if c < IN_CHUNKS[l]:
                        sp.wait_ge(s_proj[l], c + 1)
                    chunk(l, 0, 0, c)
                sp.wait_ge(s_lo[l], UNITS)
                if l == 0:
                    sp.wait_ge(s_ssa, 3 * 4)
                for c in range(OUT_CHUNKS + 1, OUT_CHUNKS + 1 + IN_BIAS):
                    chunk(l, 1, 1, c)
                for m in range(OUT_CHUNKS):
                    sp.wait_ge(s_od[l], 3 + m + 1)
                    chunk(l, 1, 1, OUT_ORDER[l][m * KPC] // KPC)
                sp.wait_ge(s_xn, 4 * l + 4)
                chunk(l, 1, 1, OUT_CHUNKS + ONCE - 2)
                sp.wait_ge(s_ss, 2 * (2 * l + 1) + 2)
                chunk(l, 1, 1, OUT_CHUNKS + ONCE - 1)
                sp.wait_ge(s_lg[l], 2)
                chunk(l, 1, 1, OUT_CHUNKS)
                for c in range(OUT_CHUNKS + ONCE, CHUNKS):
                    sp.wait_ge(s_used[l], used_before(1, c))
                    chunk(l, 1, 1, c)
                for i in range(2, ROUND):
                    if l == 0 and i == 3:
                        sp.wait_ge(s_used[0], CHUNKS + OUT_CHUNKS + 1 + IN_BIAS)
                        sp.dma_start(bias[:, :, :], raw_rows(1, C_HEADS)).then_inc(s_z[1], 16)
                    for c in range(CHUNKS):
                        sp.wait_ge(s_used[l], used_before(i, c))
                        chunk(l, i, i, c)
                sp.wait_ge(s_go[l], 1)
                trips = sp.snap(sp.value_load(more_passes[0:1, 0:1], min_val=0, max_val=MAX_PASSES - 1) * PAIRS + PAIRS)
                with sp.Fori(0, trips // ROUND - 1) as g:
                    for i in range(ROUND, 2 * ROUND):
                        for c in range(CHUNKS):
                            sp.wait_ge(s_used[l], g * (ROUND * CHUNKS) + used_before(i, c))
                            chunk(l, (g * ROUND + i) % PAIRS, i, c)
            for q in range(2 * NT):
                t, cols = q // 2, slice(q % 2 * D // 2, (q % 2 + 1) * D // 2)
                sp.wait_ge(s_xn, 2 * 4 + q + 1)
                sp.dma_start(out[0, t * P:(t + 1) * P, cols], xn[:, t, cols]).then_inc(s_final, 16)
            sp.wait_ge(s_final, 16 * 2 * NT)

        @block.gpsimd
        def _(pool):
            pool.memset(half, -0.5).then_inc(s_half, 1)
            pool.dma_start(hot5, hot_t5).then_inc(s_tab, 16)
            pool.dma_start(tab5, t5).then_inc(s_tab, 16)
            pool.dma_start(hotr, hot_rel.rearrange("(a p) n -> p a n", p=P)).then_inc(s_tab, 16)
            pool.dma_start(tabr, rel[0, 1:1 + 2 * P, :].rearrange("(a p) n -> p a n", p=P)).then_inc(s_tab, 16)
            def rstd_of(n, t):
                pool.wait_ge(s_ss, 2 * n + t + 1)
                pool.tensor_scalar(rstd[:, t:t + 1], ss[:, t:t + 1], 1.0 / D, EPS, ALU.mult, ALU.add).then_inc(s_ms, 1)
                pool.wait_ge(s_ms, 2 * n + t + 1)
                pool.tensor_tensor(rstd[:, t:t + 1], rstd[:, t:t + 1], half[:, 0:1], ALU.pow).then_inc(s_rs, 1)

            def carry_waits(site):
                pool.tensor_tensor(spare[:, site:site + 1], half[:, 0:1], half[:, 0:1], ALU.mult)

            pool.wait_ge(s_half, 1)
            for t in range(NT):
                rstd_of(0, t)
            pool.dma_start(lamb, lam[0:1].broadcast_to((P, 4, HD))).then_inc(s_lamin, 16)
            pool.dma_start(sublnb, subln[0:1].broadcast_to((P, A_V))).then_inc(s_lamin, 16)
            for l in range(DEPTH):
                pool.dma_start(br[:, l, 0:GROUPS], b_rg[l:l + 1].broadcast_to((P, GROUPS))).then_inc(s_br, 16)
                pool.dma_start(br[:, l, GROUPS:ROUTES], b_re[l:l + 1].broadcast_to((P, EXPERTS))).then_inc(s_br, 16)
            pool.wait_ge(s_vecsb, 2)
            pool.dma_start(bounce.ap()[0, 0:A_HEADS + B_HEADS], rows_t5).then_inc(s_vecout, 16)
            pool.dma_start(bounce.ap()[1], rows_rel).then_inc(s_vecout, 16)
            pool.wait_ge(s_vecout, 32)

            pool.dma_start(bias[:, 0:A_HEADS + B_HEADS, :], raw_rows(0, A_HEADS + B_HEADS)).then_inc(s_z[0], 16)
            for l in range(DEPTH):
                pool.dma_start(wr[:, :, 0:GROUPS], w_rg[l].rearrange("(p k) g -> p k g", k=NK)).then_inc(s_wr[l], 16)
                pool.dma_start(wr[:, :, GROUPS:ROUTES], w_re[l].rearrange("(p k) g -> p k g", k=NK)).then_inc(s_wr[l], 16)
                if l == 0:
                    for n in range(4):
                        cols = slice(2 * n, 2 * n + 2)
                        pool.wait_ge(s_ssa, 3 * n + 3)
                        pool.tensor_scalar(rsa[:, cols], ssa[:, cols], 1.0 / A_V, EPS, ALU.mult, ALU.add).then_inc(s_msa, 1)
                        pool.wait_ge(s_msa, n + 1)
                        pool.tensor_tensor(rsa[:, cols], rsa[:, cols], half[:, 0:2], ALU.pow).then_inc(s_rsa, 1)
                        pool.wait_ge(s_rsa, 2 * n + 1)
                        ya = xn[:, n % 2, CW * (n // 2):CW * (n // 2 + 1)].rearrange("p (a n) -> p a n", n=A_V)
                        pool.tensor_tensor(ya, ya, rsa[:, cols].unsqueeze(2).broadcast_to((P, 2, A_V)), ALU.mult).then_inc(s_rsa, 1)
                        pool.wait_ge(s_rsa, 2 * n + 2)
                        pool.tensor_tensor(ya, ya, sublnb.unsqueeze(1).broadcast_to((P, 2, A_V)), ALU.mult).then_inc(s_sub, 1)
                for t in range(NT):
                    rstd_of(2 * l + 1, t)

                def pick_rows(i):
                    experts = bass.ds(i % PAIRS * AT_ONCE, AT_ONCE)
                    pool.wait_ge(s_pw[l], i * PICKS)
                    pool.tensor_copy(now, rank[:, :, experts]).then_inc(s_now[l], 1)
                    pool.tensor_copy(now_w, comb[:, :, experts]).then_inc(s_now[l], 1)
                    pool.tensor_copy(now_slots, kon[:, bass.ds(i // PAIRS * SLOTS + 4 * P, SLOTS)]).then_inc(s_now[l], 1)
                    pool.wait_ge(s_now[l], i * 3)
                    pool.wait_ge(s_g[l], i * 2)
                    carry_waits(0)
                    for t in range(NT):
                        for e in range(AT_ONCE):
                            pool.tensor_scalar(pick[:, t, e * SLOTS:(e + 1) * SLOTS], now_slots, now[:, t, e:e + 1],
                                               None, ALU.is_equal).then_inc(s_pk[l], 1)
                    pool.wait_ge(s_pkt[l], i)
                    carry_waits(1)
                    for t in range(NT):
                        for e in range(AT_ONCE):
                            pool.tensor_scalar(pickw[:, t, e * SLOTS:(e + 1) * SLOTS], now_slots, now[:, t, e:e + 1],
                                               now_w[:, t, e:e + 1], ALU.is_equal, ALU.mult).then_inc(s_pw[l], 1)

                pool.wait_ge(s_pw[l], PICKS)
                pick_rows(1)
                pick_rows(2)
                pool.wait_ge(s_go[l], 1)
                more = pool.value_load(more_passes[0:1, 0:1], min_val=0, max_val=MAX_PASSES - 1)
                with pool.Fori(0, pool.snap(more * PAIRS + (PAIRS - PEELED - 1))) as i:
                    pick_rows(i + (PEELED + 1))
                if l + 1 < DEPTH:
                    for t in range(NT):
                        rstd_of(2 * l + 2, t)
            for t in range(NT):
                rstd_of(2 * DEPTH, t)

        @block.scalar
        def _(act):
            gains = [ln_mix[0:1], ln_ffn[0:1], ln_mix[1:2], ln_ffn[1:2], ln_final.rearrange("(a d) -> a d", a=1)]

            def load_gain(n):
                if n:
                    act.wait_ge(s_xn, 2 * n)
                act.dma_start(gain, gains[n].broadcast_to((P, D))).then_inc(s_gain, 16)

            def squares(n, t, junk):
                act.activation(junk, h[:, t], ACT.Square, accum_out=ss[:, t:t + 1]).then_inc(s_ss, 1)

            def turn_copy(j, t):
                act.wait_ge(s_turn, 4 * j + 2 * t + 2)
                act.activation(xT[:, 4:8, t * P:(t + 1) * P], PS[:, 2 * t + 1].rearrange("p (k n) -> p k n", k=4), ACT.Copy)\
                    .then_inc(s_ta, 1)

            def bias_copy(l, b, bank):
                act.wait_ge(s_flip[l], b + 1)
                act.activation(bias[:, 2 * b:2 * b + 2, :], PS[:, bank].rearrange("p (a n) -> p a n", a=2), ACT.Copy)\
                    .then_inc(s_ba[l], 1)

            def exps(l, u):
                act.wait_ge(s_lo[l], u + 1)
                n = unit_of(l, u)[3]
                for j in range(2):
                    act.activation(att[:, u % ATT, j, 0:n], att[:, u % ATT, j, 0:n], ACT.Exp, bias=nmax[:, u % ATT, j:j + 1],
                                   accum_out=den[:, 2 * u + j:2 * u + j + 1]).then_inc(s_ex[l], 1)

            def probs_copy(l, u):
                kind, _, _, n = unit_of(l, u)
                w = n if kind == "a" else 2 * n
                act.wait_ge(s_tp[l], u + 1)
                if u >= 2:
                    act.wait_ge(s_pv[l], u - 1)
                act.activation(pT[:, u % 2, 0:w], PS[:, 2 + u % 2, 0:w], ACT.Copy).then_inc(s_pt[l], 1)

            def outputs(l, u):
                kind, i, qt, _ = unit_of(l, u)
                act.wait_ge(s_pv[l], u + 1)
                act.activation((qB if kind == "b" else qkC)[:, i, qt * P:(qt + 1) * P], PS[:, 4 + u % 2, 0:P], ACT.Copy)\
                    .then_inc(s_out[l], 1)

            def outputs_a(u):
                g, qt = u // 4, u // 2 % 2
                n = 2 * (g - 2) + qt
                act.wait_ge(s_pv[0], u + 1)
                for j in range(2):
                    act.activation(sqa[:, n, j * A_V:(j + 1) * A_V], PS[:, 4 + qt, j * A_V:(j + 1) * A_V], ACT.Square,
                                   accum_out=ssa[:, 2 * n + j:2 * n + j + 1]).then_inc(s_ssa, 1)
                act.activation(xn[:, qt, CW * (g - 2):CW * (g - 1)], PS[:, 4 + qt, 0:CW], ACT.Copy).then_inc(s_ssa, 1)

            def spread_copy():
                act.wait_ge(s_spread, 1)
                act.activation(vB, PS[:, 5, 0:NT * HD].rearrange("p (t n) -> p t n", t=NT), ACT.Copy).then_inc(s_vb, 1)
                act.activation(wI, PS[:, 5, NT * HD:NT * (HD + IDX_HEADS)].rearrange("p (t n) -> p t n", t=NT), ACT.Copy,
                               scale=(IDX_HEADS ** -0.5) * (HD ** -0.5)).then_inc(s_vb, 1)

            def index_relu(v):
                n = P * (v // 2 + 1)
                act.wait_ge(s_is, v + 1)
                if v == 0:
                    act.wait_ge(s_vecout, 32)
                if v >= 2:
                    act.wait_ge(s_drop, 2 * (v - 1))
                act.activation(att[:, v % 2, :, 0:n], PS[:, 0:2, 0:n], ACT.Relu).then_inc(s_ir, 1)

            def mixer(l):
                for what, n, _ in events(l):
                    if what == "copy" and not by_dve(l, n):
                        act.wait_ge(s_proj[l], n + 1)
                        act.activation(proj_dst(l, ORDER[l][n]), PS[:, 6 + n % 2].rearrange("p (a n) -> p a n", a=2), ACT.Copy)\
                            .then_inc(s_pa[l], 1)
                    elif what == "flip":
                        bias_copy(0, n, 2 + n % 2)
                    elif what == "spread":
                        spread_copy()
                    elif what == "index":
                        index_relu(n)
                    elif what == "step":
                        if n == 0:
                            act.wait_ge(s_xn, 4 * l + 2)
                        if 2 <= n <= UNITS + 1:
                            probs_copy(l, n - 2)
                        if n < UNITS:
                            exps(l, n)
                        if output_due(n) and unit_of(l, n - FLUSH)[0] == "a":
                            outputs_a(n - FLUSH)
                        if n >= FLUSH and unit_of(l, n - FLUSH)[0] != "a":
                            outputs(l, n - FLUSH)

            load_gain(0)
            act.dma_start(kon[:, :], consts).then_inc(s_kon, 16)
            for t in range(NT):
                act.wait_ge(s_x[t], 16)
                squares(0, t, xn[:, t])
            for t in range(NT):
                turn_copy(0, t)
            act.wait_ge(s_vec, 2)
            act.activation(rows_rel, PS[0:C_HEADS, 5, 0:BW], ACT.Copy).then_inc(s_vecsb, 1)
            act.wait_ge(s_lred, 2)
            act.activation(lsum[:, 2:4], lsum[:, 0:2], ACT.Exp).then_inc(s_lexp, 1)
            for l in range(DEPTH):
                if l:
                    for t in range(NT):
                        turn_copy(3 * l, t)
                mixer(l)
                act.wait_ge(s_pv[l], UNITS)
                load_gain(2 * l + 1)
                if l == 0:
                    for t in range(NT):
                        act.wait_ge(s_turn, 4 + 2 * t + 2)
                        act.activation(xT[:, 2:4, t * P:(t + 1) * P], PS[:, 2 * t + 1, 0:2 * P].rearrange("p (k n) -> p k n", k=2),
                                       ACT.Copy).then_inc(s_ta, 1)
                for t in range(NT):
                    act.wait_ge(s_h, 4 * l + 2 * t + 2)
                    squares(2 * l + 1, t, mix[:, (4 + t) * D:(5 + t) * D])
                    turn_copy(2 * l + 2, t)
                    act.wait_ge(s_lT[l], t + 1)
                    act.activation(logT[0:ROUTES, t], PS[0:ROUTES, 6 + t, 0:P], ACT.Copy).then_inc(s_lc[l], 1)
                    for j, (a, b) in enumerate(((rd_g, re_g), (rd_e, re_e))):
                        act.wait_ge(s_rd[l], 2 * t + j + 1)
                        act.activation(b[:, t], a[:, t], ACT.Exp).then_inc(s_re[l], 1)

                def gathered_copy(i, b, first=False):
                    act.wait_ge(s_g[l], i * 2 + (b + 1))
                    if b == 0 and not first:
                        act.wait_ge(s_used[l], i * CHUNKS - (CHUNKS - 2 * UP_CHUNKS))
                    act.activation(xg[:, 4 * b:4 * b + 4, :], PS[:, b].rearrange("p (k n) -> p k n", k=4), ACT.Copy)\
                        .then_inc(s_xg[l], 1)

                def experts(i, first=False, final=False):
                    act.wait_ge(s_used[l], i * CHUNKS + UP_CHUNKS)
                    if not first:
                        act.wait_ge(s_ht[l], i)
                    act.activation(hid, PS[:, 2], ACT.Silu).then_inc(s_si[l], 1)
                    if not final:
                        gathered_copy(i + 1, 0)
                    act.wait_ge(s_ht[l], i + 1)
                    act.activation(hidT, PS[:, 4].rearrange("p (k n) -> p k n", k=NF), ACT.Copy).then_inc(s_hT[l], 1)
                    if not final:
                        gathered_copy(i + 1, 1)
                    act.wait_ge(s_used[l], i * CHUNKS + CHUNKS)
                    if not first:
                        act.wait_ge(s_sca[l], i * 4)
                    act.activation(ye[:, 0:512], PS[:, 6], ACT.Copy).then_inc(s_ya[l], 1)

                for b in range(2):
                    gathered_copy(0, b, True)
                experts(0, first=True)
                experts(1)
                act.wait_ge(s_used[l], CHUNKS + OUT_CHUNKS + ONCE - 1)
                load_gain(2 * l + 2)
                act.wait_ge(s_go[l], 1)
                more = act.value_load(more_passes[0:1, 0:1], min_val=0, max_val=MAX_PASSES - 1)
                trips = act.snap(more * PAIRS + PAIRS)
                with act.Fori(0, trips - (PEELED + LAST)) as i:
                    experts(i + PEELED)
                if l == 0:
                    for b in range(C_HEADS // 2):
                        bias_copy(1, b, b % 2)
                for n in range(LAST, 0, -1):
                    experts(trips - n, final=(n == 1))
                for t in range(NT):
                    act.wait_ge(s_add[l], trips * 4 - 2 * (NT - 1 - t))
                    squares(2 * l + 2, t, xn[:, t])

        @block.vector
        def _(dve):
            chain = [0]

            def link(ins):
                chain[0] += 1
                ins.then_inc(s_dve, 1)
                dve.wait_ge(s_dve, chain[0])

            def scaled(n, t, cols=slice(0, D)):
                dve.wait_ge(s_rs, 2 * n + t + 1)
                dve.wait_ge(s_gain, 16 * (n + 1))
                dve.scalar_tensor_tensor(xn[:, t, cols], h[:, t, cols], rstd[:, t:t + 1], gain[:, cols], ALU.mult, ALU.mult)\
                    .then_inc(s_xn, 1)

            def norm(n):
                for t in range(NT):
                    scaled(n, t)

            def turn_copy(j, t):
                dve.wait_ge(s_turn, 4 * j + 2 * t + 1)
                dve.tensor_copy(xT[:, 0:4, t * P:(t + 1) * P], PS[:, 2 * t].rearrange("p (k n) -> p k n", k=4)).then_inc(s_td, 1)

            def mask_bias(l, heads):
                dve.wait_ge(s_ba[l], heads // 2)
                link(dve.memset(bias[0:CHUNK, 0:heads, SEQ - CHUNK:SEQ], NEG))

            def first_of(k, scores, top, out_sel, w):
                link(dve.tensor_scalar(over[:, 0:w], scores, top, 0.0, ALU.is_gt, ALU.add, accum_out=left[:, 0:1]))
                link(dve.tensor_scalar(same[:, 0:w], scores, top, None, ALU.is_equal))
                link(dve.tensor_scalar(left[:, 1:2], left[:, 0:1], -1.0, float(k), ALU.mult, ALU.add))
                link(dve.tensor_tensor_scan(cand[:, 0:w], same[:, 0:w], same[:, 0:w], 0.0, ALU.add, ALU.max))
                link(dve.scalar_tensor_tensor(same[:, 0:w], cand[:, 0:w], left[:, 1:2], same[:, 0:w], ALU.is_le, ALU.mult))
                link(dve.tensor_tensor(out_sel, same[:, 0:w], over[:, 0:w], ALU.add))

            def select(qt):
                n = P * (qt + 1)
                if qt == 0:
                    dve.wait_ge(s_vb, 2)
                for v in range(2):
                    dve.wait_ge(s_ir, 2 * qt + v + 1)
                    for j in range(2):
                        hd = 2 * v + j
                        if hd == 0:
                            ins = dve.tensor_scalar(isc[:, 0:n], att[:, 0, 0, 0:n], wI[:, qt, 0:1], None, ALU.mult)
                        else:
                            ins = dve.scalar_tensor_tensor(isc[:, 0:n], att[:, v, j, 0:n], wI[:, qt, hd:hd + 1],
                                                           isc[:, 0:n], ALU.mult, ALU.add)
                        ins.then_inc(s_drop, 1)
                        dve.wait_ge(s_drop, 4 * qt + hd + 1)
                link(dve.memset(isc[0:CHUNK, n - CHUNK:n], NEG))
                link(dve.tensor_copy(cand[:, 0:n], isc[:, 0:n]))
                for r in range(TOPK // 8):
                    link(dve.max(top8, cand[:, 0:n]))
                    if r + 1 < TOPK // 8:
                        link(dve.match_replace(cand[:, 0:n], top8, cand[:, 0:n], GONE))
                first_of(TOPK, isc[:, 0:n], top8[:, 7:8], same[:, 0:n], n)
                link(dve.tensor_scalar(drop[qt][:, 0:n], same[:, 0:n], -1.0, -NEG, ALU.add, ALU.mult))

            def logits(l, u):
                kind, j, qt, n = unit_of(l, u)
                hd = {"a": j, "b": A_HEADS + 2 * j, "c": 2 * j}[kind]
                if kind == "a":
                    tile = bias[:, hd:hd + 1, SEQ - n:SEQ].broadcast_to((P, 2, n))
                else:
                    tile = bias[:, hd:hd + 2, SEQ - n:SEQ]
                dve.wait_ge(s_sc[l], u + 1)
                if u >= ATT:
                    dve.wait_ge(s_tp[l], u - ATT + 1)
                a = att[:, u % ATT, :, 0:n]
                dve.scalar_tensor_tensor(a, PS[:, 0:2, 0:n], SCALE, tile, ALU.mult, ALU.add).then_inc(s_sr[l], 1)
                dve.wait_ge(s_sr[l], u + 1)
                if kind == "b":
                    link(dve.tensor_tensor(a, a, drop[qt][:, 0:n].unsqueeze(1).broadcast_to((P, 2, n)), ALU.add))
                dve.tensor_reduce(nmax[:, u % ATT, :], a, AX.X, ALU.max, negate=True).then_inc(s_lo[l], 1)

            def combine(l, u):
                kind, _, _, n = unit_of(l, u)
                dve.wait_ge(s_ex[l], 2 * u + 2)
                link(dve.reciprocal(rden[:, 2 * u:2 * u + 2], den[:, 2 * u:2 * u + 2]))
                if kind != "a":
                    a = att[:, u % ATT, :, 0:n]
                    dve.tensor_tensor(a, a, rden[:, 2 * u:2 * u + 2].unsqueeze(2).broadcast_to((P, 2, n)), ALU.mult)\
                        .then_inc(s_co[l], 1)
                    return
                link(dve.tensor_scalar(att[:, u % ATT, 1, 0:n], att[:, u % ATT, 1, 0:n], rden[:, 2 * u + 1:2 * u + 2], nlam,
                                       ALU.mult, ALU.mult))
                dve.scalar_tensor_tensor(att[:, u % ATT, 0, 0:n], att[:, u % ATT, 0, 0:n], rden[:, 2 * u:2 * u + 1],
                                         att[:, u % ATT, 1, 0:n], ALU.mult, ALU.add).then_inc(s_co[l], 1)

            def mixer(l):
                for what, n, _ in events(l):
                    if what == "copy" and by_dve(l, n):
                        dve.wait_ge(s_proj[l], n + 1)
                        src = PS[:, 6 + n % 2].rearrange("p (a n) -> p a n", a=2)
                        if (l, ORDER[l][n]) == (0, A_CHUNKS - 1):
                            m = AB_IN % P
                            dve.tensor_copy(kqi[:, 2], src[:, 0])
                            dve.tensor_copy(kqi[0:m, 3], src[0:m, 1]).then_inc(s_pd[l], 1)
                        else:
                            dve.tensor_copy(proj_dst(l, ORDER[l][n]), src).then_inc(s_pd[l], 1)
                    elif what == "spread":
                        dve.wait_ge(s_spread, 2)
                        dve.tensor_copy(kqi[HD:P, 0:4:3], PS[HD:P, 4].rearrange("p (a n) -> p a n", a=2)).then_inc(s_twice, 1)
                    elif what == "index" and n % 2 == 1:
                        select(n // 2)
                    elif what == "step":
                        if l == 0 and n == 0:
                            mask_bias(0, A_HEADS + B_HEADS)
                        if n < UNITS:
                            logits(l, n)
                        if 1 <= n <= UNITS:
                            combine(l, n - 1)

            def residual(l, q):
                t, n = q // 2, q % 2
                dve.wait_ge(s_od[l], q + 1 if q < 3 else 3 + OUT_CHUNKS)
                dve.tensor_tensor(h[:, t, 512 * n:512 * n + 512], PS[:, OUT_BANK[q]], h[:, t, 512 * n:512 * n + 512], ALU.add)\
                    .then_inc(s_h, 1)

            def gained(l, t, b):
                dve.wait_ge(s_h, 4 * l + 2 * t + b + 1)
                if t == 0 and b == 0:
                    dve.wait_ge(s_gain, 16 * (2 * l + 2))
                cols = slice(512 * b, 512 * b + 512)
                ins = dve.tensor_tensor(xn[:, t, cols], h[:, t, cols], gain[:, cols], ALU.mult)
                if b:
                    ins.then_inc(s_xn, 1)

            def rescaled(l, t):
                dve.wait_ge(s_turn, 4 * (2 * l + 2) + 2 * t + 2)
                dve.wait_ge(s_rs, 2 * (2 * l + 1) + t + 1)
                dve.tensor_scalar(xn[:, t], xn[:, t], rstd[:, t:t + 1], None, ALU.mult)

            rsm_view = lambda o, n: rsm[:, o:o + NT * n].rearrange("p (t n) -> p t n", n=n)
            group, upg = rsm_view(48, GROUPS), rsm_view(56, GROUPS)
            es, sel, t8 = rsm_view(64, PER_GROUP), rsm_view(80, PER_GROUP), rsm_view(96, 8)
            mor, sam, upe = rsm_view(112, PER_GROUP), rsm_view(128, PER_GROUP), rsm_view(144, PER_GROUP)
            gm, gs, em, es1, cnt, fac = (rsm[:, 160 + 2 * j:162 + 2 * j] for j in range(6))
            mxc, stp = rsm[:, 180:181], rsm[:, 184:188]

            def ge(a):
                return a.rearrange("p (g e) -> p g e", g=GROUPS)

            def by_expert(t):
                return group[:, t].unsqueeze(2).broadcast_to((P, GROUPS, PER_GROUP))

            def route(l, t):
                def col(a):
                    return a[:, t:t + 1]

                dve.wait_ge(s_lg[l], t + 1)
                if t == 0:
                    dve.wait_ge(s_br, 16 * 4)
                link(dve.scalar_tensor_tensor(lg[:, t], PS[:, 6 + t, P:P + ROUTES], rstd[:, t:t + 1], br[:, l], ALU.mult, ALU.add))
                link(dve.tensor_reduce(col(gm), lg[:, t, 0:GROUPS], AX.X, ALU.max))
                dve.tensor_scalar(rd_g[:, t], lg[:, t, 0:GROUPS], col(gm), None, ALU.subtract).then_inc(s_rd[l], 1)
                link(dve.tensor_scalar(group[:, t], lg[:, t, 0:GROUPS], col(gm), None, ALU.is_equal))
                link(dve.tensor_tensor_scan(upg[:, t], group[:, t], group[:, t], 0.0, ALU.add, ALU.max))
                link(dve.scalar_tensor_tensor(group[:, t], upg[:, t], 1.0, group[:, t], ALU.is_le, ALU.mult))
                g4 = by_expert(t)
                link(dve.tensor_tensor(ge(prod[:, t]), ge(lg[:, t, GROUPS:ROUTES]), g4, ALU.mult))
                link(dve.tensor_reduce(es[:, t], prod[:, t].rearrange("p (g e) -> p e g", g=GROUPS), AX.X, ALU.add))
                link(dve.max(t8[:, t], es[:, t]))
                dve.tensor_scalar(rd_e[:, t], es[:, t], t8[:, t, 0:1], None, ALU.subtract).then_inc(s_rd[l], 1)
                dve.tensor_scalar(sam[:, t], es[:, t], t8[:, t, 1:2], None, ALU.is_equal)
                link(dve.tensor_scalar(mor[:, t], es[:, t], t8[:, t, 1:2], 0.0, ALU.is_gt, ALU.add, accum_out=col(cnt)))
                link(dve.tensor_tensor_scan(upe[:, t], sam[:, t], sam[:, t], 0.0, ALU.add, ALU.max))
                link(dve.tensor_scalar(upe[:, t], upe[:, t], col(cnt), float(TOP_EXPERTS), ALU.add, ALU.is_le))
                link(dve.tensor_tensor(sam[:, t], upe[:, t], sam[:, t], ALU.mult))
                link(dve.tensor_tensor(sel[:, t], sam[:, t], mor[:, t], ALU.add))
                dve.tensor_tensor(ge(chose[:, t]), g4, sel[:, t].unsqueeze(1).broadcast_to((P, GROUPS, PER_GROUP)),
                                  ALU.mult).then_inc(s_ch[l], 1)

            def weights(l, t):
                def col(a):
                    return a[:, t:t + 1]

                ee = re_e[:, t]
                dve.wait_ge(s_re[l], 2 * t + 1)
                link(dve.tensor_reduce(col(gs), re_g[:, t], AX.X, ALU.add))
                dve.wait_ge(s_re[l], 2 * t + 2)
                link(dve.tensor_tensor(ee, ee, sel[:, t], ALU.mult))
                link(dve.tensor_reduce(col(es1), ee, AX.X, ALU.add))
                link(dve.tensor_tensor(col(fac), col(es1), col(gs), ALU.mult))
                link(dve.reciprocal(col(fac), col(fac)))
                link(dve.tensor_scalar(ee, ee, col(fac), None, ALU.mult))
                link(dve.tensor_tensor(ge(comb[:, t]), by_expert(t), ee.unsqueeze(1).broadcast_to((P, GROUPS, PER_GROUP)), ALU.mult))

            def ranks(l):
                dve.wait_ge(s_ch[l], 2)
                dve.wait_ge(s_rk[l], 1)
                link(dve.scalar_tensor_tensor(rank, PS[:, 4, 0:NT * EXPERTS].rearrange("p (t n) -> p t n", t=NT), 1.0, chose,
                                              ALU.add, ALU.mult))
                shape = (P, AT_ONCE, SLOTS)
                split = lambda a: a.rearrange("p (e s) -> p e s", e=AT_ONCE)
                for t in range(NT):
                    dve.tensor_tensor(split(pick[:, t]), kon[:, 4 * P:4 * P + SLOTS].unsqueeze(1).broadcast_to(shape),
                                      rank[:, t, 0:AT_ONCE].unsqueeze(2).broadcast_to(shape), ALU.is_equal)\
                        .then_inc(s_pk[l], PICKS // NT)
                weights(l, 1)
                dve.wait_ge(s_pk[l], PICKS)
                for t in range(NT):
                    dve.tensor_tensor(split(pickw[:, t]), split(pick[:, t]),
                                      comb[:, t, 0:AT_ONCE].unsqueeze(2).broadcast_to(shape), ALU.mult)\
                        .then_inc(s_pw[l], PICKS // NT)
                dve.wait_ge(s_rk[l], 2)
                link(dve.tensor_reduce(mxc, PS[:, 5, 0:EXPERTS], AX.X, ALU.max))
                for j in range(1, MAX_PASSES):
                    link(dve.tensor_scalar(stp[:, j:j + 1], mxc, float(SLOTS * j), None, ALU.is_gt))
                link(dve.tensor_reduce(stp[:, 0:1], stp[:, 1:MAX_PASSES], AX.X, ALU.add))
                dve.tensor_copy(more_passes[:, :], stp[0:1, 0:1]).then_inc(s_go[l], 1)

            norm(0)
            for t in range(NT):
                turn_copy(0, t)
            dve.wait_ge(s_vec, 1)
            dve.tensor_copy(rows_t5, PS[0:A_HEADS + B_HEADS, 4, 0:BW]).then_inc(s_vecsb, 1)
            dve.wait_ge(s_lamin, 32)
            for j in range(2):
                link(dve.tensor_tensor(lamb[:, 2 * j], lamb[:, 2 * j], lamb[:, 2 * j + 1], ALU.mult))
                dve.tensor_reduce(lsum[:, j:j + 1], lamb[:, 2 * j], AX.X, ALU.add).then_inc(s_lred, 1)
            dve.wait_ge(s_lexp, 1)
            link(dve.tensor_tensor(nlam, lsum[:, 3:4], lsum[:, 2:3], ALU.subtract))
            link(dve.tensor_scalar(nlam, nlam, -LAM_INIT, None, ALU.add))
            link(dve.tensor_scalar(sublnb, sublnb, 1.0 - LAM_INIT, None, ALU.mult))
            for l in range(DEPTH):
                if l:
                    norm(2 * l)
                    for t in range(NT):
                        turn_copy(3 * l, t)
                mixer(l)
                if l == 0:
                    for t in range(NT):
                        dve.wait_ge(s_turn, 4 + 2 * t + 1)
                        dve.tensor_copy(xT[:, 0:2, t * P:(t + 1) * P], PS[:, 2 * t, 0:2 * P].rearrange("p (k n) -> p k n", k=2))\
                            .then_inc(s_td, 1)
                residual(l, 0)
                gained(l, 0, 0)
                residual(l, 1)
                gained(l, 0, 1)
                residual(l, 2)
                turn_copy(2 * l + 2, 0)
                rescaled(l, 0)
                gained(l, 1, 0)
                route(l, 0)
                weights(l, 0)
                residual(l, 3)
                gained(l, 1, 1)
                turn_copy(2 * l + 2, 1)
                rescaled(l, 1)
                route(l, 1)
                ranks(l)

                def experts(i, first):
                    dve.wait_ge(s_used[l], i * CHUNKS + 2 * UP_CHUNKS)
                    dve.wait_ge(s_si[l], i + 1)
                    dve.tensor_tensor(hid, PS[:, 3], hid, ALU.mult).then_inc(s_hi[l], 1)
                    dve.wait_ge(s_pkt[l], i + 1)
                    if not first:
                        dve.wait_ge(s_sca[l], i * 4)
                    dve.tensor_copy(pickT, PS[:, 5, 0:NT * P].rearrange("p (t n) -> p t n", t=NT)).then_inc(s_pkT[l], 1)
                    dve.wait_ge(s_used[l], i * CHUNKS + CHUNKS)
                    if not first:
                        dve.wait_ge(s_sca[l], i * 4)
                    dve.tensor_copy(ye[:, 512:1024], PS[:, 7]).then_inc(s_yd[l], 1)
                    if not first:
                        dve.wait_ge(s_add[l], i * 4)
                    for q in range(4):
                        t, n = q // 2, q % 2
                        dve.wait_ge(s_sca[l], i * 4 + (q + 1))
                        dve.tensor_tensor(h[:, t, 512 * n:512 * n + 512], PS[:, n], h[:, t, 512 * n:512 * n + 512],
                                          ALU.add).then_inc(s_add[l], 1)

                experts(0, True)
                experts(1, False)
                dve.wait_ge(s_go[l], 1)
                more = dve.value_load(more_passes[0:1, 0:1], min_val=0, max_val=MAX_PASSES - 1)
                trips = dve.snap(more * PAIRS + PAIRS)
                with dve.Fori(0, trips - (PEELED + LAST)) as i:
                    experts(i + PEELED, False)
                if l == 0:
                    mask_bias(1, C_HEADS)
                for n in range(LAST, 0, -1):
                    experts(trips - n, False)
                dve.wait_ge(s_add[l], trips * 4)
            for t in range(NT):
                for b in range(2):
                    scaled(2 * DEPTH, t, slice(512 * b, 512 * b + 512))

        @block.tensor
        def _(pe):
            mm = nc.tensor.matmul
            turns = [0]

            def turn(t):
                for b in range(2):
                    for kk in range(4):
                        last = nc.tensor.transpose(PS[:, 2 * t + b, kk * P:(kk + 1) * P], xn[:, t, 4 * b + kk:D:NK], ident)
                    last.then_inc(s_turn, 1)
                turns[0] += 1

            def turned(t=1):
                pe.wait_ge(s_td, turns[0] + t - 1)
                pe.wait_ge(s_ta, turns[0] + t - 1)

            def turn_bias(l, b, bank):
                mm(PS[:, bank], flip, bias[:, 2 * b:2 * b + 2, :], start=True, stop=True).then_inc(s_flip[l], 1)

            def copied(l, c):
                pos = ORDER[l].index(c)
                pe.wait_ge((s_pd if by_dve(l, pos) else s_pa)[l], copies(l, pos))

            def project_tile(l, pos, quarter):
                half, ks = quarter // 2, range(quarter % 2 * NK // 2, (quarter % 2 + 1) * NK // 2)
                c = ORDER[l][pos]
                w = place(pos).rearrange("p (k n) -> p k n", n=CW)
                bank = PS[:, 6 + pos % 2]
                if quarter == 0:
                    pe.wait_ge(s_place[l][pos], 16)
                    if pos >= 2:
                        copied(l, ORDER[l][pos - 2])
                if c not in (4, 5) if l == 0 else c < 8:
                    m = min(P, in_v[l].shape[2] - c * CW - half * P)
                    for k in ks:
                        last = mm(bank[0:m, half * SEQ:(half + 1) * SEQ], w[:, k, half * P:half * P + m], xT[:, k, :],
                                  start=(k == 0), stop=(k == NK - 1))
                else:
                    for k in ks:
                        last = mm(bank[:, half * CW:(half + 1) * CW], xT[:, k, half * P:half * P + P], w[:, k, :],
                                  start=(k == 0), stop=(k == NK - 1))
                if quarter == 3:
                    last.then_inc(s_proj[l], 1)

            def pair_scores(q, kt, qt, n, signal):
                for j in range(2):
                    last = mm(PS[:, j, 0:n], q[HD * j:HD * j + HD, qt * P:(qt + 1) * P],
                              kt[HD * j:HD * j + HD, 0:n], start=True, stop=True)
                last.then_inc(signal, 1)

            def bias_rows():
                pe.wait_ge(s_tab, 16 * 4)
                mm(PS[0:A_HEADS + B_HEADS, 4, 0:BW], tab5, hot5, start=True, stop=True).then_inc(s_vec, 1)
                for a in range(2):
                    last = mm(PS[0:C_HEADS, 5, 0:BW], tabr[:, a], hotr[:, a], start=(a == 0), stop=(a == 1))
                last.then_inc(s_vec, 1)

            def spread():
                copied(0, 8)
                copied(0, 9)
                pe.wait_ge(s_vecsb, 2)
                for t in range(NT):
                    for n, o, src in ((HD, t * HD, kqi[HD:P, 0]), (IDX_HEADS, NT * HD + t * IDX_HEADS, kqi[HD:HD + IDX_HEADS, 3])):
                        last = nc.tensor.transpose(PS[:, 5, o:o + n], src[:, t * P:(t + 1) * P], ident[HD:HD + n, HD:HD + n])
                last.then_inc(s_spread, 1)
                for j in range(2):
                    last = mm(PS[HD:P, 4, j * SEQ:(j + 1) * SEQ], ident[0:HD, 0:HD], kqi[0:HD, 3 * j], start=True, stop=True)
                last.then_inc(s_spread, 1)

            def index_scores(v):
                if v:
                    pe.wait_ge(s_ir, v)
                else:
                    pe.wait_ge(s_twice, 1)
                pair_scores(kqi[:, 1 + v % 2], kqi[:, 3], v // 2, P * (v // 2 + 1), s_is)

            def scores(l, u):
                kind, j, qt, n = unit_of(l, u)
                if u == 0 and l == 0:
                    pe.wait_ge(s_ir, 4)
                if u:
                    pe.wait_ge(s_sr[l], u)
                if kind == "a":
                    copied(0, j // 2)
                    copied(0, 2 + j // 2)
                    q, kt = qkA[:, j], qkA[:, 4 + j]
                elif kind == "b":
                    copied(0, 6 + j // 2)
                    q, kt = qB[:, j], kqi[:, 0]
                else:
                    copied(1, j // 2)
                    copied(1, 4 + j // 2)
                    q, kt = qkC[:, j], qkC[:, 8 + j]
                pair_scores(q, kt, qt, n, s_sc[l])

            def turn_probs(l, u):
                kind, _, qt, n = unit_of(l, u)
                pe.wait_ge(s_co[l], u + 1)
                if u >= 2:
                    pe.wait_ge(s_pt[l], u - 1)
                for j in range(1 if kind == "a" else 2):
                    for kt in range(n // P):
                        o = (j * (n // P) + kt) * P
                        last = nc.tensor.transpose(PS[:, 2 + u % 2, o:o + P], att[:, u % ATT, j, kt * P:(kt + 1) * P], ident)
                last.then_inc(s_tp[l], 1)

            def values(l, u):
                kind, i, qt, n = unit_of(l, u)
                g = u // 4
                pe.wait_ge(s_pt[l], u + 1)
                if kind != "a" and u >= 2:
                    pe.wait_ge(s_out[l], u - 1)
                if kind == "a" and u % 2 == 0:
                    if g == 2:
                        pe.wait_ge(s_out[0], 7 + qt)
                    else:
                        pe.wait_ge(s_ssa, 3 * (qt + 1))
                if kind == "a":
                    copied(0, 4 + i // 2)
                    for kt in range(n // P):
                        last = mm(PS[:, 4 + qt, i % 2 * A_V:(i % 2 + 1) * A_V], pT[:, u % 2, kt * P:(kt + 1) * P],
                                  vA[:, kt, i * A_V:(i + 1) * A_V], start=(kt == 0), stop=(kt == n // P - 1))
                else:
                    if kind == "b":
                        pe.wait_ge(s_vb, 2)
                    else:
                        copied(1, 8 + i // 2)
                    for kt in range(n // P):
                        for j in range(2):
                            hd, o = 2 * i + j, (j * (n // P) + kt) * P
                            last = mm(PS[j * HD:(j + 1) * HD, 4 + u % 2, 0:P],
                                      vB[:, kt] if kind == "b" else vC[:, kt, hd * HD:(hd + 1) * HD],
                                      pT[:, u % 2, o:o + P], start=(kt == 0), stop=(kt == n // P - 1))
                last.then_inc(s_pv[l], 1)

            def out_part(l, q, part, signal=False):
                t, b = q // 2, q % 2
                for m in part:
                    k = OUT_ORDER[l][m]
                    if q == 0:
                        pe.wait_ge(s_place[l][CHUNKS + k // KPC], 16)
                    if l:
                        src = qkC[:, k]
                    else:
                        src = qB[:, k - 4] if k >= 4 else xT[:, k]
                    last = mm(PS[:, OUT_BANK[q]], src[:, t * P:(t + 1) * P], wo[:, k // KPC, k % KPC, 512 * b:512 * b + 512],
                              start=(m == 0), stop=(m == NK - 1))
                    if q == 3 and m % KPC == KPC - 1:
                        last.then_inc(s_od[l], 1)
                    elif m == NK - 1:
                        last.then_inc(s_od[l], 1)

            def early_out(l, n):
                q, part = n // 2, range(n % 2 * EARLY // 2, (n % 2 + 1) * EARLY // 2)
                if n == 0:
                    pe.wait_ge(s_out[l], 8)
                if part[0] == 0:
                    copied(l, ORDER[l][q - 2])
                out_part(l, q, part)

            def turn_heads(t):
                for b in range(2):
                    for kk in range(2):
                        k = 2 * b + kk
                        last = nc.tensor.transpose(PS[:, 2 * t + b, kk * P:(kk + 1) * P], xn[:, t, k * P:(k + 1) * P], ident)
                    last.then_inc(s_turn, 1)
                turns[0] += 1

            def mixer(l):
                for what, n, quarter in events(l):
                    if what == "tile":
                        if l and (n, quarter) in ((0, 0), (0, 2)):
                            turned(quarter // 2)
                        project_tile(l, n, quarter)
                        if l == 0 and (n, quarter) == (0, 0):
                            bias_rows()
                    elif what == "flip":
                        if n == 0:
                            pe.wait_ge(s_z[0], 16)
                        if n >= 2:
                            pe.wait_ge(s_ba[0], n - 1)
                        turn_bias(0, n, 2 + n % 2)
                    elif what == "index":
                        index_scores(n)
                    elif what == "spread":
                        spread()
                    elif what == "step":
                        if n == 0 and l == 0:
                            pe.wait_ge(s_ba[0], (A_HEADS + B_HEADS) // 2)
                        if n < UNITS:
                            scores(l, n)
                        elif n - UNITS < EARLY:
                            early_out(l, n - UNITS)
                        if 2 <= n <= UNITS + 1:
                            turn_probs(l, n - 2)
                        if 3 <= n <= UNITS + 2:
                            values(l, n - 3)

            def route(l, t):
                if t == 0:
                    pe.wait_ge(s_wr[l], 32)
                for k in range(NK):
                    if k == 0:
                        pe.wait_ge(s_td, turns[0])
                    if k == NK // 2:
                        pe.wait_ge(s_ta, turns[0])
                    last = mm(PS[0:ROUTES, 6 + t, 0:P], wr[:, k, :], xT[:, k, t * P:(t + 1) * P], start=(k == 0), stop=(k == NK - 1))
                last.then_inc(s_lT[l], 1)

            def route_back(l, t):
                pe.wait_ge(s_lc[l], t + 1)
                nc.tensor.transpose(PS[:, 6 + t, P:P + ROUTES], logT[0:ROUTES, t], ident[0:ROUTES, 0:ROUTES]).then_inc(s_lg[l], 1)

            def ranks(l):
                pe.wait_ge(s_ch[l], 1)
                mm(PS[:, 4, 0:EXPERTS], before, chose[:, 0], start=True, stop=True)
                mm(PS[:, 4, EXPERTS:2 * EXPERTS], ones, chose[:, 0], start=True, stop=False)
                mm(PS[:, 5, 0:EXPERTS], ones, chose[:, 0], start=True, stop=False)
                pe.wait_ge(s_ch[l], 2)
                mm(PS[:, 4, EXPERTS:2 * EXPERTS], before, chose[:, 1], start=False, stop=True).then_inc(s_rk[l], 1)
                mm(PS[:, 5, 0:EXPERTS], ones, chose[:, 1], start=False, stop=True).then_inc(s_rk[l], 1)

            def experts(l):
                def chunk_there(n, c, rounds):
                    if once(n, c) is not None:
                        pe.wait_ge(s_once[once(n, c)], (AT_ONCE if once(n, c) == ONCE - 1 else 1) * 16 * (l + 1))
                    else:
                        pe.wait_ge(s_place[l][place_of(n, c)], rounds * (16 * (ROUND * CHUNKS // PLACES)) + 16 * loads(l, n, c))

                def gather(i, b, first):
                    if b == 0:
                        pe.wait_ge(s_pk[l], i * PICKS + PICKS)
                        if not first:
                            pe.wait_ge(s_add[l], i * 4 - 4)
                    for kk in range(4):
                        for t in range(NT):
                            last = mm(PS[:, b, kk * P:(kk + 1) * P], xn[:, t, 4 * b + kk:D:NK], pick[:, t],
                                      start=(t == 0), stop=(t == NT - 1))
                    last.then_inc(s_g[l], 1)

                def up_chunk(i, first, n, rounds, c):
                    part = c // UP_CHUNKS
                    if c % UP_CHUNKS == 0 and not first:
                        pe.wait_ge((s_si, s_hi)[part][l], i)
                    chunk_there(n, c, rounds)
                    if part == 0 and c % 2 == 0:
                        pe.wait_ge(s_xg[l], i * 2 + (c // 2 + 1))
                    w = [slot(n, c, e).rearrange("p (k n) -> p k n", k=KPU) for e in range(AT_ONCE)]
                    for kk in range(KPU):
                        k = c % UP_CHUNKS * KPU + kk
                        for e in range(AT_ONCE):
                            last = mm(PS[e * SLOTS:(e + 1) * SLOTS, 2 + part, :], xg[:, k, e * SLOTS:(e + 1) * SLOTS],
                                      w[e][:, kk, :], start=(k == 0), stop=(k == NK - 1))
                    last.then_inc(s_used[l], 1)

                def down_chunk(n, rounds, k):
                    chunk_there(n, 2 * UP_CHUNKS + k, rounds)
                    w = [slot(n, 2 * UP_CHUNKS + k, e) for e in range(AT_ONCE)]
                    for b in range(2):
                        for e in range(AT_ONCE):
                            last = mm(PS[e * SLOTS:(e + 1) * SLOTS, 6 + b, :], hidT[:, k, e * SLOTS:(e + 1) * SLOTS],
                                      w[e][:, 512 * b:512 * b + 512], start=(k == 0), stop=(k == NF - 1))
                    last.then_inc(s_used[l], 1)

                def scatter(i, q):
                    t, b = q // 2, q % 2
                    if q < 2:
                        pe.wait_ge((s_ya, s_yd)[b][l], i + 1)
                    else:
                        pe.wait_ge(s_add[l], i * 4 + (q - 1))
                    mm(PS[:, b], pickT[:, t], ye[:, 512 * b:512 * b + 512], start=True, stop=True).then_inc(s_sca[l], 1)

                def pair(i, n, rounds=0, first=False, final=False):
                    for c in range(0 if first else AHEAD, 2 * UP_CHUNKS):
                        up_chunk(i, first, n, rounds, c)
                    if not final:
                        gather(i + 1, 0, False)
                    pe.wait_ge(s_hi[l], i + 1)
                    if not first:
                        pe.wait_ge(s_hT[l], i)
                    for k in range(NF):
                        last = nc.tensor.transpose(PS[:, 4, k * P:(k + 1) * P], hid[:, k:F:NF], ident)
                    last.then_inc(s_ht[l], 1)
                    pe.wait_ge(s_pw[l], i * PICKS + PICKS)
                    if not first:
                        pe.wait_ge(s_pkT[l], i)
                    for t in range(NT):
                        last = nc.tensor.transpose(PS[:, 5, t * P:(t + 1) * P], pickw[:, t], ident)
                    last.then_inc(s_pkt[l], 1)
                    if not final:
                        gather(i + 1, 1, False)
                    pe.wait_ge(s_hT[l], i + 1)
                    if not first:
                        pe.wait_ge(s_ya[l], i)
                        pe.wait_ge(s_yd[l], i)
                    for k in range(NF):
                        down_chunk(n, rounds, k)
                    if not final:
                        up_chunk(i + 1, False, n + 1, rounds, 0)
                    pe.wait_ge(s_pkT[l], i + 1)
                    if not final:
                        pe.wait_ge(s_xg[l], i * 2 + 4)
                    scatter(i, 0)
                    scatter(i, 1)
                    if not final:
                        up_chunk(i + 1, False, n + 1, rounds, 1)
                    scatter(i, 2)
                    scatter(i, 3)

                for b in range(2):
                    gather(0, b, True)
                pair(0, 0, first=True)
                pair(1, 1)
                for n in range(2, ROUND):
                    pair(n, n)
                pe.wait_ge(s_go[l], 1)
                more = pe.value_load(more_passes[0:1, 0:1], min_val=0, max_val=MAX_PASSES - 1)
                rounds = pe.snap(more * (PAIRS // ROUND) + (PAIRS // ROUND - 2))
                with pe.Fori(0, rounds) as g:
                    for n in range(ROUND, 2 * ROUND):
                        pair(g * ROUND + n, n, g)
                for n in range(ROUND, 2 * ROUND):
                    if n == 2 * ROUND - LAST and l == 0:
                        pe.wait_ge(s_z[1], 16)
                        pe.wait_ge(s_add[0], rounds * (ROUND * 4) + n * 4)
                        for b in range(C_HEADS // 2):
                            if b >= 2:
                                pe.wait_ge(s_ba[1], b - 1)
                            turn_bias(1, b, b % 2)
                        pe.wait_ge(s_ba[1], C_HEADS // 2)
                    pair(rounds * ROUND + n, n, rounds, final=(n == 2 * ROUND - 1))

            pe.wait_ge(s_kon, 16)
            for l in range(DEPTH):
                for t in range(NT):
                    pe.wait_ge(s_xn, 4 * l + t + 1)
                    turn(t)
                if l == 0:
                    turned()
                mixer(l)
                late = range(EARLY, NK)
                if l == 0:
                    pe.wait_ge(s_sub, 3)
                    turn_heads(0)
                    turned()
                else:
                    pe.wait_ge(s_out[l], UNITS - 2)
                out_part(l, 0, late)
                if l == 0:
                    pe.wait_ge(s_sub, 4)
                    turn_heads(1)
                out_part(l, 1, late)
                if l == 0:
                    turned()
                else:
                    pe.wait_ge(s_out[l], UNITS)
                out_part(l, 2, range(NK))
                pe.wait_ge(s_xn, 4 * l + 3)
                turn(0)
                out_part(l, 3, [0])
                route(l, 0)
                out_part(l, 3, [1])
                route_back(l, 0)
                out_part(l, 3, range(2, NK))
                pe.wait_ge(s_xn, 4 * l + 4)
                turn(1)
                route(l, 1)
                route_back(l, 1)
                ranks(l)
                experts(l)


_INS = ["x", "t5_bias", "ln_mix", "ln_ffn", "ln_final", "ab_w_in", "ab_w_out", "diff_lambda", "diff_subln", "c_w_in",
        "c_w_out", "c_rel_bias", "moe_w_rg", "moe_b_rg", "moe_w_re", "moe_b_re", "moe_w_gate", "moe_w_up", "moe_w_down"]


def shape_constants():
    import math

    consts = np.zeros((P, 4 * P + SEQ), np.float32)
    consts[:, 0:P] = np.eye(P)
    consts[:, P:2 * P] = np.eye(P)[::-1]
    consts[:, 2 * P:3 * P] = np.triu(np.ones((P, P)), 1)
    consts[:, 3 * P:4 * P] = 1
    consts[:, 4 * P:] = 1 + np.arange(SEQ)
    j = np.arange(BW)
    dist = np.minimum(j, BL - 1) - (SEQ - 1)
    half, exact, far = BUCKETS // 2, BUCKETS // 4, 1024
    n = np.abs(dist)
    nf = np.maximum(n, 1).astype(np.float32)
    large = exact + (np.log(nf / np.float32(exact)) / np.float32(math.log(far / exact)) * np.float32(half - exact)).astype(np.int32)
    bucket = np.where(dist > 0, half, 0) + np.where(n < exact, n, np.minimum(large, half - 1))
    hot_t5 = (np.arange(BUCKETS)[:, None] == bucket[None, :]).astype(np.float32)
    row = np.clip(-dist, -P, P) + P - 1
    hot_rel = (np.arange(2 * P)[:, None] == row[None, :]).astype(np.float32)
    return {"consts": consts, "hot_t5": hot_t5, "hot_rel": hot_rel}


def kernel(**inputs):
    import concourse.bacc as _bacc
    from concourse.bass_utils import run_bass_kernel_spmd as _run

    nc = _bacc.Bacc("TRN2", target_bir_lowering=False, num_devices=1)
    arrays, args = {}, []
    given = {n: inputs[n] for n in _INS} | shape_constants()
    for name, a in given.items():
        a = np.ascontiguousarray(a)
        arrays[f"in_{name}"] = a
        args.append(nc.dram_tensor(f"in_{name}", a.shape, mybir.dt.from_np(a.dtype), kind="ExternalInput").ap())
    args.append(nc.dram_tensor("out_0", (1, SEQ, D), FP32, kind="ExternalOutput").ap())
    build(nc, *args)
    r = _run(nc, [arrays], core_ids=[0])
    return r.results[0]["out_0"]
```
